# Optimizing a Trainium2 kernel written in Bass

```python
import jax
import jax.numpy as jnp
from jax import lax
import numpy as np

D_MODEL = 1024
BATCH = 1
SEQ = 256
DEPTH = 2

HEAD_DIM = 64
D_MIX = D_MODEL
GROUP_WIDTH = D_MIX // 4
SWA_HEADS = GROUP_WIDTH // HEAD_DIM
SWA_KV_HEADS = 2
SWA_WINDOW = 128
ROPE_THETA = 10000.0
GLA_HEADS = 4
GLA_DK = 32
GLA_DV = GROUP_WIDTH // GLA_HEADS
GLA_LOW_RANK = 16
GLA_TAU = 16.0
GLA_CHUNK = 64
SB_HEADS = GROUP_WIDTH // HEAD_DIM
SB_BLOCK = 128
RWKV_HEADS = GROUP_WIDTH // HEAD_DIM
RWKV_DECAY_LORA = 64
RWKV_A_LORA = 64
RWKV_GATE_LORA = 128
RWKV_DECAY_SCALE = 0.6065306597126334
RWKV_GN_EPS = 64e-5
D_FF = 2816
N_EXPERTS = 8
TOP_K = 2
D_FF_EXPERT = 1408
NORM_EPS = 1e-6
N_DENSE_LAYERS = (DEPTH + 1) // 2
N_MOE_LAYERS = DEPTH // 2

A_Q = SWA_HEADS * HEAD_DIM
A_KV = SWA_KV_HEADS * HEAD_DIM
A_COLS = A_Q + 2 * A_KV
B_QK = GLA_HEADS * GLA_DK
B_V = GLA_HEADS * GLA_DV
B_COLS = 2 * B_QK + 2 * B_V + GLA_LOW_RANK
C_COLS = 3 * GROUP_WIDTH
D_COLS = 3 * GROUP_WIDTH + RWKV_DECAY_LORA + RWKV_A_LORA + RWKV_GATE_LORA
IN_COLS = A_COLS + B_COLS + C_COLS + D_COLS

kernel_name = 'hymba_style_four_mixer_hybrid'

F32 = jnp.float32

def rmsnorm(x, g, eps=NORM_EPS):
    xf = x.astype(F32)
    y = xf * lax.rsqrt(jnp.mean(xf * xf, axis=-1, keepdims=True) + eps)
    return (y * g.astype(F32)).astype(x.dtype)

def rope_tables(positions):
    inv_freq = ROPE_THETA ** (-jnp.arange(0, HEAD_DIM, 2, dtype=F32) / HEAD_DIM)
    ang = positions.astype(F32)[..., None] * inv_freq
    return jnp.cos(ang), jnp.sin(ang)

def apply_rope(x, cos, sin):
    xf = x.astype(F32)
    x1, x2 = jnp.split(xf, 2, axis=-1)
    c, s = cos[:, :, None], sin[:, :, None]
    return jnp.concatenate([x1 * c - x2 * s, x2 * c + x1 * s], axis=-1).astype(x.dtype)

def swa_sink_attention(q, k, v, sinks):
    dtype = q.dtype
    b_, s_ = q.shape[:2]
    nb = s_ // SWA_WINDOW
    grp = SWA_HEADS // SWA_KV_HEADS
    qb = q.astype(F32).reshape(b_, nb, SWA_WINDOW, SWA_KV_HEADS, grp, HEAD_DIM)

    def band(t):
        tb = t.astype(F32).reshape(b_, nb, SWA_WINDOW, SWA_KV_HEADS, HEAD_DIM)
        prev = jnp.concatenate([jnp.zeros_like(tb[:, :1]), tb[:, :-1]], axis=1)
        return jnp.concatenate([prev, tb], axis=2)

    kw, vw = band(k), band(v)
    scores = jnp.einsum('bnqhgd,bnjhd->bnhgqj', qb, kw) * HEAD_DIM ** -0.5
    i = jnp.arange(SWA_WINDOW)[:, None]
    j = jnp.arange(2 * SWA_WINDOW)[None, :]
    in_band = (j > i) & (j <= i + SWA_WINDOW)
    blk = jnp.arange(nb)[:, None, None]
    valid = in_band[None] & ((blk > 0) | (j[None] >= SWA_WINDOW))
    scores = jnp.where(valid[None, :, None, None], scores, -jnp.inf)
    sink = sinks.astype(F32).reshape(SWA_KV_HEADS, grp)[None, None, :, :, None, None]
    m = jnp.maximum(scores.max(axis=-1, keepdims=True), sink)
    p = jnp.exp(scores - m)
    w = p / (p.sum(axis=-1, keepdims=True) + jnp.exp(sink - m))
    o = jnp.einsum('bnhgqj,bnjhd->bnqhgd', w, vw)
    return o.reshape(b_, s_, SWA_HEADS, HEAD_DIM).astype(dtype)

def gla_chunked(q, k, v, log_a):
    dtype = v.dtype
    b_, s_, h, dk = q.shape
    dv = v.shape[-1]
    nc = s_ // GLA_CHUNK

    def chunks(t):
        return t.astype(F32).reshape(b_, nc, GLA_CHUNK, h, t.shape[-1]).transpose(0, 3, 1, 2, 4)

    q, k, v, la = chunks(q) * dk ** -0.5, chunks(k), chunks(v), chunks(log_a)
    b = jnp.cumsum(la, axis=3)
    b_ref = b[:, :, :, GLA_CHUNK // 2 - 1:GLA_CHUNK // 2]
    b_last = b[:, :, :, -1:]
    causal = jnp.tril(jnp.ones((GLA_CHUNK, GLA_CHUNK), dtype=bool))
    att = jnp.einsum('bhnte,bhnse->bhnts', q * jnp.exp(b - b_ref), k * jnp.exp(b_ref - b))
    att = jnp.where(causal, att, 0.0)
    o = jnp.einsum('bhnts,bhnsf->bhntf', att, v)
    kv = jnp.einsum('bhnse,bhnsf->bhnef', k * jnp.exp(b_last - b), v)
    decay = jnp.exp(b_last[:, :, :, 0])

    def step(state, inp):
        dec, kv_n = inp
        return dec[..., None] * state + kv_n, state

    _, s_prev = lax.scan(step, jnp.zeros((b_, h, dk, dv), F32),
                         (jnp.moveaxis(decay, 2, 0), jnp.moveaxis(kv, 2, 0)))
    o = o + jnp.einsum('bhnte,nbhef->bhntf', q * jnp.exp(b), s_prev)
    return o.transpose(0, 2, 3, 1, 4).reshape(b_, s_, h, dv).astype(dtype)

def stick_breaking_attention(q, k, v):
    dtype = v.dtype
    b_, s_, h, dh = q.shape
    q, k, v = (t.astype(F32).transpose(0, 2, 1, 3) for t in (q, k, v))
    outs = []
    for blk in range(s_ // SB_BLOCK):
        start, stop = blk * SB_BLOCK, (blk + 1) * SB_BLOCK
        z = jnp.einsum('bhtd,bhsd->bhts', q[:, :, start:stop], k[:, :, :stop]) * dh ** -0.5
        strict = jnp.arange(stop)[None, :] < jnp.arange(start, stop)[:, None]
        log_1mb = jnp.where(strict, jax.nn.log_sigmoid(-z), 0.0)
        between = lax.cumsum(log_1mb, axis=3, reverse=True) - log_1mb
        attn = jnp.where(strict, jnp.exp(jax.nn.log_sigmoid(z) + between), 0.0)
        outs.append(jnp.einsum('bhts,bhsd->bhtd', attn, v[:, :, :stop]))
    o = jnp.concatenate(outs, axis=2)
    return o.transpose(0, 2, 1, 3).astype(dtype)

def rwkv7_time_mix(pd, mu, w0, w2, a0, a2, g2, k_k, k_a, r_k, ln_w, ln_b):
    dtype = pd.dtype
    b_, s_, _ = pd.shape
    pd = pd.astype(F32)
    shifted = jnp.concatenate([jnp.zeros_like(pd[:, :1]), pd[:, :-1]], axis=1)
    pd = pd + (shifted - pd) * mu
    gw = GROUP_WIDTH
    r, k, v, wl, al, gl = jnp.split(
        pd, [gw, 2 * gw, 3 * gw, 3 * gw + RWKV_DECAY_LORA, 3 * gw + RWKV_DECAY_LORA + RWKV_A_LORA], axis=-1)
    log_w = -RWKV_DECAY_SCALE * jax.nn.sigmoid(w0 + jnp.tanh(wl) @ w2)
    a = jax.nn.sigmoid(a0 + al @ a2)
    g = jax.nn.sigmoid(gl) @ g2

    def heads(t):
        return t.reshape(b_, s_, RWKV_HEADS, HEAD_DIM)

    kk = heads(k * k_k)
    kk = kk * lax.rsqrt(jnp.sum(kk * kk, axis=-1, keepdims=True) + 1e-12)
    k = k * (1.0 + (a - 1.0) * k_a)
    r, k, v, a, decay = heads(r), heads(k), heads(v), heads(a), heads(jnp.exp(log_w))

    def step(state, inp):
        r_t, w_t, k_t, v_t, kk_t, b_t = inp
        sa = jnp.einsum('bhvk,bhk->bhv', state, kk_t)
        state = (state * w_t[:, :, None, :] - sa[..., None] * b_t[:, :, None, :]
                 + v_t[..., None] * k_t[:, :, None, :])
        return state, jnp.einsum('bhvk,bhk->bhv', state, r_t)

    seq_first = lambda t: jnp.moveaxis(t, 1, 0)
    _, y = lax.scan(step, jnp.zeros((b_, RWKV_HEADS, HEAD_DIM, HEAD_DIM), F32),
                    (seq_first(r), seq_first(decay), seq_first(k), seq_first(v), seq_first(kk), seq_first(kk * a)))
    y = jnp.moveaxis(y, 0, 1)
    mean = jnp.mean(y, axis=-1, keepdims=True)
    var = jnp.mean(jnp.square(y - mean), axis=-1, keepdims=True)
    y = (y - mean) * lax.rsqrt(var + RWKV_GN_EPS) * ln_w + ln_b
    y = y + jnp.sum(r * k * r_k, axis=-1, keepdims=True) * v
    return (y.reshape(b_, s_, GROUP_WIDTH) * g).astype(dtype)

def swiglu(h, w1, w3, w2):
    return (jax.nn.silu(h @ w1) * (h @ w3)) @ w2

def moe_swiglu(h, router, w1, w3, w2):
    logits = (h @ router).astype(F32)
    top_vals, top_idx = lax.top_k(logits, TOP_K)
    gates = jax.nn.softmax(top_vals, axis=-1)
    combine = jnp.sum(jax.nn.one_hot(top_idx, N_EXPERTS, dtype=F32) * gates[..., None], axis=-2)
    out = jnp.zeros_like(h)
    for e in range(N_EXPERTS):
        out = out + combine[..., e:e + 1].astype(h.dtype) * swiglu(h, w1[e], w3[e], w2[e])
    return out

def setup_inputs(seed: int = 0) -> dict:
    key = jax.random.key(seed)
    ks = iter(jax.random.split(key, 48))
    L = DEPTH

    def nrm(shape, scale):
        return jax.random.normal(next(ks), shape, F32) * scale

    def gain(shape):
        return 1.0 + nrm(shape, 0.02)

    x = nrm((BATCH, SEQ, D_MODEL), 1.0)
    offsets = jax.random.randint(next(ks), (BATCH, 1), 0, 1024, dtype=jnp.int32)
    positions = offsets + jnp.arange(SEQ, dtype=jnp.int32)[None, :]
    return {
        'x': x,
        'positions': positions,
        'attn_norm': gain((L, D_MODEL)),
        'w_in': nrm((L, D_MODEL, IN_COLS), D_MODEL ** -0.5),
        'swa_sinks': nrm((L, SWA_HEADS), 0.5),
        'swa_out_norm': gain((L, SWA_HEADS, HEAD_DIM)),
        'gla_w_a2': nrm((L, GLA_LOW_RANK, B_QK), GLA_LOW_RANK ** -0.5),
        'gla_b_a': 1.0 + nrm((L, B_QK), 0.5),
        'gla_out_norm': gain((L, GLA_HEADS, GLA_DV)),
        'sb_out_norm': gain((L, SB_HEADS, HEAD_DIM)),
        'rwkv_mu': jax.random.uniform(next(ks), (L, D_COLS), F32),
        'rwkv_w0': nrm((L, GROUP_WIDTH), 0.5),
        'rwkv_w2': nrm((L, RWKV_DECAY_LORA, GROUP_WIDTH), 0.5 * RWKV_DECAY_LORA ** -0.5),
        'rwkv_a0': nrm((L, GROUP_WIDTH), 0.5),
        'rwkv_a2': nrm((L, RWKV_A_LORA, GROUP_WIDTH), 0.5 * RWKV_A_LORA ** -0.5),
        'rwkv_g2': nrm((L, RWKV_GATE_LORA, GROUP_WIDTH), RWKV_GATE_LORA ** -0.5),
        'rwkv_k_k': 0.85 + nrm((L, GROUP_WIDTH), 0.05),
        'rwkv_k_a': 1.0 + nrm((L, GROUP_WIDTH), 0.05),
        'rwkv_r_k': nrm((L, RWKV_HEADS, HEAD_DIM), 0.1),
        'rwkv_ln_w': gain((L, RWKV_HEADS, HEAD_DIM)),
        'rwkv_ln_b': nrm((L, RWKV_HEADS, HEAD_DIM), 0.02),
        'w_out': nrm((L, D_MIX, D_MODEL), D_MIX ** -0.5),
        'ffn_norm': gain((L, D_MODEL)),
        'ffn_w1': nrm((N_DENSE_LAYERS, D_MODEL, D_FF), D_MODEL ** -0.5),
        'ffn_w3': nrm((N_DENSE_LAYERS, D_MODEL, D_FF), D_MODEL ** -0.5),
        'ffn_w2': nrm((N_DENSE_LAYERS, D_FF, D_MODEL), D_FF ** -0.5),
        'router': nrm((N_MOE_LAYERS, D_MODEL, N_EXPERTS), D_MODEL ** -0.5),
        'moe_w1': nrm((N_MOE_LAYERS, N_EXPERTS, D_MODEL, D_FF_EXPERT), D_MODEL ** -0.5),
        'moe_w3': nrm((N_MOE_LAYERS, N_EXPERTS, D_MODEL, D_FF_EXPERT), D_MODEL ** -0.5),
        'moe_w2': nrm((N_MOE_LAYERS, N_EXPERTS, D_FF_EXPERT, D_MODEL), D_FF_EXPERT ** -0.5),
        'final_norm': gain((D_MODEL,)),
    }

def reference(x, positions, attn_norm, w_in, swa_sinks, swa_out_norm, gla_w_a2, gla_b_a, gla_out_norm,
              sb_out_norm, rwkv_mu, rwkv_w0, rwkv_w2, rwkv_a0, rwkv_a2, rwkv_g2, rwkv_k_k, rwkv_k_a,
              rwkv_r_k, rwkv_ln_w, rwkv_ln_b, w_out, ffn_norm, ffn_w1, ffn_w3, ffn_w2, router,
              moe_w1, moe_w3, moe_w2, final_norm):
    b_, s_, _ = x.shape
    cos, sin = rope_tables(positions)
    for l in range(DEPTH):
        h = rmsnorm(x, attn_norm[l])
        proj = h @ w_in[l]
        pa, pb, pc, pd = jnp.split(proj, [A_COLS, A_COLS + B_COLS, A_COLS + B_COLS + C_COLS], axis=-1)

        qa, ka, va = jnp.split(pa, [A_Q, A_Q + A_KV], axis=-1)
        qa = apply_rope(qa.reshape(b_, s_, SWA_HEADS, HEAD_DIM), cos, sin)
        ka = apply_rope(ka.reshape(b_, s_, SWA_KV_HEADS, HEAD_DIM), cos, sin)
        oa = swa_sink_attention(qa, ka, va.reshape(b_, s_, SWA_KV_HEADS, HEAD_DIM), swa_sinks[l])
        oa = rmsnorm(oa, swa_out_norm[l]).reshape(b_, s_, GROUP_WIDTH)

        qb, kb, vb, gb, lrb = jnp.split(pb, [B_QK, 2 * B_QK, 2 * B_QK + B_V, 2 * B_QK + 2 * B_V], axis=-1)
        log_a = jax.nn.log_sigmoid((lrb @ gla_w_a2[l] + gla_b_a[l]).astype(F32)) / GLA_TAU
        ob = gla_chunked(qb.reshape(b_, s_, GLA_HEADS, GLA_DK), kb.reshape(b_, s_, GLA_HEADS, GLA_DK),
                         vb.reshape(b_, s_, GLA_HEADS, GLA_DV), log_a.reshape(b_, s_, GLA_HEADS, GLA_DK))
        ob = rmsnorm(ob, gla_out_norm[l]).reshape(b_, s_, GROUP_WIDTH) * jax.nn.silu(gb)

        qc, kc, vc = jnp.split(pc, 3, axis=-1)
        oc = stick_breaking_attention(qc.reshape(b_, s_, SB_HEADS, HEAD_DIM), kc.reshape(b_, s_, SB_HEADS, HEAD_DIM),
                                      vc.reshape(b_, s_, SB_HEADS, HEAD_DIM))
        oc = rmsnorm(oc, sb_out_norm[l]).reshape(b_, s_, GROUP_WIDTH)

        od = rwkv7_time_mix(pd, rwkv_mu[l], rwkv_w0[l], rwkv_w2[l], rwkv_a0[l], rwkv_a2[l], rwkv_g2[l],
                            rwkv_k_k[l], rwkv_k_a[l], rwkv_r_k[l], rwkv_ln_w[l], rwkv_ln_b[l])

        mix = jnp.concatenate([oa, ob, oc, od], axis=-1).astype(x.dtype)
        x = x + mix @ w_out[l]

        h = rmsnorm(x, ffn_norm[l])
        if l % 2 == 0:
            x = x + swiglu(h, ffn_w1[l // 2], ffn_w3[l // 2], ffn_w2[l // 2])
        else:
            x = x + moe_swiglu(h, router[l // 2], moe_w1[l // 2], moe_w3[l // 2], moe_w2[l // 2])
    return rmsnorm(x, final_norm)


_drawn_inputs = setup_inputs


def setup_inputs(seed=0):
    import zlib

    import numpy as np

    out = dict(_drawn_inputs(seed))
    spreads = {}
    factors = {'swa_sinks': 32.152,
     'swa_out_norm': 8.234,
     'gla_out_norm': 17.198,
     'sb_out_norm': 9.649,
     'rwkv_k_k': 17.337,
     'rwkv_ln_w': 17.668,
     'rwkv_ln_b': 14.632,
     'final_norm': 7.692,
     'ffn_norm': 5.411}
    for name, (base, spread) in spreads.items():
        noise = np.random.default_rng([zlib.crc32(name.encode()), seed]).standard_normal(out[name].shape)
        drawn = base * np.exp(spread * noise) if base else spread * noise
        out[name] = jnp.asarray(drawn.astype(out[name].dtype))
    for name, factor in factors.items():
        out[name] = (out[name] * factor).astype(out[name].dtype)
    return out
```

```python
from contextlib import ExitStack

import numpy as np

import concourse.bass as bass
from concourse import mybir

F32 = mybir.dt.float32
I32 = mybir.dt.int32
ALU = mybir.AluOpType
ACT = mybir.ActivationFunctionType
AX_X = mybir.AxisListType.X

P = 128
D = 1024
KC = D // P
SEQ = 256
NT = SEQ // P
DEPTH = 2
GW = 256
HD = 64
A_Q, A_KV = 256, 128
B_QK, B_V, LR = 128, 256, 16
A_OFF = 0
B_OFF = A_Q + 2 * A_KV
C_OFF = B_OFF + 2 * B_QK + 2 * B_V + LR
D_OFF = C_OFF + 3 * GW
D_COLS = 3 * GW + 256
IN_COLS = D_OFF + D_COLS
D_FF = 2816
N_EXPERTS = 8
D_FFE = 1408
UPC = D_FFE // P
UP2 = (UPC + 1) // 2
EPS = 1e-6
GN_EPS = 64e-5
DECAY = 0.6065306597126334
ROPE_THETA = 10000.0
NEG = -1.0e30
MAGIC = 12582912.0
TWO_PI = 6.283185307179586
TWO_PI_1 = 6.28125
TWO_PI_2 = float(np.float32(np.round((TWO_PI - TWO_PI_1) * 2.0 ** 20) / 2.0 ** 20))
TWO_PI_3 = TWO_PI - TWO_PI_1 - TWO_PI_2

SLOT = KC * 272
SLOTS = 6

CAP = 96
MAX_PASSES = -(-SEQ // CAP)

CONST = {}
_at = 0
for _name, _n in (("ident", 128), ("rev_cum", 128), ("rev_all", 128), ("c_mask", 128), ("a_mask", 256),
                  ("upper", 256), ("lower", 128), ("blk16", 128), ("off32", 128), ("off64", 128),
                  ("off128", 128), ("gla_mask", 64), ("same_head", 128), ("head_sel", 2),
                  ("reset64", 256), ("reset128", 512), ("inv_freq", 32), ("all", 128),
                  ("iota", CAP)):
    CONST[_name] = (_at, _n)
    _at += _n
N_CONST = _at

PARAM = {}
_at = 0
for _name, _n in (("attn_norm", 8), ("ffn_norm", 8), ("mu", 8), ("w0", 2), ("a0", 2), ("k_k", 2), ("k_a", 2),
                  ("r_k", 2), ("b_a", 1)):
    PARAM[_name] = (_at, _n)
    _at += _n
N_PARAM = _at
ROWS = {}
_at = 0
for _name, _n in (("swa", 256), ("gla", 256), ("sb", 256), ("ln_w", 256), ("ln_b", 256), ("sinks", 4)):
    ROWS[_name] = (_at, _n)
    _at += _n
N_ROWS = _at


def shape_constants():
    t = np.zeros((P, N_CONST), np.float32)
    i = np.arange(P)[:, None]
    j = np.arange(P)[None, :]

    def put(name, value):
        at, n = CONST[name]
        t[:, at:at + n] = value

    put("ident", i == j)
    put("rev_cum", -1.0 * (i >= j))
    put("rev_all", -1.0)
    put("c_mask", np.where(i < j, 0.0, NEG))
    put("a_mask", np.concatenate([np.where(j > i, 0.0, NEG), np.where(j <= i, 0.0, NEG)], 1))
    put("upper", np.concatenate([i < j, i <= j], 1))
    put("lower", i > j)
    put("blk16", -1.0 * (i // 16 == j // 16))
    for b in (32, 64, 128):
        put(f"off{b}", (i // b == j // b) & (i // (b // 2) != j // (b // 2)))
    put("gla_mask", (i % 64) <= np.arange(64)[None, :])
    put("same_head", i // HD == j // HD)
    put("head_sel", i // HD == np.arange(2)[None, :])
    put("reset64", np.arange(256)[None, :] % 64 != 0)
    put("reset128", np.arange(512)[None, :] % 128 != 0)
    put("all", 1.0)
    put("iota", np.arange(CAP)[None, :])
    put("inv_freq", (np.float32(ROPE_THETA) ** (-np.arange(0, HD, 2, dtype=np.float32) / np.float32(HD)))[None, :])
    return t


def piece_plan():
    out = []
    for l in range(DEPTH):
        for at, n in ((D_OFF + 768, 256), (D_OFF, 256), (D_OFF + 256, 256), (D_OFF + 512, 256),
                      (C_OFF, 256), (C_OFF + 256, 256), (C_OFF + 512, 256),
                      (B_OFF, 256), (B_OFF + 256, 256), (B_OFF + 512, 272), (A_OFF, 256), (A_OFF + 256, 256)):
            out.append(("w_in", l, at, n))
        for k in range(KC // 2):
            out.append(("w_out", l, 2 * k, 2))
        if l % 2 == 0:
            for i in range(D_FF // 256):
                out.append(("w1", l, 256 * i, 256))
                out.append(("w3", l, 256 * i, 256))
            for i in range(D_FF // 256):
                out.append(("w2", l, 2 * i, 2))
    return out


IN_PIECES = ("P0", "P1", "P2", "P3", "P4", "P5", "P6", "P7", "P8", "P10", "P11", "P12")


def psum_plan():
    count = [0] * 8
    uses = {}

    def use(name, l, bank):
        uses[name, l] = (bank, count[bank])
        count[bank] += 1

    for l in range(DEPTH):
        for name, bank in (("T0", 0), ("T1", 1), ("T2", 0), ("T3", 1), ("P0", 0), ("P1", 1), ("LW", 2), ("LA", 3),
                           ("P2", 0), ("P3", 1), ("G", 4), ("P4", 0), ("P5", 1), ("P6", 0),
                           ("Z0", 5), ("Z1", 6), ("Z2", 7), ("KN", 2), ("P7", 1), ("P8", 0), ("P9", 1), ("P10", 0),
                           ("GA", 3), ("VT", 4), ("ZC0", 5), ("ZC1", 6), ("ZC2", 7), ("P11", 1), ("P12", 0),
                           ("CO", 5), ("BON", 2), ("BKT", 6), ("KDT", 7), ("GAT", 3),
                           ("BG00", 2), ("BG01", 4), ("KG00", 5), ("KG01", 6), ("LP0", 7),
                           ("KV0", 2), ("KV1", 4), ("KV2", 5), ("GO", 6),
                           ("BG10", 2), ("BG11", 3), ("KG10", 4), ("KG11", 5), ("LP1", 7)):
            use(name, l, bank)
        a_steps = (("QT", 0), ("KT", 1), None, ("S0", 0), ("S10", 1), ("S11", 0), None,
                   ("PT0", 1), ("PT1", 0), ("PT2", 1), None, ("AO", 0), None)
        at = 0
        for names in ROUNDS:
            while at < len(a_steps) and a_steps[at] is not None:
                use(a_steps[at][0], l, a_steps[at][1])
                at += 1
            at += 1
            for c in range(NT):
                for n in names:
                    use(f"{n}_{c}", l, 2 + 3 * c + ROUND_BANK[n])
        for name, bank in (("RH0", 2), ("U0", 3), ("Y0", 4), ("SU", 2), ("RH1", 5), ("U1", 6), ("Y1", 7),
                           ("M0", 0), ("M1", 1), ("M2", 0), ("M3", 1), ("O0", 2), ("O1", 3), ("O2", 4), ("O3", 5),
                           ("F0", 0), ("F1", 1), ("F2", 0), ("F3", 1)):
            use(name, l, bank)
        if l % 2 == 0:
            for j in range(D_FF // P):
                use(f"up{j}", l, j % 2)
            for i in range(4):
                use(f"dn{i}", l, 2 + i)
        else:
            for name, bank in (("RT", 6), ("POS", 7), ("G0", 6), ("G1", 7)):
                use(name, l, bank)
    return uses, count


ROUNDS = (("N2", "N2t"), ("N4", "N4t", "T2", "T2t"), ("N8", "T3", "T3t"), ("T4", "T4t"),
          ("Xa",), ("Ta", "Tat"), ("Xb",), ("Tb", "Tbt"), ("Xc",), ("Tct",))
ROUND_BANK = {"N2": 0, "N2t": 1, "N4": 2, "N4t": 0, "T2": 1, "T2t": 2, "N8": 0, "T3": 1, "T3t": 2,
              "T4": 0, "T4t": 1, "Xa": 2, "Ta": 0, "Tat": 1, "Xb": 2, "Tb": 0, "Tbt": 1, "Xc": 2, "Tct": 0}


def build(nc, t_in, out):
    ctx = ExitStack()
    with ctx:
        def sb(name, shape, dt=F32):
            return ctx.enter_context(nc.sbuf_tensor(name, shape, dt))

        x_sb = sb("x_sb", [P, NT, D])
        tok = sb("tok", [P, NT, D])
        hT = sb("hT", [P, KC, SEQ])
        hT_flat = hT[:, :, :].rearrange("p c t -> p (c t)")
        consts = sb("consts", [P, N_CONST])
        params = sb("params", [P, N_PARAM])
        rows = sb("rows", [P, N_ROWS])
        lora = sb("lora", [P, 256 + 256 + 128])
        router_sb = sb("router_sb", [P, KC, N_EXPERTS])
        ring = sb("ring", [P, SLOTS, SLOT])
        region_e = sb("region_e", [P, 8192])
        region_f = sb("region_f", [P, 4096])
        region_g = sb("region_g", [P, 3072])
        region_m = sb("region_m", [P, 5128])
        normed = sb("normed", [P, 2, 512])
        ar = sb("ar", [P, 2, 2, NT, 256])
        c_q = sb("c_q", [P, 2, 2, SEQ])
        b_q = sb("b_q", [P, 4, SEQ])
        b_att = sb("b_att", [P, NT, 4, P])
        a_k = sb("a_k", [P, 2, SEQ])
        small = sb("small", [P, 160])
        pos_i = sb("pos_i", [P, NT], I32)
        trig = sb("trig", [P, 6, 2 * 32])

        banks = [ctx.enter_context(nc.psum_tensor(f"bank{i}", [P, 512], F32)) for i in range(8)]

        def const(name):
            at, n = CONST[name]
            return consts[:, at:at + n]

        def param(name, c, p0=0, p1=P):
            at = PARAM[name][0] + c
            return params[p0:p1, at:at + 1]

        def row(name):
            at, n = ROWS[name]
            return rows[:, at:at + n]

        ident = const("ident")

        def over(ap, n):
            return ap.unsqueeze(1).broadcast_to([ap.shape[0], n, ap.shape[1]])

        def along(ap, n):
            return ap.unsqueeze(2).broadcast_to([ap.shape[0], ap.shape[1], n])

        def E(a, n):
            return region_e[:, a:a + n]

        mixed = E(0, 2048).rearrange("p (c t) -> p c t", c=8)
        temps = [E(2048 + 512 * i, 512) for i in range(12)]
        d_lw, d_cum, d_cen, d_ep, d_em, d_es, d_a, d_kk, d_kk2, d_rn, d_kp, d_tmp = temps
        lg = E(0, 2048).rearrange("p (c h n) -> p c h n", c=NT, h=4)
        mg = E(2048, 2048).rearrange("p (c h n) -> p c h n", c=NT, h=4)

        def inverse_buffers(base):
            v = [base[:, 512 * i:512 * i + 512] for i in range(8)]
            return {"N": v[0], "Nt": v[1], "N2": v[2], "N2t": v[3], "N4": v[0], "N4t": v[1], "N8": v[2],
                    "T": v[4], "Tt": v[5], "Et": v[6], "X": v[7], "L": v[7]}

        inv = [inverse_buffers(region_e[:, 4096:8192]), inverse_buffers(region_f[:, 0:4096])]
        G = [region_g[:, 512 * i:512 * i + 512] for i in range(6)]
        d_bt, d_kt, d_rk, d_v, d_g, d_bk = G
        raw = region_m[:, 0:2056].rearrange("p (c t) -> p c t", c=8)
        d_th = region_m[:, 2056:2312]
        d_gl = region_m[:, 2312:2568]
        b_raw = region_m[:, 2568:3080].rearrange("p (c t) -> p c t", c=2)
        b_v = region_m[:, 3080:3592].rearrange("p (t n) -> p t n", t=NT)
        b_g = region_m[:, 3592:4104].rearrange("p (t n) -> p t n", t=NT)
        b_lr = d_th
        a_raw = region_m[:, 4104:4872].rearrange("p (t s d) -> p t s d", t=NT, s=6)
        a_v = region_m[:, 4872:5128].rearrange("p (t n) -> p t n", t=NT)
        b_x = region_m[:, 0:256]
        b_e = region_m[:, 256:512]
        b_cum = region_m[:, 512:768]
        b_arg = region_m[:, 768:1792]
        b_kh = hT_flat[:, 0:256]
        b_qd = hT_flat[:, 256:512]
        b_kd = hT_flat[:, 512:768]
        b_kdt = hT_flat[:, 768:1024].rearrange("p (t n) -> p t n", t=NT)
        b_kv = hT_flat[:, 1024:1792].rearrange("p (n f) -> p n f", n=3)
        a_rot = region_m[:, 0:768].rearrange("p (t s d) -> p t s d", t=NT, s=6)
        a_t1 = region_m[:, 768:1152].rearrange("p (t s d) -> p t s d", t=NT, s=6)
        a_t2 = region_m[:, 1152:1536].rearrange("p (t s d) -> p t s d", t=NT, s=6)
        a_s0 = region_m[:, 2568:3080].rearrange("p (s k) -> p s k", s=4)
        a_s1 = region_m[:, 3080:4104].rearrange("p (s k) -> p s k", s=4)
        a_pt = hT_flat[:, 0:1536].rearrange("p (n q) -> p n q", q=P)
        a_qt = hT_flat[:, 1536:2048].rearrange("p (j t) -> p j t", j=2)
        c_k = region_f[:, 0:512].rearrange("p (c t) -> p c t", c=2)
        c_v = region_f[:, 512:1024].rearrange("p (t n) -> p t n", t=NT)
        c_e = [region_f[:, 1024 + 512 * i:1536 + 512 * i] for i in range(3)]
        c_s = [region_f[:, 2560 + 512 * i:3072 + 512 * i] for i in range(3)]
        d_rh = inv[0]["N"].rearrange("p (c n) -> p c n", c=NT)
        d_u = inv[0]["Nt"].rearrange("p (c n) -> p c n", c=NT)
        d_s = inv[0]["N2"][:, 0:128].rearrange("p (j n) -> p j n", j=2)
        act_t = region_e[:, 0:22 * SEQ].rearrange("p (c t) -> p c t", c=22)
        silu_tmp = region_f[:, 0:512].rearrange("p (b t) -> p b t", b=2)
        final_row = region_f[:, 1024:2048]
        W = MAX_PASSES * N_EXPERTS + N_EXPERTS
        slot_act = region_e[:, 0:UPC * CAP].rearrange("p (c s) -> p c s", c=UPC)
        slot_silu = region_f[:, 0:2 * CAP].rearrange("p (b s) -> p b s", b=2)
        slot_h = region_m[:, 0:KC * CAP].rearrange("p (c s) -> p c s", c=KC)
        pick = region_m[:, 768:768 + NT * CAP].rearrange("p (t s) -> p t s", t=NT)
        weigh = region_m[:, 960:960 + NT * CAP].rearrange("p (t s) -> p t s", t=NT)
        weigh_t = region_m[0:CAP, 1152:1152 + SEQ].rearrange("p (t n) -> p t n", t=NT)
        slot_y = region_m[0:CAP, 1408:1408 + D]
        place = region_m[:, 2432:2432 + NT * W].rearrange("p (t i) -> p t i", t=NT)
        chosen = region_m[:, 2432 + NT * W:2432 + 2 * NT * W].rearrange("p (t i) -> p t i", t=NT)
        share = region_m[:, 2432 + 2 * NT * W:2432 + 3 * NT * W].rearrange("p (t i) -> p t i", t=NT)
        count = region_m[:, 3072:3072 + N_EXPERTS]
        most = region_m[:, 3080:3088]

        ss, ms, rstd = small[:, 0:2], small[:, 2:4], small[:, 4:6]
        h_ss, h_ms, h_rstd = small[:, 8:16], small[:, 16:24], small[:, 24:32]
        m_half = small[:, 32:40]
        a_max, a_neg, a_den, a_es = small[:, 40:48], small[:, 48:56], small[:, 56:64], small[:, 64:72]
        bonus = small[:, 72:80]
        d_end, d_arg, d_eend = small[:, 80:82], small[:, 82:84], small[:, 84:86]
        b_dec = small[:, 86:90]
        logits, comb = small[:, 96:112], small[:, 112:128]
        r_tmp, r_oh = small[:, 128:144], small[:, 144:160]
        r_s = sb("r_s", [P, 8])
        passes_i = sb("passes_i", [P, 1], I32)
        descend = sb("descend", [P, N_EXPERTS])

        def heads(ap):
            return ap.rearrange("p (g d) -> p g d", d=HD)

        uses, before_loop = psum_plan()
        full = [ctx.enter_context(nc.semaphore(f"bank{i}_full")) for i in range(8)]
        free = [ctx.enter_context(nc.semaphore(f"bank{i}_free")) for i in range(8)]
        landed = [ctx.enter_context(nc.semaphore(f"slot{i}_landed")) for i in range(SLOTS)]
        sems = {}

        def sem(name):
            if name not in sems:
                sems[name] = ctx.enter_context(nc.semaphore(name))
            return sems[name]

        def bank(name, l):
            return banks[uses[name, l][0]]

        def wait_full(eng, name, l):
            b, n = uses[name, l]
            eng.wait_ge(full[b], n + 1)

        def wait_evacuated(eng, name, l):
            b, n = uses[name, l]
            eng.wait_ge(free[b], n + 1)

        def wait_open(pe, name, l):
            b, n = uses[name, l]
            if n:
                pe.wait_ge(free[b], n)

        def fills(ins, name, l):
            ins.then_inc(full[uses[name, l][0]], 1)

        def frees(ins, name, l):
            ins.then_inc(free[uses[name, l][0]], 1)

        pieces = piece_plan()
        order = {p: n for n, p in enumerate(pieces)}
        FIRST_MOE = len(pieces)

        def slot(n):
            return n % SLOTS

        def wait_piece(pe, n):
            pe.wait_ge(landed[slot(n)], 16 * (n // SLOTS + 1))

        E_PIECES = 3 * UP2
        assert E_PIECES % SLOTS == 0
        per = [(UPC + 1) // 2, UPC // 2, 3, 2, 1, 1, 1, 1]

        def nth(i, b, k):
            return i * per[b] + before_loop[b] + k

        block = ctx.enter_context(nc.Block())

        def norm_index(l, which):
            return 2 * l + which

        @block.sync
        def _(sp):
            for t in range(NT):
                sp.dma_start(x_sb[:, t, :], t_in["x"][0, t * P:(t + 1) * P, :]).then_inc(sem("x_landed"), 16)
            down_in = [0]

            def wait_released(n):
                what, l, at, _ = pieces[n]
                if what == "w_in":
                    k = n - order["w_in", l, D_OFF + 768, 256]
                    wait_full(sp, IN_PIECES[k], l)
                elif what == "w_out":
                    if at < KC - 2:
                        sp.wait_ge(sem("w_out_used"), (KC // 2 - 1) * l + at // 2 + 1)
                    else:
                        wait_full(sp, "O3", l)
                elif what in ("w1", "w3"):
                    wait_full(sp, f"up{2 * (at // 256) + 1}", l)
                elif at < 2 * (D_FF // 256 - 1):
                    sp.wait_ge(sem("w2_used"), at // 2 + 1)
                else:
                    wait_full(sp, "dn3", l)

            def source(what, l, at, n):
                if what == "w_in":
                    return t_in["w_in"][l].rearrange("(c p) n -> p c n", p=P)[:, :, at:at + n]
                if what == "w_out":
                    return t_in["w_out"][l].rearrange("(c p) n -> p c n", p=P)[:, at:at + n, :]
                if what == "w2":
                    return t_in["ffn_w2"][l // 2].rearrange("(c p) n -> p c n", p=P)[:, at:at + n, :]
                return t_in["ffn_" + what][l // 2].rearrange("(c p) n -> p c n", p=P)[:, :, at:at + n]

            for n, (what, l, at, m) in enumerate(pieces):
                if n >= SLOTS:
                    wait_released(n - SLOTS)
                size = (KC if what in ("w_in", "w1", "w3") else D) * m
                dst = ring[:, slot(n), 0:size].rearrange("p (c n) -> p c n", n=m if size == KC * m and what not in ("w_out", "w2") else D)
                sp.dma_start(dst, source(what, l, at, m)).then_inc(landed[slot(n)], 16)

            def expert_piece(e, k):
                s = slot(FIRST_MOE + k)
                if k < 2 * UP2:
                    i = k // 2
                    m = min(256, D_FFE - 256 * i)
                    w = t_in["moe_w1" if k % 2 == 0 else "moe_w3"]
                    src = w[0, e].rearrange("(c p) n -> p c n", p=P)[:, :, 256 * i:256 * i + m]
                    dst = ring[:, s, 0:KC * m].rearrange("p (c n) -> p c n", n=m)
                else:
                    i = k - 2 * UP2
                    m = min(2, UPC - 2 * i)
                    src = t_in["moe_w2"][0, e].rearrange("(c p) n -> p c n", p=P)[:, 2 * i:2 * i + m, :]
                    dst = ring[:, s, 0:m * D].rearrange("p (c n) -> p c n", n=D)
                sp.dma_start(dst, src).then_inc(landed[s], 16)

            def expert_released(i, k):
                if k < 2 * UP2:
                    j = min(2 * (k // 2) + 1, UPC - 1)
                    sp.wait_ge(full[j % 2], nth(i, j % 2, j // 2 + 1))
                elif k < E_PIECES - 1:
                    sp.wait_ge(sem("moe_w2_used"), i * (UP2 - 1) + k - 2 * UP2 + 1)
                else:
                    sp.wait_ge(full[3], nth(i, 3, 1))
                sp.sem_inc(sem("slot_turns"), 1)

            for k in range(SLOTS):
                wait_released(FIRST_MOE + k - SLOTS)
                expert_piece(0, k)
            sp.wait_ge(sem("passes_ready"), 1)
            n = sp.value_load(passes_i[0:1, 0:1], min_val=1, max_val=MAX_PASSES)
            with sp.Fori(0, n * N_EXPERTS - 1) as i:
                for k in range(SLOTS, E_PIECES):
                    expert_released(i, k - SLOTS)
                    expert_piece(i % N_EXPERTS, k)
                for k in range(SLOTS):
                    expert_released(i, k + E_PIECES - SLOTS)
                    expert_piece((i + 1) % N_EXPERTS, k)
            last_i = n * N_EXPERTS - 1
            for k in range(SLOTS, E_PIECES):
                expert_released(last_i, k - SLOTS)
                expert_piece(N_EXPERTS - 1, k)
            for t in range(NT):
                sp.wait_ge(sem("out_ready"), t + 1)
                sp.dma_start(out[0, t * P:(t + 1) * P, :], tok[:, t, :]).then_inc(sem("stored"), 16)
            sp.wait_ge(sem("stored"), 32)

        @block.tensor
        def _(pe):
            def mm(o, lhsT, rhs, start=False, stop=False):
                return nc.tensor.matmul(o, lhsT, rhs, start=start, stop=stop, skip_group_check=True)

            def to_features(names, l):
                for c2 in range(4):
                    wait_open(pe, names[c2], l)
                    for t in range(NT):
                        for cc in range(2):
                            last = nc.tensor.transpose(bank(names[c2], l)[:, cc * 256 + t * P:cc * 256 + t * P + P],
                                                       tok[:, t, (2 * c2 + cc) * P:(2 * c2 + cc + 1) * P], ident)
                    fills(last, names[c2], l)

            def project_features(name, l, n, cols):
                wait_piece(pe, n)
                wait_open(pe, name, l)
                w = ring[:, slot(n), 0:KC * pieces[n][3]].rearrange("p (c n) -> p c n", c=KC)
                for j, (c0, m) in enumerate(cols):
                    for k in range(KC):
                        last = mm(bank(name, l)[0:m, j * SEQ:(j + 1) * SEQ], w[:, k, c0:c0 + m], hT[:, k, :],
                                  start=(j == 0 and k == 0), stop=(k == KC - 1))
                fills(last, name, l)

            def project_tokens(name, l, n, m):
                wait_piece(pe, n)
                wait_open(pe, name, l)
                w = ring[:, slot(n), 0:KC * pieces[n][3]].rearrange("p (c n) -> p c n", c=KC)
                for t in range(NT):
                    for k in range(KC):
                        last = mm(bank(name, l)[:, t * m:(t + 1) * m], hT[:, k, t * P:(t + 1) * P], w[:, k, 0:m],
                                  start=(t == 0 and k == 0), stop=(k == KC - 1))
                fills(last, name, l)

            def layer_mixers(l):
                both = ((0, 128), (128, 128))
                n0 = order["w_in", l, D_OFF + 768, 256]
                pe.wait_ge(sem("h_ready"), NT * (norm_index(l, 0) + 1))
                to_features(("T0", "T1", "T2", "T3"), l)
                wait_evacuated(pe, "T2", l)
                wait_evacuated(pe, "T3", l)
                project_features("P0", l, n0, both)
                project_features("P1", l, n0 + 1, both)
                pe.wait_ge(sem("lora_in"), l + 1)
                wait_open(pe, "LW", l)
                for j in range(2):
                    last = mm(bank("LW", l)[:, j * SEQ:(j + 1) * SEQ], lora[0:64, j * P:(j + 1) * P], d_th[0:64, :],
                              start=(j == 0), stop=True)
                fills(last, "LW", l)
                wait_open(pe, "LA", l)
                pe.wait_ge(sem("al_mixed"), l + 1)
                for j in range(2):
                    last = mm(bank("LA", l)[:, j * SEQ:(j + 1) * SEQ], lora[64:128, j * P:(j + 1) * P],
                              mixed[64:128, 6, :], start=(j == 0), stop=True)
                fills(last, "LA", l)
                project_features("P2", l, n0 + 2, both)
                project_features("P3", l, n0 + 3, both)
                wait_open(pe, "G", l)
                pe.wait_ge(sem("gl_sig"), l + 1)
                for t in range(NT):
                    last = mm(bank("G", l)[:, t * GW:(t + 1) * GW], d_gl[:, t * P:(t + 1) * P], lora[:, 256:512],
                              start=(t == 0), stop=True)
                fills(last, "G", l)
                project_features("P4", l, n0 + 4, both)
                project_features("P5", l, n0 + 5, both)
                project_tokens("P6", l, n0 + 6, GW)
                wait_evacuated(pe, "P4", l)
                wait_evacuated(pe, "P5", l)
                for j in range(2):
                    name = f"Z{j}"
                    wait_open(pe, name, l)
                    z = bank(name, l)
                    mm(z[:, :], c_k[:, j, 0:P], c_q[:, j, :, :].rearrange("p h t -> p (h t)"), start=True)
                    fills(mm(z[:, :].rearrange("p (h t) -> p h t", h=2)[:, :, 0:P], ident, over(const("c_mask"), 2),
                             stop=True), name, l)
                wait_open(pe, "Z2", l)
                z = bank("Z2", l)
                for j in range(2):
                    mm(z[:, j * 256:(j + 1) * 256].rearrange("p (h t) -> p h t", h=2), c_k[:, j, P:SEQ],
                       c_q[:, j, :, P:SEQ], start=(j == 0))
                fills(mm(z[:, :].rearrange("p (h t) -> p h t", h=4), ident, over(const("c_mask"), 4), stop=True), "Z2", l)
                wait_open(pe, "KN", l)
                pe.wait_ge(sem("kk_squared"), l + 1)
                fills(mm(bank("KN", l)[:, :], const("same_head"), d_kk2, start=True, stop=True), "KN", l)
                project_features("P7", l, n0 + 7, both)
                project_tokens("P8", l, n0 + 8, GW)
                project_tokens("P9", l, n0 + 9, GW)
                project_features("P10", l, n0 + 9, ((256, LR),))
                wait_evacuated(pe, "P10", l)
                wait_open(pe, "GA", l)
                fills(mm(bank("GA", l)[:, 0:SEQ], lora[0:LR, 512:640], b_lr[0:LR, :], start=True, stop=True), "GA", l)
                wait_open(pe, "VT", l)
                pe.wait_ge(sem("v_mixed"), l + 1)
                for t in range(NT):
                    for j in range(2):
                        last = nc.tensor.transpose(bank("VT", l)[:, t * GW + j * P:t * GW + (j + 1) * P],
                                                   mixed[:, 4 + j, t * P:(t + 1) * P], ident)
                fills(last, "VT", l)
                for i in range(3):
                    wait_evacuated(pe, f"Z{i}", l)
                for j in range(2):
                    wait_open(pe, f"ZC{j}", l)
                    z = bank(f"ZC{j}", l)
                    mm(z[:, :], const("rev_cum"), c_s[j])
                    fills(mm(z[:, :].rearrange("p (h t) -> p h t", h=2)[:, :, P:SEQ], const("rev_all"),
                             c_s[2][:, j * 256:(j + 1) * 256].rearrange("p (h t) -> p h t", h=2), stop=True),
                          f"ZC{j}", l)
                wait_open(pe, "ZC2", l)
                fills(mm(bank("ZC2", l)[:, :], const("rev_cum"), c_s[2], stop=True), "ZC2", l)
                project_tokens("P11", l, n0 + 10, GW)
                project_tokens("P12", l, n0 + 11, GW)
                for i in range(3):
                    wait_evacuated(pe, f"ZC{i}", l)
                wait_evacuated(pe, "P6", l)
                wait_open(pe, "CO", l)
                for h in range(4):
                    j, hh = h // 2, h % 2
                    a0 = c_e[j].rearrange("p (h t) -> p h t", h=2)
                    a1 = c_e[2].rearrange("p (h t) -> p h t", h=4)
                    v = slice(h * HD, (h + 1) * HD)
                    o = bank("CO", l)
                    mm(o[:, h * HD:(h + 1) * HD], a0[:, hh, 0:P], c_v[:, 0, v], start=(h == 0), stop=True)
                    mm(o[:, GW + h * HD:GW + (h + 1) * HD], a0[:, hh, P:SEQ], c_v[:, 0, v])
                    last = mm(o[:, GW + h * HD:GW + (h + 1) * HD], a1[:, h, :], c_v[:, 1, v], stop=True)
                fills(last, "CO", l)
                pe.wait_ge(sem("rk_ready"), l + 1)
                wait_open(pe, "BON", l)
                for t in range(NT):
                    for j in range(2):
                        last = mm(bank("BON", l)[:, t * 4 + 2 * j:t * 4 + 2 * j + 2],
                                  d_rk[:, j * SEQ + t * P:j * SEQ + (t + 1) * P], const("head_sel"),
                                  start=(t == 0 and j == 0), stop=True)
                fills(last, "BON", l)
                pe.wait_ge(sem("bk_ready"), l + 1)
                wait_open(pe, "BKT", l)
                for i, src in enumerate((d_bt, d_kt)):
                    for j in range(2):
                        last = nc.tensor.transpose(bank("BKT", l)[:, i * 256 + j * P:i * 256 + (j + 1) * P],
                                                   src[:, j * SEQ:j * SEQ + P], ident)
                fills(last, "BKT", l)
                pe.wait_ge(sem("gla_ready"), l + 1)
                wait_open(pe, "KDT", l)
                for t in range(NT):
                    last = nc.tensor.transpose(bank("KDT", l)[:, t * P:(t + 1) * P], b_kd[:, t * P:(t + 1) * P], ident)
                fills(last, "KDT", l)
                wait_open(pe, "GAT", l)
                for n in range(4):
                    p0 = (n % 2) * 64
                    o = bank("GAT", l)[p0:p0 + 64, (n // 2) * 256:(n // 2) * 256 + 256]
                    last = mm(o.rearrange("p (h t) -> p h t", h=4), b_kh[:, n * 64:(n + 1) * 64],
                              b_q[:, :, n * 64:(n + 1) * 64], start=(n < 2), stop=True)
                fills(last, "GAT", l)
                grams(l, 0)
                wait_evacuated(pe, "KDT", l)
                wait_evacuated(pe, "P8", l)
                for n in range(3):
                    p0 = (n % 2) * 64
                    wait_open(pe, f"KV{n}", l)
                    fills(mm(bank(f"KV{n}", l)[:, 0:256], b_kdt[p0:p0 + 64, n // 2, :], b_v[p0:p0 + 64, n // 2, :],
                             start=True, stop=True), f"KV{n}", l)
                wait_evacuated(pe, "GAT", l)
                wait_open(pe, "GO", l)
                o = bank("GO", l)
                for t in range(NT):
                    for h in range(4):
                        mm(o[:, t * GW + h * HD:t * GW + (h + 1) * HD], b_att[:, t, h, :],
                           b_v[:, t, h * HD:(h + 1) * HD], start=(t == 0 and h == 0), stop=True)
                pe.wait_ge(sem("gla_state"), l + 1)
                for n in range(1, 4):
                    p0 = (n % 2) * 64
                    last = mm(o[p0:p0 + 64, (n // 2) * GW:(n // 2 + 1) * GW], b_qd[:, n * 64:(n + 1) * 64],
                              b_kv[:, n - 1, :], stop=True)
                fills(last, "GO", l)
                grams(l, 1)
                steps = [a_transpose, a_scores, a_probs, a_output]
                for r in range(len(ROUNDS)):
                    if r < len(steps):
                        steps[r](l)
                    for c in range(NT):
                        inverse_round(l, r, c)
                recurrence(l)

            def grams(l, c):
                if c == 0:
                    pe.wait_ge(sem("ar_ready"), l + 1)
                for kind, src in (("BG", d_bt), ("KG", d_kt)):
                    for j in range(2):
                        name = f"{kind}{c}{j}"
                        wait_open(pe, name, l)
                        fills(mm(bank(name, l)[:, :].rearrange("p (h n) -> p h n", h=2),
                                 src[:, j * SEQ + c * P:j * SEQ + (c + 1) * P], ar[:, j, :, c, :],
                                 start=True, stop=True), name, l)
                wait_open(pe, f"LP{c}", l)
                for h in range(4):
                    last = mm(bank(f"LP{c}", l)[:, h * P:(h + 1) * P], ar[:, h // 2, h % 2, c, 0:P],
                              d_bt[:, (h // 2) * SEQ + c * P:(h // 2) * SEQ + (c + 1) * P], start=(h == 0), stop=True)
                fills(last, f"LP{c}", l)

            PRODUCTS = {"N2": ("Nt", "N"), "N2t": ("N", "Nt"), "N4": ("N2t", "N2"), "N4t": ("N2", "N2t"),
                        "T2": ("Tt", "N2"), "T2t": ("N2", "Tt"), "N8": ("N4t", "N4"), "T3": ("Tt", "N4"),
                        "T3t": ("N4", "Tt"), "T4": ("Tt", "N8"), "T4t": ("N8", "Tt"),
                        "X": ("Et", "T"), "T": ("Tt", "X"), "Tt": ("X", "Tt")}

            def inverse_round(l, r, c):
                buf = inv[c]
                if r == 0:
                    pe.wait_ge(sem(f"n_ready{c}"), l + 1)
                else:
                    for name in ROUNDS[r - 1]:
                        wait_evacuated(pe, f"{name}_{c}", l)
                if r == 1:
                    pe.wait_ge(sem(f"t_ready{c}"), l + 1)
                if r in (4, 6, 8):
                    pe.wait_ge(sem(f"e_ready{c}"), 3 * l + (r - 4) // 2 + 1)
                for name in ROUNDS[r]:
                    key = name if r < 4 else {"X": "X", "T": "T"}[name[0]] + ("t" if name.endswith("t") else "")
                    a, b = PRODUCTS[key]
                    wait_open(pe, f"{name}_{c}", l)
                    for h in range(4):
                        s = slice(h * P, (h + 1) * P)
                        last = mm(bank(f"{name}_{c}", l)[:, s], buf[a][:, s], buf[b][:, s], start=(h == 0), stop=True)
                    fills(last, f"{name}_{c}", l)

            def a_transpose(l):
                pe.wait_ge(sem("rotated"), l + 1)
                for name, slots, o in (("QT", (0, 1), 0), ("KT", (2,), 0)):
                    wait_open(pe, name, l)
                    for i, s in enumerate(slots):
                        for t in range(NT):
                            last = nc.tensor.transpose(
                                bank(name, l)[:, i * SEQ + t * P:i * SEQ + (t + 1) * P],
                                a_rot[:, t, 2 * s:2 * s + 2, :].rearrange("p s d -> p (s d)"), ident)
                    fills(last, name, l)

            def a_scores(l):
                wait_evacuated(pe, "QT", l)
                wait_evacuated(pe, "KT", l)
                wait_open(pe, "S0", l)
                for j in range(2):
                    last = mm(bank("S0", l)[:, j * 256:(j + 1) * 256].rearrange("p (g k) -> p g k", g=2),
                              a_qt[:, j, 0:P], a_k[:, :, 0:P], start=(j == 0), stop=True)
                fills(last, "S0", l)
                for j in range(2):
                    wait_open(pe, f"S1{j}", l)
                    fills(mm(bank(f"S1{j}", l)[:, :], a_qt[:, j, P:SEQ], a_k[:, :, :].rearrange("p g k -> p (g k)"),
                             start=True, stop=True), f"S1{j}", l)

            def a_probs(l):
                pe.wait_ge(sem("probs"), l + 1)
                for i in range(3):
                    wait_open(pe, f"PT{i}", l)
                    for s in range(4):
                        src = a_s0[:, s, :] if i == 0 else a_s1[:, s, (i - 1) * P:i * P]
                        last = nc.tensor.transpose(bank(f"PT{i}", l)[:, s * P:(s + 1) * P], src, ident)
                    fills(last, f"PT{i}", l)

            def a_output(l):
                for i in range(3):
                    wait_evacuated(pe, f"PT{i}", l)
                wait_open(pe, "AO", l)
                o = bank("AO", l)
                for s in range(4):
                    g = s % 2
                    v = slice(g * HD, (g + 1) * HD)
                    c = slice(s * HD, (s + 1) * HD)
                    mm(o[:, c], a_pt[:, s, :], a_v[:, 0, v], start=(s == 0), stop=True)
                    c = slice(GW + s * HD, GW + (s + 1) * HD)
                    mm(o[:, c], a_pt[:, 4 + s, :], a_v[:, 0, v])
                    last = mm(o[:, c], a_pt[:, 8 + s, :], a_v[:, 1, v], stop=True)
                fills(last, "AO", l)

            def recurrence(l):
                for c in range(NT):
                    name = f"RH{c}"
                    if c == 1:
                        pe.wait_ge(sem("state"), l + 1)
                    wait_open(pe, name, l)
                    for h in range(4):
                        o = bank(name, l)[:, h * HD:(h + 1) * HD]
                        last = mm(o, mg[:, c, h, 0:P], d_v[:, c * GW + h * HD:c * GW + (h + 1) * HD],
                                  start=(h == 0), stop=(c == 0))
                        if c == 1:
                            last = mm(o, ar[:, h // 2, h % 2, 1, 0:P], d_s[:, h // 2, :], stop=True)
                    fills(last, name, l)
                    wait_evacuated(pe, name, l)
                    wait_evacuated(pe, f"Tct_{c}", l)
                    wait_open(pe, f"U{c}", l)
                    for h in range(4):
                        last = mm(bank(f"U{c}", l)[:, h * HD:(h + 1) * HD], inv[c]["Tt"][:, h * P:(h + 1) * P],
                                  d_rh[:, c, h * HD:(h + 1) * HD], start=(h == 0), stop=True)
                    fills(last, f"U{c}", l)
                    wait_evacuated(pe, f"U{c}", l)
                    if c == 0:
                        wait_open(pe, "SU", l)
                        for j in range(2):
                            o = bank("SU", l)[:, j * P:(j + 1) * P]
                            mm(o, d_bk[:, j * P:(j + 1) * P], d_u[:, 0, j * P:(j + 1) * P], start=(j == 0))
                            last = mm(o, d_bk[:, 256 + j * P:256 + (j + 1) * P], d_v[:, j * P:(j + 1) * P], stop=True)
                        fills(last, "SU", l)
                    wait_open(pe, f"Y{c}", l)
                    for h in range(4):
                        o = bank(f"Y{c}", l)[:, h * HD:(h + 1) * HD]
                        s = slice(h * HD, (h + 1) * HD)
                        mm(o, lg[:, c, h, P:256], d_u[:, c, s], start=(h == 0))
                        last = mm(o, mg[:, c, h, P:256], d_v[:, c * GW + h * HD:c * GW + (h + 1) * HD], stop=(c == 0))
                        if c == 1:
                            last = mm(o, ar[:, h // 2, h % 2, 1, P:256], d_s[:, h // 2, :], stop=True)
                    fills(last, f"Y{c}", l)

            def output_projection(l):
                pe.wait_ge(sem("mix_ready"), l + 1)
                to_features(("M0", "M1", "M2", "M3"), l)
                wait_evacuated(pe, "M2", l)
                wait_evacuated(pe, "M3", l)
                for i in range(4):
                    wait_open(pe, f"O{i}", l)
                for k2 in range(KC // 2):
                    n = order["w_out", l, 2 * k2, 2]
                    wait_piece(pe, n)
                    w = ring[:, slot(n), 0:2 * D].rearrange("p (c n) -> p c n", c=2)
                    for i in range(4):
                        t, half = i // 2, i % 2
                        for kk in range(2):
                            k = 2 * k2 + kk
                            last = mm(bank(f"O{i}", l)[:, :], hT[:, k, t * P:(t + 1) * P],
                                      w[:, kk, half * 512:(half + 1) * 512], start=(k == 0), stop=(k == KC - 1))
                        if k2 == KC // 2 - 1:
                            fills(last, f"O{i}", l)
                    if k2 < KC // 2 - 1:
                        last.then_inc(sem("w_out_used"), 1)

            def up_chunk(o, w1, w3):
                for i, w in enumerate((w1, w3)):
                    for k in range(KC):
                        last = mm(o[:, i * SEQ:(i + 1) * SEQ], w[:, k, :], hT[:, k, :], start=(i == 0 and k == 0),
                                  stop=(k == KC - 1))
                return last

            def dense(l):
                for i in range(D_FF // 256):
                    n1, n3 = order["w1", l, 256 * i, 256], order["w3", l, 256 * i, 256]
                    wait_piece(pe, n1)
                    wait_piece(pe, n3)
                    w1 = ring[:, slot(n1), 0:KC * 256].rearrange("p (c n) -> p c n", c=KC)
                    w3 = ring[:, slot(n3), 0:KC * 256].rearrange("p (c n) -> p c n", c=KC)
                    for jj in range(2):
                        name = f"up{2 * i + jj}"
                        wait_open(pe, name, l)
                        fills(up_chunk(bank(name, l), w1[:, :, jj * P:(jj + 1) * P], w3[:, :, jj * P:(jj + 1) * P]),
                              name, l)
                for i in range(4):
                    wait_open(pe, f"dn{i}", l)
                steps = D_FF // 256
                for k2 in range(steps):
                    n = order["w2", l, 2 * k2, 2]
                    wait_piece(pe, n)
                    wait_evacuated(pe, f"up{2 * k2}", l)
                    wait_evacuated(pe, f"up{2 * k2 + 1}", l)
                    w = ring[:, slot(n), 0:2 * D].rearrange("p (c n) -> p c n", c=2)
                    for i in range(4):
                        t, half = i // 2, i % 2
                        for kk in range(2):
                            k = 2 * k2 + kk
                            last = mm(bank(f"dn{i}", l)[:, :], act_t[:, k, t * P:(t + 1) * P],
                                      w[:, kk, half * 512:(half + 1) * 512], start=(k == 0), stop=(k == 2 * steps - 1))
                        if k2 == steps - 1:
                            fills(last, f"dn{i}", l)
                    if k2 < steps - 1:
                        last.then_inc(sem("w2_used"), 1)

            def experts(l):
                wait_open(pe, "RT", l)
                for t in range(NT):
                    for k in range(KC):
                        last = mm(bank("RT", l)[:, t * N_EXPERTS:(t + 1) * N_EXPERTS], hT[:, k, t * P:(t + 1) * P],
                                  router_sb[:, k, :], start=(t == 0 and k == 0), stop=(k == KC - 1))
                fills(last, "RT", l)

                pe.wait_ge(sem("chosen_ready"), 1)
                wait_open(pe, "POS", l)
                o = bank("POS", l)
                before, sel = const("upper")[:, 0:P], (chosen[:, 0, 0:N_EXPERTS], chosen[:, 1, 0:N_EXPERTS])
                mm(o[:, 0:8], before, sel[0], start=True, stop=True)
                mm(o[:, 8:16], const("all"), sel[0])
                mm(o[:, 8:16], before, sel[1], stop=True)
                mm(o[:, 16:24], const("all"), sel[0])
                fills(mm(o[:, 16:24], const("all"), sel[1], stop=True), "POS", l)

                def gather(b, waits):
                    for h in range(2):
                        if waits is not None:
                            pe.wait_ge(free[6 + h], waits[h])
                        for c in range(4):
                            for t in range(NT):
                                last = mm(banks[6 + h][:, c * CAP:(c + 1) * CAP],
                                          tok[:, t, (4 * h + c) * P:(4 * h + c + 1) * P], pick[:, t, :],
                                          start=(c == 0 and t == 0), stop=(t == NT - 1))
                        last.then_inc(full[6 + h], 1)

                pe.wait_ge(sem("picks"), 1)
                wait_open(pe, "G0", l)
                wait_open(pe, "G1", l)
                gather(0, None)

                def landed_piece(i, k):
                    n = FIRST_MOE + k
                    pe.wait_ge(landed[slot(n)], i * (16 * (E_PIECES // SLOTS)) + 16 * (n // SLOTS + 1))
                    return slot(n)

                pe.wait_ge(sem("passes_ready"), 1)
                n_passes = pe.value_load(passes_i[0:1, 0:1], min_val=1, max_val=MAX_PASSES)
                with pe.Fori(0, n_passes * N_EXPERTS) as i:
                    pe.wait_ge(free[6], nth(i, 6, 0))
                    pe.wait_ge(free[7], nth(i, 7, 0))
                    for p2 in range(UP2):
                        m = min(256, D_FFE - 256 * p2)
                        s1 = landed_piece(i, 2 * p2)
                        s3 = landed_piece(i, 2 * p2 + 1)
                        w1 = ring[:, s1, 0:KC * m].rearrange("p (c n) -> p c n", c=KC)
                        w3 = ring[:, s3, 0:KC * m].rearrange("p (c n) -> p c n", c=KC)
                        for jj in range(m // P):
                            j = 2 * p2 + jj
                            b = j % 2
                            pe.wait_ge(free[b], nth(i, b, j // 2))
                            for f, w in enumerate((w1, w3)):
                                for k in range(KC):
                                    last = mm(banks[b][:, f * CAP:(f + 1) * CAP], w[:, k, jj * P:(jj + 1) * P],
                                              slot_h[:, k, :], start=(f == 0 and k == 0), stop=(k == KC - 1))
                            last.then_inc(full[b], 1)
                    pe.wait_ge(sem("weighs"), i + 1)
                    pe.wait_ge(free[2], nth(i, 2, 0))
                    for t in range(NT):
                        last = nc.tensor.transpose(banks[2][0:CAP, t * P:(t + 1) * P], weigh[:, t, :], ident)
                    last.then_inc(full[2], 1)
                    pe.wait_ge(sem("picks"), i + 2)
                    gather(i, (nth(i, 6, 0), nth(i, 7, 0)))
                    pe.wait_ge(free[2], nth(i, 2, 1))
                    pe.wait_ge(free[3], nth(i, 3, 0))
                    for k2 in range(UP2):
                        m = min(2, UPC - 2 * k2)
                        s2 = landed_piece(i, 2 * UP2 + k2)
                        w = ring[:, s2, 0:m * D].rearrange("p (c n) -> p c n", c=m)
                        for kk in range(m):
                            j = 2 * k2 + kk
                            pe.wait_ge(free[j % 2], nth(i, j % 2, j // 2 + 1))
                        for half in range(2):
                            for kk in range(m):
                                k = 2 * k2 + kk
                                last = mm(banks[2 + half][0:CAP, :], slot_act[:, k, :],
                                          w[:, kk, half * 512:(half + 1) * 512], start=(k == 0), stop=(k == UPC - 1))
                            if k2 == UP2 - 1:
                                last.then_inc(full[2 + half], 1)
                        if k2 < UP2 - 1:
                            last.then_inc(sem("moe_w2_used"), 1)
                    for q, (b, t, half) in enumerate(SCATTER):
                        pe.wait_ge(free[2 + half], nth(i, 2 + half, 2 - half))
                        if b > 3:
                            pe.wait_ge(free[b], nth(i, b, 0))
                        mm(banks[b][:, :], weigh_t[:, t, :], slot_y[:, half * 512:(half + 1) * 512],
                           start=True, stop=True).then_inc(full[b], 1)

            pe.wait_ge(sem("tables_landed"), 16)
            for l in range(DEPTH):
                pe.wait_ge(sem("params_landed"), 16 * N_PARAM_DMAS * (l + 1))
                layer_mixers(l)
                output_projection(l)
                pe.wait_ge(sem("h_ready"), NT * (norm_index(l, 1) + 1))
                to_features(("F0", "F1", "F2", "F3"), l)
                wait_evacuated(pe, "F2", l)
                wait_evacuated(pe, "F3", l)
                if l % 2 == 0:
                    dense(l)
                else:
                    pe.wait_ge(sem("router_landed"), 16)
                    experts(l)

        @block.scalar
        def _(act):
            chain = [0]

            def link(ins):
                chain[0] += 1
                ins.then_inc(sem("act_chain"), 1)
                act.wait_ge(sem("act_chain"), chain[0])

            def load_params(l):
                w2, a2 = t_in["rwkv_w2"][l], t_in["rwkv_a2"][l]
                act.dma_start(params[:, :], t_in["params"][l]).then_inc(sem("params_landed"), 16)
                act.dma_start(rows[:, :], t_in["rows"][l:l + 1, :].broadcast_to([P, N_ROWS])).then_inc(
                    sem("params_landed"), 16)
                act.dma_start(lora[0:64, 0:256], w2).then_inc(sem("params_landed"), 16)
                act.dma_start(lora[64:128, 0:256], a2).then_inc(sem("params_landed"), 16)
                act.dma_start(lora[:, 256:512], t_in["rwkv_g2"][l]).then_inc(sem("params_landed"), 16)
                act.dma_start(lora[0:LR, 512:640], t_in["gla_w_a2"][l]).then_inc(sem("params_landed"), 16)

            def square_sums(l, which):
                for t in range(NT):
                    nc.scalar.activation(tok[:, t, :], x_sb[:, t, :], ACT.Square,
                                         accum_out=ss[:, t:t + 1]).then_inc(sem("squares"), 1)

            def feature_evacuation(names, l, gain):
                for c2 in (0, 2):
                    wait_full(act, names[c2], l)
                    for cc in range(2):
                        src = bank(names[c2], l)[:, cc * 256:(cc + 1) * 256]
                        dst = hT[:, 2 * c2 + cc, :]
                        if gain is None:
                            last = nc.scalar.copy(dst, src)
                        else:
                            last = nc.scalar.activation(dst, src, ACT.Copy, scale=param(gain, 2 * c2 + cc))
                    frees(last, names[c2], l)

            def evacuate(name, l, dst, src):
                wait_full(act, name, l)
                frees(nc.scalar.copy(dst, src), name, l)

            def both(ap):
                return ap.rearrange("p (c t) -> p c t", c=2)

            def layer_mixers(l):
                feature_evacuation(("T0", "T1", "T2", "T3"), l, "attn_norm")
                evacuate("P0", l, raw[:, 6:8, 1:257], both(bank("P0", l)[:, :]))
                evacuate("P1", l, raw[:, 0:2, 1:257], both(bank("P1", l)[:, :]))
                act.wait_ge(sem("al_mixed"), l + 1)
                nc.scalar.activation(d_th[0:64, :], mixed[0:64, 6, :], ACT.Tanh).then_inc(sem("lora_in"), 1)
                act.wait_ge(sem("gl_mixed"), l + 1)
                nc.scalar.activation(d_gl, mixed[:, 7, :], ACT.Sigmoid).then_inc(sem("gl_sig"), 1)
                for name, off, dst in (("LW", "w0", d_lw), ("LA", "a0", d_a)):
                    wait_full(act, name, l)
                    for j in range(2):
                        last = nc.scalar.activation(dst[:, j * SEQ:(j + 1) * SEQ],
                                                    bank(name, l)[:, j * SEQ:(j + 1) * SEQ], ACT.Sigmoid,
                                                    bias=param(off, j))
                    frees(last, name, l)
                evacuate("P2", l, raw[:, 2:4, 1:257], both(bank("P2", l)[:, :]))
                evacuate("P3", l, raw[:, 4:6, 1:257], both(bank("P3", l)[:, :]))
                evacuate("G", l, d_g, bank("G", l)[:, :])
                wait_full(act, "P4", l)
                for hh in range(2):
                    r = slice(hh * 64, (hh + 1) * 64)
                    last = nc.scalar.mul(c_q[r, :, hh, :], both(bank("P4", l)[r, :]), HD ** -0.5)
                frees(last, "P4", l)
                evacuate("P5", l, c_k, both(bank("P5", l)[:, :]))
                evacuate("P6", l, c_v, both(bank("P6", l)[:, :]))
                act.wait_ge(sem("decays_summed"), l + 1)
                nc.scalar.activation(d_ep, d_cen, ACT.Exp)
                nc.scalar.activation(d_em, d_cen, ACT.Exp, scale=-1.0)
                nc.scalar.activation(d_es, d_es, ACT.Exp)
                nc.scalar.activation(d_eend, d_arg, ACT.Exp).then_inc(sem("decay_exps"), 1)
                for i in range(3):
                    wait_full(act, f"Z{i}", l)
                    last = nc.scalar.activation(c_e[i], bank(f"Z{i}", l)[:, :], ACT.Abs)
                link(last)
                for i in range(3):
                    last = nc.scalar.activation(c_e[i], c_e[i], ACT.Exp, scale=-1.0)
                link(last)
                for i in range(3):
                    last = nc.scalar.activation(c_e[i], c_e[i], ACT.Ln, bias=1.0)
                last.then_inc(sem("log_terms"), 1)
                act.wait_ge(sem("kk_sums"), l + 1)
                nc.scalar.activation(d_rn, d_rn, ACT.Sqrt).then_inc(sem("kk_roots"), 1)
                evacuate("P7", l, b_raw, both(bank("P7", l)[:, :]))
                evacuate("P8", l, b_v, both(bank("P8", l)[:, :]))
                wait_full(act, "P9", l)
                frees(nc.scalar.activation(b_g, both(bank("P9", l)[:, :]), ACT.Silu), "P9", l)
                evacuate("P10", l, b_lr[0:LR, :], bank("P10", l)[0:LR, 0:SEQ])
                evacuate("VT", l, d_v, bank("VT", l)[:, :])
                wait_evacuated(act, "GA", l)
                link(nc.scalar.activation(b_e, b_x, ACT.Abs))
                link(nc.scalar.activation(b_e, b_e, ACT.Exp, scale=-1.0))
                nc.scalar.activation(b_e, b_e, ACT.Ln, bias=1.0).then_inc(sem("gate_log"), 1)
                for i in range(3):
                    wait_full(act, f"ZC{i}", l)
                    frees(nc.scalar.activation(c_e[i], bank(f"ZC{i}", l)[:, :], ACT.Exp), f"ZC{i}", l)
                wait_full(act, "P11", l)
                for t in range(NT):
                    src = bank("P11", l)[:, t * GW:(t + 1) * GW].rearrange("p (g j d) -> p g j d", g=2, j=2)
                    dst = a_raw[:, t, 0:4, :].rearrange("p (j g) d -> p g j d", g=2)
                    last = nc.scalar.mul(dst, src, HD ** -0.5)
                frees(last, "P11", l)
                wait_full(act, "P12", l)
                src = bank("P12", l)[:, :].rearrange("p (t s n) -> p t s n", t=NT, s=2)
                nc.scalar.copy(a_v, src[:, :, 1, :])
                frees(nc.scalar.copy(a_raw[:, :, 4:6, :], src[:, :, 0, :].rearrange("p t (s d) -> p t s d", s=2)),
                      "P12", l)
                act.wait_ge(sem("gla_sums"), l + 1)
                nc.scalar.activation(b_arg, b_arg, ACT.Exp, scale=1.0 / 16.0).then_inc(sem("gla_exps"), 1)
                evacuate("BKT", l, d_bk, bank("BKT", l)[:, :])
                evacuate("KDT", l, b_kdt, both(bank("KDT", l)[:, 0:256]))
                for r in range(len(ROUNDS)):
                    if r == 0:
                        evacuate("QT", l, a_qt, both(bank("QT", l)[:, :]))
                    if r == 2:
                        act.wait_ge(sem("a_masked"), l + 1)
                        for s in range(4):
                            nc.scalar.activation(a_s0[:, s, :], a_s0[:, s, :], ACT.Exp, bias=a_neg[:, s:s + 1],
                                                 accum_out=a_den[:, s:s + 1])
                        for s in range(4):
                            nc.scalar.activation(a_s1[:, s, :], a_s1[:, s, :], ACT.Exp, bias=a_neg[:, 4 + s:5 + s],
                                                 accum_out=a_den[:, 4 + s:5 + s])
                        nc.scalar.activation(a_es, a_es, ACT.Exp).then_inc(sem("probs"), 1)
                        for i in range(3):
                            evacuate(f"PT{i}", l, a_pt[:, 4 * i:4 * i + 4, :],
                                     bank(f"PT{i}", l)[:, :].rearrange("p (n q) -> p n q", n=4))
                    for c in range(NT):
                        for name in ROUNDS[r]:
                            if name[0] in "NX":
                                evacuate(f"{name}_{c}", l, inv[c]["X" if name[0] == "X" else name],
                                         bank(f"{name}_{c}", l)[:, :])
                for c in range(NT):
                    wait_full(act, f"RH{c}", l)
                    frees(nc.scalar.mul(d_rh[:, c, :], bank(f"RH{c}", l)[:, 0:GW], -1.0), f"RH{c}", l)
                    evacuate(f"U{c}", l, d_u[:, c, :], bank(f"U{c}", l)[:, 0:GW])
                feature_evacuation(("M0", "M1", "M2", "M3"), l, None)

            act.dma_start(consts[:, :], t_in["consts"]).then_inc(sem("tables_landed"), 16)
            act.dma_start(pos_i[:, :], t_in["positions"]).then_inc(sem("positions_landed"), 16)
            load_params(0)
            act.dma_start(router_sb[:, :, :], t_in["router"][0].rearrange("(c p) e -> p c e", p=P)).then_inc(
                sem("router_landed"), 16)
            act.wait_ge(sem("angles"), 1)
            nc.scalar.activation(trig[:, 1, :], trig[:, 1, :], ACT.Sin)
            nc.scalar.activation(trig[:, 2, :], trig[:, 2, :], ACT.Sin).then_inc(sem("sines"), 1)
            act.wait_ge(sem("x_landed"), 32)
            act.wait_ge(sem("params_landed"), 16 * N_PARAM_DMAS)
            for l in range(DEPTH):
                if l:
                    act.wait_ge(sem("x_updated"), 2 * l)
                square_sums(l, 0)
                if l:
                    act.wait_ge(sem("params_landed"), 16 * N_PARAM_DMAS * (l + 1))
                layer_mixers(l)
                act.wait_ge(sem("x_updated"), 2 * l + 1)
                square_sums(l, 1)
                feature_evacuation(("F0", "F1", "F2", "F3"), l, "ffn_norm")
                if l + 1 < DEPTH:
                    act.wait_ge(sem("params_used"), l + 1)
                    wait_evacuated(act, "F2", l)
                    load_params(l + 1)
                if l % 2 == 0:
                    for j in range(D_FF // P):
                        wait_full(act, f"up{j}", l)
                        nc.scalar.activation(silu_tmp[:, j % 2, :], bank(f"up{j}", l)[:, 0:SEQ],
                                             ACT.Silu).then_inc(sem("silu"), 1)
                else:
                    act.wait_ge(sem("gates_shifted"), 1)
                    nc.scalar.activation(comb, comb, ACT.Exp)
                    nc.scalar.activation(r_s[:, 0:2], r_s[:, 0:2], ACT.Exp).then_inc(sem("gates_exp"), 1)
                    def slots_in(c, b):
                        return nc.scalar.activation(slot_h[:, c, :], banks[b][:, (c % 4) * CAP:(c % 4 + 1) * CAP],
                                                    ACT.Copy, scale=param("ffn_norm", c))

                    wait_full(act, "G0", l)
                    for c in range(4):
                        last = slots_in(c, 6)
                    frees(last, "G0", l)
                    act.wait_ge(sem("passes_ready"), 1)
                    n_passes = act.value_load(passes_i[0:1, 0:1], min_val=1, max_val=MAX_PASSES)
                    with act.Fori(0, n_passes * N_EXPERTS) as i:
                        for j in range(UPC):
                            b = j % 2
                            act.wait_ge(full[b], nth(i, b, j // 2 + 1))
                            nc.scalar.activation(slot_silu[:, b, :], banks[b][:, 0:CAP],
                                                 ACT.Silu).then_inc(sem("moe_silu"), 1)
                        act.wait_ge(full[2], nth(i, 2, 1))
                        nc.scalar.copy(weigh_t, banks[2][0:CAP, 0:SEQ].rearrange("p (t n) -> p t n", t=NT)).then_inc(
                            free[2], 1)
                        act.wait_ge(full[6], nth(i, 6, 1))
                        for c in range(4):
                            last = slots_in(c, 6)
                        last.then_inc(free[6], 1)
                        act.wait_ge(full[2], nth(i, 2, 2))
                        nc.scalar.copy(slot_y[:, 0:512], banks[2][0:CAP, :]).then_inc(free[2], 1)
            act.wait_ge(sem("x_updated"), 2 * DEPTH)
            square_sums(DEPTH, 0)
            act.dma_start(final_row, t_in["final_norm"].broadcast_to([P, D])).then_inc(sem("final_landed"), 16)

        @block.gpsimd
        def _(pool):
            g = nc.gpsimd

            def power(k, ap_in, ap_out, n):
                pool.wait_ge(sem("means_ready"), k)
                g.tensor_tensor(ap_out[:, 0:n], ap_in[:, 0:n], m_half[:, 0:n], ALU.pow).then_inc(sem("rstd_ready"), 1)

            g.memset(c_q[:, :, :, :], 0.0)
            g.memset(ar[:, :, :, :, :], 0.0)
            g.memset(b_q[:, :, :], 0.0)
            g.memset(b_att[:, :, :, :], 0.0)
            g.memset(a_k[:, :, :], 0.0)
            g.memset(m_half, -0.5)
            for i in range(N_EXPERTS):
                last = g.memset(descend[:, i:i + 1], float(N_EXPERTS - i))
            last.then_inc(sem("cleared"), 1)
            pool.wait_ge(sem("cleared"), 1)
            pool.wait_ge(sem("tables_landed"), 16)
            k = 0
            for l in range(DEPTH):
                k += 1
                power(k, ms, rstd, 2)
                for _ in range(2):
                    k += 1
                    power(k, h_ms, h_rstd, 8)
                for c in range(NT):
                    buf = inv[c]
                    v = {n: buf[n].rearrange("p (h n) -> p h n", h=4) for n in buf}
                    lt = lg[:, c, :, 0:P]
                    pool.wait_ge(sem(f"lt_ready{c}"), l + 1)
                    g.tensor_tensor(v["Nt"], lt, over(const("blk16"), 4), ALU.mult)
                    pool.wait_ge(sem(f"l_ready{c}"), l + 1)
                    g.tensor_tensor(v["N"], v["L"], over(const("blk16"), 4), ALU.mult).then_inc(sem(f"n_ready{c}"), 1)
                    pool.wait_ge(sem(f"n_ready{c}"), l + 1)
                    g.tensor_tensor(v["T"], v["N"], over(ident, 4), ALU.add)
                    g.tensor_tensor(v["Tt"], v["Nt"], over(ident, 4), ALU.add).then_inc(sem(f"t_ready{c}"), 1)
                    g.tensor_tensor(v["Et"], lt, over(const("off32"), 4), ALU.mult).then_inc(sem(f"e_ready{c}"), 1)
                k += 1
                power(k, h_ms, h_rstd, 8)
                for name, before in (("off64", "Xa"), ("off128", "Xb")):
                    for c in range(NT):
                        v = inv[c]["Et"].rearrange("p (h n) -> p h n", h=4)
                        wait_full(pool, f"{before}_{c}", l)
                        g.tensor_tensor(v, lg[:, c, :, 0:P], over(const(name), 4),
                                        ALU.mult).then_inc(sem(f"e_ready{c}"), 1)
                k += 1
                power(k, h_ms, h_rstd, 8)
                k += 1
                power(k, ms, rstd, 2)
            k += 1
            power(k, ms, rstd, 2)

        @block.vector
        def _(dve):
            v = nc.vector
            chain = [0]
            means = [0]

            def link(ins):
                chain[0] += 1
                ins.then_inc(sem("dve_chain"), 1)
                dve.wait_ge(sem("dve_chain"), chain[0])

            def tt(o, a, b, op):
                return v.tensor_tensor(o, a, b, op)

            def stt(o, a, s, b, op0, op1):
                return v.scalar_tensor_tensor(out=o, in0=a, scalar=s, in1=b, op0=op0, op1=op1)

            def root(ins):
                means[0] += 1
                ins.then_inc(sem("means_ready"), 1)
                dve.wait_ge(sem("rstd_ready"), means[0])

            def norm_rows(k, l, to):
                dve.wait_ge(sem("squares"), NT * (k + 1))
                root(v.tensor_scalar(ms, ss, 1.0 / D, EPS, ALU.mult, ALU.add))
                for t in range(NT):
                    v.tensor_scalar(to[:, t, :], x_sb[:, t, :], rstd[:, t:t + 1], None,
                                    ALU.mult).then_inc(sem("h_ready"), 1)

            def feature_evacuation(names, l, gain):
                for c2 in (1, 3):
                    wait_full(dve, names[c2], l)
                    for cc in range(2):
                        src = bank(names[c2], l)[:, cc * 256:(cc + 1) * 256]
                        dst = hT[:, 2 * c2 + cc, :]
                        if gain is None:
                            last = v.tensor_copy(dst, src)
                        else:
                            last = v.tensor_scalar(dst, src, param(gain, 2 * c2 + cc), None, ALU.mult)
                    frees(last, names[c2], l)

            def mix_tokens(name, l, c0):
                wait_evacuated(dve, name, l)
                link(tt(mixed[:, c0:c0 + 2, :], raw[:, c0:c0 + 2, 0:256], raw[:, c0:c0 + 2, 1:257], ALU.subtract))
                for c in (c0, c0 + 1):
                    last = stt(mixed[:, c, :], mixed[:, c, :], param("mu", c), raw[:, c, 1:257], ALU.mult, ALU.add)
                    if c == 6:
                        last.then_inc(sem("al_mixed"), 1)
                    elif c == 7:
                        last.then_inc(sem("gl_mixed"), 1)
                    elif c == 5:
                        last.then_inc(sem("v_mixed"), 1)
                    else:
                        link(last)

            def head_norm(src, gain, dst, times=None):
                link(tt(normed[:, 1, :], src, src, ALU.mult))
                link(v.tensor_reduce(h_ss, heads(normed[:, 1, :]), AX_X, ALU.add))
                root(v.tensor_scalar(h_ms, h_ss, 1.0 / HD, EPS, ALU.mult, ALU.add))
                link(tt(heads(normed[:, 1, :]), heads(src), along(h_rstd, HD), ALU.mult))
                n = normed[:, 1, :].rearrange("p (t n) -> p t n", t=NT)
                if times is None:
                    return tt(dst, n, over(gain, NT), ALU.mult)
                link(tt(n, n, over(gain, NT), ALU.mult))
                return tt(dst, n, times, ALU.mult)

            def layer_mixers(l):
                link(v.memset(raw[:, :, 0:1], 0.0))
                feature_evacuation(("T0", "T1", "T2", "T3"), l, "attn_norm")
                mix_tokens("P0", l, 6)
                mix_tokens("P1", l, 0)
                wait_evacuated(dve, "LW", l)
                link(v.tensor_scalar(d_lw, d_lw, -DECAY, None, ALU.mult))
                link(v.tensor_tensor_scan(d_cum, const("reset128"), d_lw, 0.0, ALU.mult, ALU.add))
                c4 = d_cum.rearrange("p (b t) -> p b t", b=4)
                link(tt(d_cen.rearrange("p (b t) -> p b t", b=4), c4, c4[:, :, 63:64].broadcast_to([P, 4, P]),
                        ALU.subtract))
                e4 = d_cen.rearrange("p (b t) -> p b t", b=4)
                tt(d_es, d_cen, d_lw, ALU.subtract)
                b2 = "p (j c) t -> p j c t"
                tt(d_arg.unsqueeze(2), e4.rearrange(b2, j=2)[:, :, 0, 127:128], c4.rearrange(b2, j=2)[:, :, 1, 63:64],
                   ALU.add).then_inc(sem("decays_summed"), 1)
                mix_tokens("P2", l, 2)
                mix_tokens("P3", l, 4)
                r_, k_ = mixed[:, 0:2, :], mixed[:, 2:4, :]
                kk3 = d_kk.rearrange("p (j t) -> p j t", j=2)
                for j in range(2):
                    last = v.tensor_scalar(kk3[:, j, :], k_[:, j, :], param("k_k", j), None, ALU.mult)
                link(last)
                tt(d_kk2, d_kk, d_kk, ALU.mult).then_inc(sem("kk_squared"), 1)
                wait_evacuated(dve, "LA", l)
                for j in range(2):
                    last = v.tensor_scalar(d_tmp[:, j * SEQ:(j + 1) * SEQ], d_a[:, j * SEQ:(j + 1) * SEQ], -1.0,
                                           param("k_a", j), ALU.add, ALU.mult)
                link(last)
                kp3 = d_kp.rearrange("p (j t) -> p j t", j=2)
                link(stt(kp3, d_tmp.rearrange("p (j t) -> p j t", j=2), 1.0, k_, ALU.add, ALU.mult))
                for j in range(2):
                    last = stt(d_rk[:, j * SEQ:(j + 1) * SEQ], r_[:, j, :], param("r_k", j), kp3[:, j, :],
                               ALU.mult, ALU.mult)
                last.then_inc(sem("rk_ready"), 1)
                wait_full(dve, "KN", l)
                kn = v.tensor_scalar(d_rn, bank("KN", l)[:, :], 1e-12, None, ALU.add)
                frees(kn, "KN", l)
                wait_evacuated(dve, "KN", l)
                v.sem_inc(sem("kk_sums"), 1)
                dve.wait_ge(sem("log_terms"), l + 1)
                for i in range(3):
                    frees(stt(c_s[i], bank(f"Z{i}", l)[:, :], 0.0, c_e[i], ALU.max, ALU.add), f"Z{i}", l)
                dve.wait_ge(sem("kk_roots"), l + 1)
                link(v.reciprocal(d_rn, d_rn))
                link(tt(d_kk, d_kk, d_rn, ALU.mult))
                link(tt(d_kk2, d_kk, d_a, ALU.mult))
                dve.wait_ge(sem("decay_exps"), l + 1)
                tt(d_bt, d_kk2, d_em, ALU.mult)
                tt(d_kt, d_kp, d_em, ALU.mult).then_inc(sem("bk_ready"), 1)
                for hh in range(2):
                    r = slice(hh * 64, (hh + 1) * 64)

                    def four(ap):
                        return ap[r, :].rearrange("p (j c t) -> p j c t", j=2, c=NT)

                    tt(ar[r, :, hh, :, 0:P], four(d_kk), four(d_es), ALU.mult)
                    last = tt(ar[r, :, hh, :, P:256], r_[r, :, :].rearrange("p j (c t) -> p j c t", c=NT), four(d_ep),
                              ALU.mult)
                last.then_inc(sem("ar_ready"), 1)
                wait_full(dve, "GA", l)
                v_x = v.tensor_scalar(b_x, bank("GA", l)[:, 0:SEQ], param("b_a", 0), None, ALU.add)
                frees(v_x, "GA", l)
                wait_evacuated(dve, "GA", l)
                dve.wait_ge(sem("gate_log"), l + 1)
                link(stt(b_e, b_x, 0.0, b_e, ALU.min, ALU.subtract))
                link(v.tensor_tensor_scan(b_cum, const("reset64"), b_e, 0.0, ALU.mult, ALU.add))
                bc = b_cum.rearrange("p (n t) -> p n t", n=4)
                arg = b_arg.rearrange("p (i n t) -> p i n t", i=4, n=4)
                v.tensor_copy(arg[:, 2, :, :], bc)
                tt(arg[:, 1, :, :], bc[:, :, 31:32].broadcast_to([P, 4, 64]), bc, ALU.subtract)
                tt(arg[:, 3, :, :], bc[:, :, 63:64].broadcast_to([P, 4, 64]), bc, ALU.subtract)
                tt(arg[:, 0, :, :], bc, bc[:, :, 31:32].broadcast_to([P, 4, 64]),
                   ALU.subtract).then_inc(sem("gla_sums"), 1)
                wait_full(dve, "CO", l)
                frees(v.tensor_copy(normed[:, 0, :], bank("CO", l)[:, :]), "CO", l)
                wait_evacuated(dve, "CO", l)
                head_norm(normed[:, 0, :], row("sb"), tok[:, :, 2 * GW:3 * GW])
                wait_full(dve, "BON", l)
                frees(v.tensor_copy(bonus, bank("BON", l)[:, 0:8]), "BON", l)
                dve.wait_ge(sem("gla_exps"), l + 1)
                wait_evacuated(dve, "P7", l)
                ex = b_arg.rearrange("p (i t) -> p i t", i=4)
                q_, kb = b_raw[:, 0, :], b_raw[:, 1, :]
                v.tensor_copy(b_dec.unsqueeze(2), arg[:, 2, :, 63:64])
                stt(b_qd, q_, 32.0 ** -0.5, ex[:, 2, :], ALU.mult, ALU.mult)
                tt(b_kh, kb, ex[:, 1, :], ALU.mult)
                tt(b_kd, kb, ex[:, 3, :], ALU.mult)
                for h in range(4):
                    r = slice(32 * h, 32 * h + 32)
                    last = stt(b_q[r, h, :], q_[r, :], 32.0 ** -0.5, ex[r, 0, :], ALU.mult, ALU.mult)
                last.then_inc(sem("gla_ready"), 1)
                wait_full(dve, "GAT", l)
                for t in range(NT):
                    for half in range(2):
                        r = slice(half * 64, half * 64 + 64)
                        last = v.copy_predicated(
                            b_att[r, t, :, half * 64:half * 64 + 64],
                            over(const("gla_mask")[r, :], 4).bitcast(I32),
                            bank("GAT", l)[r, t * 256:(t + 1) * 256].rearrange("p (h t) -> p h t", h=4))
                frees(last, "GAT", l)
                gram_evacuation(l, 0)
                blocks = [slice(32 * h, 32 * h + 32) for h in range(4)]
                for n in range(3):
                    wait_full(dve, f"KV{n}", l)
                    last = v.memset(b_kv[:, n, :], 0.0)
                    link(last)
                    for h in range(4):
                        r, c = blocks[h], slice(h * HD, (h + 1) * HD)
                        if n == 0:
                            last = v.tensor_copy(b_kv[r, n, c], bank(f"KV{n}", l)[r, c])
                        else:
                            last = stt(b_kv[r, n, c], b_kv[r, n - 1, c], b_dec[r, n:n + 1], bank(f"KV{n}", l)[r, c],
                                       ALU.mult, ALU.add)
                    frees(last, f"KV{n}", l)
                    wait_evacuated(dve, f"KV{n}", l)
                v.sem_inc(sem("gla_state"), 1)
                wait_evacuated(dve, "P11", l)
                wait_evacuated(dve, "P12", l)
                if l == 0:
                    dve.wait_ge(sem("trig_ready"), 1)
                x1, x2 = a_raw[:, :, :, 0:32], a_raw[:, :, :, 32:64]
                cos = trig[:, 3, :].rearrange("p (t d) -> p t d", t=NT).unsqueeze(2).broadcast_to([P, NT, 6, 32])
                sin = trig[:, 1, :].rearrange("p (t d) -> p t d", t=NT).unsqueeze(2).broadcast_to([P, NT, 6, 32])
                tt(a_t1, x1, cos, ALU.mult)
                link(tt(a_t2, x2, sin, ALU.mult))
                link(tt(a_rot[:, :, :, 0:32], a_t1, a_t2, ALU.subtract))
                tt(a_t1, x2, cos, ALU.mult)
                link(tt(a_t2, x1, sin, ALU.mult))
                tt(a_rot[:, :, :, 32:64], a_t1, a_t2, ALU.add).then_inc(sem("rotated"), 1)
                wait_full(dve, "GO", l)
                frees(v.tensor_copy(normed[:, 0, :], bank("GO", l)[:, :]), "GO", l)
                wait_evacuated(dve, "GO", l)
                wait_evacuated(dve, "P9", l)
                head_norm(normed[:, 0, :], row("gla"), tok[:, :, GW:2 * GW], b_g).then_inc(sem("gla_done"), 1)
                dve.wait_ge(sem("gla_done"), l + 1)
                gram_evacuation(l, 1)
                for r in range(len(ROUNDS)):
                    if r == 0:
                        wait_full(dve, "KT", l)
                        for g in range(2):
                            s = slice(g * 64, (g + 1) * 64)
                            last = v.tensor_copy(a_k[s, g, :], bank("KT", l)[s, 0:SEQ])
                        frees(last, "KT", l)
                    if r == 1:
                        window_masks(l)
                    if r == 3:
                        window_output(l)
                    for c in range(NT):
                        for name in ROUNDS[r]:
                            if name[0] == "T":
                                dst = inv[c]["Tt" if name.endswith("t") else "T"]
                                wait_full(dve, f"{name}_{c}", l)
                                frees(tt(dst, dst, bank(f"{name}_{c}", l)[:, :], ALU.add if r < 4 else ALU.subtract),
                                      f"{name}_{c}", l)
                wait_full(dve, "SU", l)
                for j in range(2):
                    for hh in range(2):
                        s = slice(hh * 64, (hh + 1) * 64)
                        last = v.tensor_scalar(d_s[s, j, :], bank("SU", l)[s, j * P + hh * 64:j * P + hh * 64 + 64],
                                               d_eend[s, j:j + 1], None, ALU.mult)
                frees(last, "SU", l)
                wait_evacuated(dve, "SU", l)
                v.sem_inc(sem("state"), 1)
                rwkv_output(l)

            def gram_evacuation(l, c):
                if c == 0:
                    dve.wait_ge(sem("ar_ready"), l + 1)
                up = over(const("upper"), 2)
                for kind, dst in (("BG", lg), ("KG", mg)):
                    for j in range(2):
                        name = f"{kind}{c}{j}"
                        wait_full(dve, name, l)
                        frees(tt(dst[:, c, 2 * j:2 * j + 2, :], bank(name, l)[:, :].rearrange("p (h n) -> p h n", h=2),
                                 up, ALU.mult), name, l)
                    if kind == "BG":
                        wait_evacuated(dve, name, l)
                        v.sem_inc(sem(f"lt_ready{c}"), 1)
                wait_full(dve, f"LP{c}", l)
                frees(tt(inv[c]["L"].rearrange("p (h n) -> p h n", h=4),
                         bank(f"LP{c}", l)[:, :].rearrange("p (h n) -> p h n", h=4), over(const("lower"), 4),
                         ALU.mult), f"LP{c}", l)
                wait_evacuated(dve, f"LP{c}", l)
                v.sem_inc(sem(f"l_ready{c}"), 1)

            def window_masks(l):
                mask = const("a_mask")
                wait_full(dve, "S0", l)
                frees(tt(a_s0, bank("S0", l)[:, :].rearrange("p (s k) -> p s k", s=4), over(mask[:, P:256], 4),
                         ALU.add), "S0", l)
                for j in range(2):
                    wait_full(dve, f"S1{j}", l)
                    frees(tt(a_s1[:, 2 * j:2 * j + 2, :], bank(f"S1{j}", l)[:, :].rearrange("p (s k) -> p s k", s=2),
                             over(mask, 2), ALU.add), f"S1{j}", l)
                wait_evacuated(dve, "S0", l)
                wait_evacuated(dve, "S10", l)
                wait_evacuated(dve, "S11", l)
                v.tensor_reduce(a_max[:, 0:4], a_s0, AX_X, ALU.max)
                link(v.tensor_reduce(a_max[:, 4:8], a_s1, AX_X, ALU.max))
                sinks = row("sinks").rearrange("p (g j) -> p j g", g=2).unsqueeze(1).broadcast_to([P, NT, 2, 2])
                m4 = a_max.rearrange("p (t j g) -> p t j g", t=NT, j=2)
                link(tt(m4, m4, sinks, ALU.max))
                v.tensor_scalar(a_neg, a_max, -1.0, None, ALU.mult)
                tt(a_es.rearrange("p (t j g) -> p t j g", t=NT, j=2), sinks, m4,
                   ALU.subtract).then_inc(sem("a_masked"), 1)

            def window_output(l):
                dve.wait_ge(sem("probs"), l + 1)
                link(tt(a_den, a_den, a_es, ALU.add))
                link(v.reciprocal(a_den, a_den))
                wait_full(dve, "AO", l)
                for t in range(NT):
                    src = bank("AO", l)[:, t * GW:(t + 1) * GW].rearrange("p (j g d) -> p g j d", j=2, g=2)
                    den = a_den[:, 4 * t:4 * t + 4].rearrange("p (j g) -> p g j", j=2).unsqueeze(3).broadcast_to(
                        [P, 2, 2, HD])
                    last = tt(normed[:, 0, t * GW:(t + 1) * GW].rearrange("p (g j d) -> p g j d", g=2, j=2), src, den,
                              ALU.mult)
                frees(last, "AO", l)
                wait_evacuated(dve, "AO", l)
                link(head_norm(normed[:, 0, :], row("swa"), tok[:, :, 0:GW]))

            def rwkv_output(l):
                y = normed[:, 0, :]
                for c in range(NT):
                    wait_full(dve, f"Y{c}", l)
                    frees(v.tensor_copy(y[:, c * GW:(c + 1) * GW], bank(f"Y{c}", l)[:, 0:GW]), f"Y{c}", l)
                    wait_evacuated(dve, f"Y{c}", l)
                link(v.tensor_reduce(h_ss, heads(y), AX_X, ALU.add))
                link(v.tensor_scalar(h_ms, h_ss, 1.0 / HD, None, ALU.mult))
                link(tt(heads(y), heads(y), along(h_ms, HD), ALU.subtract))
                link(tt(normed[:, 1, :], y, y, ALU.mult))
                link(v.tensor_reduce(h_ss, heads(normed[:, 1, :]), AX_X, ALU.add))
                root(v.tensor_scalar(h_ms, h_ss, 1.0 / HD, GN_EPS, ALU.mult, ALU.add))
                link(tt(heads(y), heads(y), along(h_rstd, HD), ALU.mult))
                y2 = y.rearrange("p (t n) -> p t n", t=NT)
                link(tt(y2, y2, over(row("ln_w"), NT), ALU.mult))
                link(tt(y2, y2, over(row("ln_b"), NT), ALU.add))
                link(tt(heads(normed[:, 1, :]), heads(d_v), along(bonus, HD), ALU.mult))
                link(tt(y, y, normed[:, 1, :], ALU.add))
                tt(tok[:, :, 3 * GW:4 * GW], y2, d_g.rearrange("p (t n) -> p t n", t=NT),
                   ALU.mult).then_inc(sem("mix_ready"), 1)

            def add_banks(prefix, l):
                for i in range(4):
                    wait_full(dve, f"{prefix}{i}", l)
                    s = x_sb[:, i // 2, (i % 2) * 512:(i % 2 + 1) * 512]
                    frees(tt(s, s, bank(f"{prefix}{i}", l)[:, :], ALU.add), f"{prefix}{i}", l)
                for i in range(4):
                    wait_evacuated(dve, f"{prefix}{i}", l)
                v.sem_inc(sem("x_updated"), 1)

            def rope_angles():
                ang, sn, hf, cs, tmp, num = [trig[:, i, :] for i in range(6)]
                dve.wait_ge(sem("tables_landed"), 16)
                dve.wait_ge(sem("positions_landed"), 16)
                link(v.tensor_copy(r_s[:, 0:2], pos_i[:, :]))
                for t in range(NT):
                    last = v.tensor_scalar(ang[:, t * 32:(t + 1) * 32], const("inv_freq"), r_s[:, t:t + 1], None,
                                           ALU.mult)
                link(last)
                link(v.tensor_scalar(num, ang, 1.0 / TWO_PI, MAGIC, ALU.mult, ALU.add))
                link(v.tensor_scalar(num, num, -MAGIC, None, ALU.add))
                for part in (TWO_PI_1, TWO_PI_2, TWO_PI_3):
                    link(stt(ang, num, -part, ang, ALU.mult, ALU.add))
                v.tensor_scalar(sn, ang, 3.1415925, -3.1415925, ALU.min, ALU.max)
                v.tensor_scalar(hf, ang, 0.5, None, ALU.mult).then_inc(sem("angles"), 1)
                dve.wait_ge(sem("sines"), 1)
                link(tt(cs, hf, hf, ALU.mult))
                v.tensor_scalar(cs, cs, -2.0, 1.0, ALU.mult, ALU.add).then_inc(sem("trig_ready"), 1)

            def gates(l):
                wait_full(dve, "RT", l)
                lg3 = logits.rearrange("p (t e) -> p t e", t=NT)
                oh = r_oh.rearrange("p (t e) -> p t e", t=NT)
                tm = r_tmp.rearrange("p (t e) -> p t e", t=NT)
                cb = comb.rearrange("p (t e) -> p t e", t=NT)
                best, second, rank = r_s[:, 2:4], r_s[:, 4:6], r_s[:, 6:8]
                frees(v.tensor_copy(logits, bank("RT", l)[:, 0:16]), "RT", l)
                wait_evacuated(dve, "RT", l)

                def first_of(src, top, o):
                    link(v.tensor_reduce(top, src, AX_X, ALU.max))
                    link(tt(o, src, along(top, N_EXPERTS), ALU.is_equal))
                    link(tt(o, o, over(descend[:, :], NT), ALU.mult))
                    link(v.tensor_reduce(rank, o, AX_X, ALU.max))
                    link(tt(o, over(descend[:, :], NT), along(rank, N_EXPERTS), ALU.is_equal))

                first_of(lg3, best, oh)
                link(stt(tm, oh, -3.0e38, lg3, ALU.mult, ALU.add))
                first_of(tm, second, cb)
                link(tt(oh, oh, cb, ALU.add))
                link(tt(cb, lg3, along(best, N_EXPERTS), ALU.subtract))
                tt(r_s[:, 0:2], second, best, ALU.subtract).then_inc(sem("gates_shifted"), 1)
                dve.wait_ge(sem("gates_exp"), 1)
                link(v.tensor_scalar(r_s[:, 0:2], r_s[:, 0:2], 1.0, None, ALU.add))
                link(v.reciprocal(r_s[:, 0:2], r_s[:, 0:2]))
                link(tt(cb, cb, oh, ALU.mult))
                link(tt(cb, cb, along(r_s[:, 0:2], N_EXPERTS), ALU.mult))
                for q in range(MAX_PASSES + 1):
                    e8 = slice(q * N_EXPERTS, (q + 1) * N_EXPERTS)
                    v.tensor_copy(chosen[:, :, e8], oh)
                    last = v.tensor_copy(share[:, :, e8], cb)
                last.then_inc(sem("chosen_ready"), 1)
                wait_full(dve, "POS", l)
                at = bank("POS", l)[:, 0:16].rearrange("p (t e) -> p t e", t=NT)
                for q in range(MAX_PASSES + 1):
                    v.tensor_scalar(place[:, :, q * N_EXPERTS:(q + 1) * N_EXPERTS], at, -float(CAP * q), None, ALU.add)
                frees(v.tensor_copy(count, bank("POS", l)[:, 16:24]), "POS", l)
                wait_evacuated(dve, "POS", l)
                link(v.tensor_reduce(most[:, 0:1], count, AX_X, ALU.max))
                for q in range(1, MAX_PASSES):
                    last = v.tensor_scalar(most[:, q:q + 1], most[:, 0:1], float(CAP * q), None, ALU.is_gt)
                link(last)
                link(v.tensor_reduce(most[:, 4:5], most[:, 1:MAX_PASSES], AX_X, ALU.add))
                v.tensor_scalar(passes_i[:, :], most[:, 4:5], 1.0, None, ALU.add).then_inc(sem("passes_ready"), 1)
                dve.wait_ge(sem("passes_ready"), 1)

            dve.wait_ge(sem("cleared"), 1)
            rope_angles()
            dve.wait_ge(sem("x_landed"), 32)
            for l in range(DEPTH):
                dve.wait_ge(sem("params_landed"), 16 * N_PARAM_DMAS * (l + 1))
                norm_rows(norm_index(l, 0), l, tok)
                layer_mixers(l)
                feature_evacuation(("M0", "M1", "M2", "M3"), l, None)
                add_banks("O", l)
                norm_rows(norm_index(l, 1), l, tok)
                feature_evacuation(("F0", "F1", "F2", "F3"), l, "ffn_norm")
                wait_evacuated(dve, "F3", l)
                v.sem_inc(sem("params_used"), 1)
                if l % 2 == 0:
                    for j in range(D_FF // P):
                        dve.wait_ge(sem("silu"), j + 1)
                        frees(tt(act_t[:, j, :], silu_tmp[:, j % 2, :], bank(f"up{j}", l)[:, SEQ:2 * SEQ], ALU.mult),
                              f"up{j}", l)
                    add_banks("dn", l)
                else:
                    gates(l)
                    def slots_in(c, b):
                        return v.tensor_scalar(slot_h[:, c, :], banks[b][:, (c % 4) * CAP:(c % 4 + 1) * CAP],
                                               param("ffn_norm", c), None, ALU.mult)

                    def one_hot(dst, i, values):
                        for t in range(NT):
                            last = v.tensor_scalar(dst[:, t, :], const("iota"), place[:, t, bass.ds(i, 1)],
                                                   values[:, t, bass.ds(i, 1)], ALU.is_equal, ALU.mult)
                        return last

                    one_hot(pick, 0, chosen).then_inc(sem("picks"), 1)
                    wait_full(dve, "G1", l)
                    for c in range(4, 8):
                        last = slots_in(c, 7)
                    frees(last, "G1", l)
                    n_passes = dve.value_load(passes_i[0:1, 0:1], min_val=1, max_val=MAX_PASSES)
                    with dve.Fori(0, n_passes * N_EXPERTS) as i:
                        one_hot(weigh, i, share).then_inc(sem("weighs"), 1)
                        one_hot(pick, i + 1, chosen).then_inc(sem("picks"), 1)
                        for j in range(UPC):
                            dve.wait_ge(sem("moe_silu"), i * UPC + j + 1)
                            tt(slot_act[:, j, :], slot_silu[:, j % 2, :], banks[j % 2][:, CAP:2 * CAP],
                               ALU.mult).then_inc(free[j % 2], 1)
                        dve.wait_ge(full[7], nth(i, 7, 1))
                        for c in range(4, 8):
                            last = slots_in(c, 7)
                        last.then_inc(free[7], 1)
                        dve.wait_ge(full[3], nth(i, 3, 1))
                        v.tensor_copy(slot_y[:, 512:1024], banks[3][0:CAP, :]).then_inc(free[3], 1)
                        for b, t, half in SCATTER:
                            dve.wait_ge(full[b], nth(i, b, per[b]))
                            s = x_sb[:, t, half * 512:(half + 1) * 512]
                            tt(s, s, banks[b][:, :], ALU.add).then_inc(free[b], 1)
                        for b, t, half in SCATTER:
                            dve.wait_ge(free[b], nth(i, b, per[b]))
                    v.sem_inc(sem("x_updated"), 1)
            dve.wait_ge(sem("squares"), NT * (2 * DEPTH + 1))
            root(v.tensor_scalar(ms, ss, 1.0 / D, EPS, ALU.mult, ALU.add))
            dve.wait_ge(sem("final_landed"), 16)
            for t in range(NT):
                link(v.tensor_scalar(tok[:, t, :], x_sb[:, t, :], rstd[:, t:t + 1], None, ALU.mult))
                tt(tok[:, t, :], tok[:, t, :], final_row, ALU.mult).then_inc(sem("out_ready"), 1)


N_PARAM_DMAS = 6
SCATTER = ((4, 0, 0), (5, 0, 1), (2, 1, 0), (3, 1, 1))


def kernel(**inputs):
    import concourse.bacc as bacc
    from concourse.bass_utils import run_bass_kernel_spmd

    nc = bacc.Bacc("TRN2", target_bir_lowering=False, num_devices=1)
    a = {k: np.ascontiguousarray(v) for k, v in inputs.items()}

    def columns(v, n):
        return np.moveaxis(v.reshape(DEPTH, n, P), 1, 2)

    arrays = {
        "x": a["x"],
        "positions": np.ascontiguousarray(a["positions"].reshape(NT, P).T),
        "params": np.ascontiguousarray(np.concatenate([
            columns(a["attn_norm"], 8), columns(a["ffn_norm"], 8), columns(a["rwkv_mu"], 8), columns(a["rwkv_w0"], 2),
            columns(a["rwkv_a0"], 2), columns(a["rwkv_k_k"], 2), columns(a["rwkv_k_a"], 2),
            columns(a["rwkv_r_k"], 2), columns(a["gla_b_a"], 1)], axis=2)),
        "rows": np.ascontiguousarray(np.concatenate([
            a["swa_out_norm"].reshape(DEPTH, GW), a["gla_out_norm"].reshape(DEPTH, GW),
            a["sb_out_norm"].reshape(DEPTH, GW), a["rwkv_ln_w"].reshape(DEPTH, GW),
            a["rwkv_ln_b"].reshape(DEPTH, GW), a["swa_sinks"]], axis=1)),
        "final_norm": a["final_norm"].reshape(1, D),
        "consts": shape_constants(),
    }
    for name in ("w_in", "w_out", "gla_w_a2", "rwkv_w2", "rwkv_a2", "rwkv_g2", "ffn_w1", "ffn_w3", "ffn_w2",
                 "router", "moe_w1", "moe_w3", "moe_w2"):
        arrays[name] = a[name]
    t_in = {n: nc.dram_tensor(f"in_{n}", v.shape, mybir.dt.from_np(v.dtype), kind="ExternalInput").ap()
            for n, v in arrays.items()}
    out = nc.dram_tensor("out", (1, SEQ, D), F32, kind="ExternalOutput").ap()
    build(nc, t_in, out)
    r = run_bass_kernel_spmd(nc, [{f"in_{n}": v for n, v in arrays.items()}], core_ids=[0])
    return r.results[0]["out"]
```

```python
from contextlib import ExitStack

import numpy as np

import concourse.bass as bass
from concourse import mybir

F32 = mybir.dt.float32
I32 = mybir.dt.int32
ALU = mybir.AluOpType
ACT = mybir.ActivationFunctionType
AX_X = mybir.AxisListType.X

P = 128
D = 1024
KC = D // P
SEQ = 256
NT = SEQ // P
DEPTH = 2
GW = 256
HD = 64
A_Q, A_KV = 256, 128
B_QK, B_V, LR = 128, 256, 16
A_OFF = 0
B_OFF = A_Q + 2 * A_KV
C_OFF = B_OFF + 2 * B_QK + 2 * B_V + LR
D_OFF = C_OFF + 3 * GW
D_COLS = 3 * GW + 256
IN_COLS = D_OFF + D_COLS
D_FF = 2816
N_EXPERTS = 8
D_FFE = 1408
UPC = D_FFE // P
UP2 = (UPC + 1) // 2
EPS = 1e-6
GN_EPS = 64e-5
DECAY = 0.6065306597126334
ROPE_THETA = 10000.0
NEG = -1.0e30
MAGIC = 12582912.0
TWO_PI = 6.283185307179586
TWO_PI_1 = 6.28125
TWO_PI_2 = float(np.float32(np.round((TWO_PI - TWO_PI_1) * 2.0 ** 20) / 2.0 ** 20))
TWO_PI_3 = TWO_PI - TWO_PI_1 - TWO_PI_2

SLOT = KC * 272
SLOTS = 6

CAP = 96
MAX_PASSES = -(-SEQ // CAP)

CONST = {}
_at = 0
for _name, _n in (("ident", 128), ("rev_cum", 128), ("rev_all", 128), ("c_mask", 128), ("a_mask", 256),
                  ("upper", 256), ("lower", 128), ("blk16", 128), ("off32", 128), ("off64", 128),
                  ("off128", 128), ("gla_mask", 64), ("same_head", 128), ("head_sel", 2),
                  ("reset64", 256), ("reset128", 512), ("inv_freq", 32), ("all", 128),
                  ("iota", CAP)):
    CONST[_name] = (_at, _n)
    _at += _n
N_CONST = _at

PARAM = {}
_at = 0
for _name, _n in (("attn_norm", 8), ("ffn_norm", 8), ("mu", 8), ("w0", 2), ("a0", 2), ("k_k", 2), ("k_a", 2),
                  ("r_k", 2), ("b_a", 1)):
    PARAM[_name] = (_at, _n)
    _at += _n
N_PARAM = _at
ROWS = {}
_at = 0
for _name, _n in (("swa", 256), ("gla", 256), ("sb", 256), ("ln_w", 256), ("ln_b", 256), ("sinks", 4)):
    ROWS[_name] = (_at, _n)
    _at += _n
N_ROWS = _at


def shape_constants():
    t = np.zeros((P, N_CONST), np.float32)
    i = np.arange(P)[:, None]
    j = np.arange(P)[None, :]

    def put(name, value):
        at, n = CONST[name]
        t[:, at:at + n] = value

    put("ident", i == j)
    put("rev_cum", -1.0 * (i >= j))
    put("rev_all", -1.0)
    put("c_mask", np.where(i < j, 0.0, NEG))
    put("a_mask", np.concatenate([np.where(j > i, 0.0, NEG), np.where(j <= i, 0.0, NEG)], 1))
    put("upper", np.concatenate([i < j, i <= j], 1))
    put("lower", i > j)
    put("blk16", -1.0 * (i // 16 == j // 16))
    for b in (32, 64, 128):
        put(f"off{b}", (i // b == j // b) & (i // (b // 2) != j // (b // 2)))
    put("gla_mask", (i % 64) <= np.arange(64)[None, :])
    put("same_head", i // HD == j // HD)
    put("head_sel", i // HD == np.arange(2)[None, :])
    put("reset64", np.arange(256)[None, :] % 64 != 0)
    put("reset128", np.arange(512)[None, :] % 128 != 0)
    put("all", 1.0)
    put("iota", np.arange(CAP)[None, :])
    put("inv_freq", (np.float32(ROPE_THETA) ** (-np.arange(0, HD, 2, dtype=np.float32) / np.float32(HD)))[None, :])
    return t


def piece_plan():
    out = []
    for l in range(DEPTH):
        for at, n in ((D_OFF + 768, 256), (D_OFF, 256), (D_OFF + 256, 256), (D_OFF + 512, 256),
                      (C_OFF, 256), (C_OFF + 256, 256), (C_OFF + 512, 256),
                      (B_OFF, 256), (B_OFF + 256, 256), (B_OFF + 512, 272), (A_OFF, 256), (A_OFF + 256, 256)):
            out.append(("w_in", l, at, n))
        for k in W_OUT_ORDER:
            out.append(("w_out", l, 2 * k, 2))
        if l % 2 == 0:
            for i in range(D_FF // 256):
                out.append(("w1", l, 256 * i, 256))
                out.append(("w3", l, 256 * i, 256))
            for i in range(D_FF // 256):
                out.append(("w2", l, 2 * i, 2))
    return out


W_OUT_ORDER = (1, 2, 0, 3)
IN_PIECES = ("P0", "P1", "P2", "P3", "P4", "P5", "P6", "P7", "P8", "P10", "P11", "P12")


def psum_plan():
    count = [0] * 8
    uses = {}

    def use(name, l, bank):
        uses[name, l] = (bank, count[bank])
        count[bank] += 1

    for l in range(DEPTH):
        for name, bank in (("T0", 0), ("T1", 1), ("T2", 6), ("T3", 7), ("P0", 0), ("P1", 1), ("P2", 0),
                           ("LW", 2), ("LA", 3), ("P3", 1), ("G", 4), ("P4", 0), ("P5", 1), ("P6", 0),
                           ("Z0", 5), ("Z1", 6), ("Z2", 7), ("KN", 2), ("P7", 1), ("P8", 0), ("P9", 1), ("P10", 0),
                           ("GA", 3), ("VT", 4), ("ZC0", 5), ("ZC1", 6), ("ZC2", 7), ("BKT", 2), ("BON", 3),
                           ("P11", 1), ("BG00", 4), ("BG01", 2), ("KG00", 3), ("KG01", 4), ("LP0", 2), ("CO", 5),
                           ("BG10", 6), ("BG11", 7), ("KG10", 5), ("KG11", 6), ("LP1", 7), ("P12", 0)):
            use(name, l, bank)
        for r, names in enumerate(ROUNDS):
            for name, bank in FILLERS.get(r, ()):
                use(name, l, bank)
            for c in range(NT):
                for n in names:
                    use(f"{n}_{c}", l, 2 + 3 * c + ROUND_BANK[n])
                if c == 0 and r in MIDDLE:
                    use(MIDDLE[r][0], l, MIDDLE[r][1])
        for name, bank in (("M1", 0), ("U0", 6), ("M2", 1), ("SU", 7), ("Y0", 0), ("M0", 1),
                           ("O0", 2), ("O1", 3), ("O2", 4), ("O3", 5), ("RH1", 6), ("U1", 7), ("Y1", 0), ("M3", 1),
                           ("F0", 0), ("F1", 1), ("F2", 6), ("F3", 7)):
            use(name, l, bank)
        if l % 2 == 0:
            for j in range(D_FF // P):
                use(f"up{j}", l, j % 2)
            for i in range(4):
                use(f"dn{i}", l, 2 + i)
        else:
            for name, bank in (("RT", 6), ("POS", 7), ("G0", 6), ("G1", 7)):
                use(name, l, bank)
    return uses, count


FILLERS = {1: (("KDT", 1), ("GAT", 0)), 2: (("KV0", 1), ("KV1", 0)), 3: (("QT", 1), ("KT", 0)),
           4: (("S0", 1), ("S10", 0)), 5: (("GO", 0),), 6: (("RH0", 1),), 7: (("PT0", 0), ("PT1", 1)), 8: (("AO", 1),)}
MIDDLE = {2: ("KV2", 1), 4: ("S11", 1), 7: ("PT2", 0)}

ROUNDS = (("N2", "N2t"), ("N4", "N4t", "T2", "T2t"), ("N8", "T3", "T3t"), ("T4", "T4t"),
          ("Xa",), ("Ta", "Tat"), ("Xb",), ("Tb", "Tbt"), ("Xc",), ("Tct",))
ROUND_BANK = {"N2": 0, "N2t": 1, "N4": 2, "N4t": 0, "T2": 1, "T2t": 2, "N8": 0, "T3": 1, "T3t": 2,
              "T4": 0, "T4t": 1, "Xa": 2, "Ta": 0, "Tat": 1, "Xb": 2, "Tb": 0, "Tbt": 1, "Xc": 2, "Tct": 0}


def build(nc, t_in, out):
    ctx = ExitStack()
    with ctx:
        def sb(name, shape, dt=F32):
            return ctx.enter_context(nc.sbuf_tensor(name, shape, dt))

        x_sb = sb("x_sb", [P, NT, D])
        tok = sb("tok", [P, NT, D])
        hT = sb("hT", [P, KC, SEQ])
        hT_flat = hT[:, :, :].rearrange("p c t -> p (c t)")
        consts = sb("consts", [P, N_CONST])
        params = sb("params", [P, N_PARAM])
        rows = sb("rows", [P, N_ROWS])
        lora = sb("lora", [P, 256 + 256 + 128])
        router_sb = sb("router_sb", [P, KC, N_EXPERTS])
        ring = sb("ring", [P, SLOTS, SLOT])
        region_e = sb("region_e", [P, 8192])
        region_f = sb("region_f", [P, 4096])
        region_g = sb("region_g", [P, 3072])
        region_m = sb("region_m", [P, 5128])
        normed = sb("normed", [P, 2, 512])
        ar = sb("ar", [P, 2, 2, NT, 256])
        c_q = sb("c_q", [P, 2, 2, SEQ])
        b_q = sb("b_q", [P, 4, SEQ])
        b_att = sb("b_att", [P, NT, 4, P])
        a_k = sb("a_k", [P, 2, SEQ])
        small = sb("small", [P, 160])
        pos_i = sb("pos_i", [P, NT], I32)
        trig = sb("trig", [P, 6, 2 * 32])

        banks = [ctx.enter_context(nc.psum_tensor(f"bank{i}", [P, 512], F32)) for i in range(8)]

        def const(name):
            at, n = CONST[name]
            return consts[:, at:at + n]

        def param(name, c, p0=0, p1=P):
            at = PARAM[name][0] + c
            return params[p0:p1, at:at + 1]

        def row(name):
            at, n = ROWS[name]
            return rows[:, at:at + n]

        ident = const("ident")

        def over(ap, n):
            return ap.unsqueeze(1).broadcast_to([ap.shape[0], n, ap.shape[1]])

        def along(ap, n):
            return ap.unsqueeze(2).broadcast_to([ap.shape[0], ap.shape[1], n])

        def E(a, n):
            return region_e[:, a:a + n]

        mixed = E(0, 2048).rearrange("p (c t) -> p c t", c=8)
        temps = [E(2048 + 512 * i, 512) for i in range(12)]
        d_lw, d_cum, d_cen, d_ep, d_em, d_es, d_a, d_kk, d_kk2, d_rn, d_kp, d_tmp = temps
        lg = E(0, 2048).rearrange("p (c h n) -> p c h n", c=NT, h=4)
        mg = E(2048, 2048).rearrange("p (c h n) -> p c h n", c=NT, h=4)

        def inverse_buffers(base):
            v = [base[:, 512 * i:512 * i + 512] for i in range(8)]
            return {"N": v[0], "Nt": v[1], "N2": v[2], "N2t": v[3], "N4": v[0], "N4t": v[1], "N8": v[2],
                    "T": v[4], "Tt": v[5], "Et": v[6], "X": v[7], "L": v[7]}

        inv = [inverse_buffers(region_e[:, 4096:8192]), inverse_buffers(region_f[:, 0:4096])]
        G = [region_g[:, 512 * i:512 * i + 512] for i in range(6)]
        d_bt, d_kt, d_rk, d_v, d_g, d_bk = G
        raw = region_m[:, 0:2056].rearrange("p (c t) -> p c t", c=8)
        d_th = region_m[:, 2056:2312]
        d_gl = region_m[:, 2312:2568]
        b_raw = region_m[:, 2568:3080].rearrange("p (c t) -> p c t", c=2)
        b_v = region_m[:, 3080:3592].rearrange("p (t n) -> p t n", t=NT)
        b_g = region_m[:, 3592:4104].rearrange("p (t n) -> p t n", t=NT)
        b_lr = d_th
        a_raw = region_m[:, 4104:4872].rearrange("p (t s d) -> p t s d", t=NT, s=6)
        a_v = region_m[:, 4872:5128].rearrange("p (t n) -> p t n", t=NT)
        b_x = region_m[:, 0:256]
        b_e = region_m[:, 256:512]
        b_cum = region_m[:, 512:768]
        b_arg = region_m[:, 768:1792]
        b_kh = hT_flat[:, 0:256]
        b_qd = hT_flat[:, 256:512]
        b_kd = hT_flat[:, 512:768]
        b_kdt = hT_flat[:, 768:1024].rearrange("p (t n) -> p t n", t=NT)
        b_kv = hT_flat[:, 1024:1792].rearrange("p (n f) -> p n f", n=3)
        a_rot = region_m[:, 0:768].rearrange("p (t s d) -> p t s d", t=NT, s=6)
        a_t1 = region_m[:, 768:1152].rearrange("p (t s d) -> p t s d", t=NT, s=6)
        a_t2 = region_m[:, 1152:1536].rearrange("p (t s d) -> p t s d", t=NT, s=6)
        a_s0 = region_m[:, 2568:3080].rearrange("p (s k) -> p s k", s=4)
        a_s1 = region_m[:, 1536:2560].rearrange("p (s k) -> p s k", s=4)
        a_pt = hT_flat[:, 0:1536].rearrange("p (n q) -> p n q", q=P)
        a_qt = region_m[:, 768:1280].rearrange("p (j t) -> p j t", j=2)
        c_k = region_f[:, 0:512].rearrange("p (c t) -> p c t", c=2)
        c_v = region_f[:, 512:1024].rearrange("p (t n) -> p t n", t=NT)
        c_e = [region_f[:, 1024 + 512 * i:1536 + 512 * i] for i in range(3)]
        c_s = [region_f[:, 2560 + 512 * i:3072 + 512 * i] for i in range(3)]
        d_rh = inv[0]["N"].rearrange("p (c n) -> p c n", c=NT)
        d_u = inv[0]["Nt"].rearrange("p (c n) -> p c n", c=NT)
        d_s = inv[0]["N2"][:, 0:128].rearrange("p (j n) -> p j n", j=2)
        act_t = region_e[:, 0:22 * SEQ].rearrange("p (c t) -> p c t", c=22)
        silu_tmp = region_f[:, 0:512].rearrange("p (b t) -> p b t", b=2)
        final_row = region_f[:, 1024:2048]
        W = MAX_PASSES * N_EXPERTS + N_EXPERTS
        slot_act = region_e[:, 0:UPC * CAP].rearrange("p (c s) -> p c s", c=UPC)
        slot_silu = region_f[:, 0:2 * CAP].rearrange("p (b s) -> p b s", b=2)
        slot_h = region_m[:, 0:KC * CAP].rearrange("p (c s) -> p c s", c=KC)
        pick = region_m[:, 768:768 + NT * CAP].rearrange("p (t s) -> p t s", t=NT)
        weigh = region_m[:, 960:960 + NT * CAP].rearrange("p (t s) -> p t s", t=NT)
        weigh_t = region_m[0:CAP, 1152:1152 + SEQ].rearrange("p (t n) -> p t n", t=NT)
        slot_y = region_m[0:CAP, 1408:1408 + D]
        place = region_m[:, 2432:2432 + NT * W].rearrange("p (t i) -> p t i", t=NT)
        chosen = region_m[:, 2432 + NT * W:2432 + 2 * NT * W].rearrange("p (t i) -> p t i", t=NT)
        share = region_m[:, 2432 + 2 * NT * W:2432 + 3 * NT * W].rearrange("p (t i) -> p t i", t=NT)
        count = region_m[:, 3072:3072 + N_EXPERTS]
        most = region_m[:, 3080:3088]

        ss, ms, rstd = small[:, 90:94], small[:, 2:4], small[:, 4:6]
        h_ss, h_ms, h_rstd = small[:, 8:16], small[:, 16:24], small[:, 24:32]
        m_half = small[:, 32:40]
        a_max, a_neg, a_den, a_es = small[:, 40:48], small[:, 48:56], small[:, 56:64], small[:, 64:72]
        bonus = small[:, 72:80]
        d_end, d_arg, d_eend = small[:, 80:82], small[:, 82:84], small[:, 84:86]
        b_dec = small[:, 86:90]
        logits, comb = small[:, 96:112], small[:, 112:128]
        r_tmp, r_oh = small[:, 128:144], small[:, 144:160]
        r_s = sb("r_s", [P, 8])
        passes_i = sb("passes_i", [P, 1], I32)
        descend = sb("descend", [P, N_EXPERTS])

        def heads(ap):
            return ap.rearrange("p (g d) -> p g d", d=HD)

        uses, before_loop = psum_plan()
        full = [ctx.enter_context(nc.semaphore(f"bank{i}_full")) for i in range(8)]
        free = [ctx.enter_context(nc.semaphore(f"bank{i}_free")) for i in range(8)]
        landed = [ctx.enter_context(nc.semaphore(f"slot{i}_landed")) for i in range(SLOTS)]
        sems = {}

        def sem(name):
            if name not in sems:
                sems[name] = ctx.enter_context(nc.semaphore(name))
            return sems[name]

        def bank(name, l):
            return banks[uses[name, l][0]]

        def wait_full(eng, name, l):
            b, n = uses[name, l]
            eng.wait_ge(full[b], n + 1)

        def wait_evacuated(eng, name, l):
            b, n = uses[name, l]
            eng.wait_ge(free[b], n + 1)

        def wait_open(pe, name, l):
            b, n = uses[name, l]
            if n:
                pe.wait_ge(free[b], n)

        def fills(ins, name, l):
            ins.then_inc(full[uses[name, l][0]], 1)

        def frees(ins, name, l):
            ins.then_inc(free[uses[name, l][0]], 1)

        pieces = piece_plan()
        order = {p: n for n, p in enumerate(pieces)}
        FIRST_MOE = len(pieces)

        def slot(n):
            return n % SLOTS

        MORE = 3
        SLOTS_E = SLOTS + MORE
        more_slots = region_e[:, 8192 - MORE * SLOT:8192].rearrange("p (s n) -> p s n", s=MORE)
        more_landed = [ctx.enter_context(nc.semaphore(f"more_slot{i}_landed")) for i in range(MORE)]

        def expert_slot(k, n):
            r = k % SLOTS_E
            return ring[:, slot(FIRST_MOE + r), 0:n] if r < SLOTS else more_slots[:, r - SLOTS, 0:n]

        def expert_landed(i, k):
            r = k % SLOTS_E
            before = (FIRST_MOE + r) // SLOTS if r < SLOTS else 0
            s = landed[slot(FIRST_MOE + r)] if r < SLOTS else more_landed[r - SLOTS]
            return s, i * (16 * (E_PIECES // SLOTS_E)) + 16 * (before + k // SLOTS_E + 1)

        def wait_piece(pe, n):
            pe.wait_ge(landed[slot(n)], 16 * (n // SLOTS + 1))

        E_PIECES = 3 * UP2
        assert E_PIECES % SLOTS_E == 0
        per = [(UPC + 1) // 2, UPC // 2, 3, 2, 1, 1, 1, 1]

        def nth(i, b, k):
            return i * per[b] + before_loop[b] + k

        block = ctx.enter_context(nc.Block())

        def norm_index(l, which):
            return 2 * l + which

        @block.sync
        def _(sp):
            for t in range(NT):
                sp.dma_start(x_sb[:, t, :], t_in["x"][0, t * P:(t + 1) * P, :]).then_inc(sem(f"x_landed{t}"), 16)
            sp.dma_start(ident, t_in["consts"][:, 0:P]).then_inc(sem("ident_landed"), 16)

            def wait_released(n):
                what, l, at, _ = pieces[n]
                if what == "w_in":
                    k = n - order["w_in", l, D_OFF + 768, 256]
                    wait_full(sp, IN_PIECES[k], l)
                elif what == "w_out":
                    if at < KC - 2:
                        sp.wait_ge(sem("w_out_used"), (KC // 2 - 1) * l + W_OUT_ORDER.index(at // 2) + 1)
                    else:
                        wait_full(sp, "O3", l)
                elif what in ("w1", "w3"):
                    wait_full(sp, f"up{2 * (at // 256) + 1}", l)
                elif at < 2 * (D_FF // 256 - 1):
                    sp.wait_ge(sem("w2_used"), at // 2 + 1)
                else:
                    wait_full(sp, "dn3", l)

            def source(what, l, at, n):
                if what == "w_in":
                    return t_in["w_in"][l].rearrange("(c p) n -> p c n", p=P)[:, :, at:at + n]
                if what == "w_out":
                    return t_in["w_out"][l].rearrange("(c p) n -> p c n", p=P)[:, at:at + n, :]
                if what == "w2":
                    return t_in["ffn_w2"][l // 2].rearrange("(c p) n -> p c n", p=P)[:, at:at + n, :]
                return t_in["ffn_" + what][l // 2].rearrange("(c p) n -> p c n", p=P)[:, :, at:at + n]

            for n, (what, l, at, m) in enumerate(pieces):
                if n >= SLOTS:
                    wait_released(n - SLOTS)
                if n == 1:
                    sp.dma_start(consts[:, P:], t_in["consts"][:, P:]).then_inc(sem("tables_landed"), 16)
                elif n == 2:
                    sp.wait_ge(landed[slot(0)], 16)
                size = (KC if what in ("w_in", "w1", "w3") else D) * m
                dst = ring[:, slot(n), 0:size].rearrange("p (c n) -> p c n", n=m if size == KC * m and what not in ("w_out", "w2") else D)
                sp.dma_start(dst, source(what, l, at, m)).then_inc(landed[slot(n)], 16)

            def expert_piece(e, k):
                if k < 2 * UP2:
                    i = k // 2
                    m = min(256, D_FFE - 256 * i)
                    w = t_in["moe_w1" if k % 2 == 0 else "moe_w3"]
                    src = w[0, e].rearrange("(c p) n -> p c n", p=P)[:, :, 256 * i:256 * i + m]
                    dst = expert_slot(k, KC * m).rearrange("p (c n) -> p c n", n=m)
                else:
                    i = k - 2 * UP2
                    m = min(2, UPC - 2 * i)
                    src = t_in["moe_w2"][0, e].rearrange("(c p) n -> p c n", p=P)[:, 2 * i:2 * i + m, :]
                    dst = expert_slot(k, m * D).rearrange("p (c n) -> p c n", n=D)
                sp.dma_start(dst, src).then_inc(expert_landed(e, k)[0], 16)

            def expert_released(i, k):
                if k < 2 * UP2:
                    j = min(2 * (k // 2) + 1, UPC - 1)
                    sp.wait_ge(full[j % 2], nth(i, j % 2, j // 2 + 1))
                elif k < E_PIECES - 1:
                    sp.wait_ge(sem("moe_w2_used"), i * (UP2 - 1) + k - 2 * UP2 + 1)
                else:
                    sp.wait_ge(full[3], nth(i, 3, 1))
                sp.sem_inc(sem("slot_turns"), 1)

            for k in range(SLOTS_E):
                if k < SLOTS:
                    wait_released(FIRST_MOE + k - SLOTS)
                elif k == SLOTS:
                    sp.wait_ge(sem("x_updated"), 2 * NT * (2 * (DEPTH - 1) + 1))
                expert_piece(0, k)
            sp.wait_ge(sem("passes_ready"), 1)
            n = sp.value_load(passes_i[0:1, 0:1], min_val=1, max_val=MAX_PASSES)
            with sp.Fori(0, n * N_EXPERTS - 1) as i:
                for k in range(SLOTS_E, E_PIECES):
                    expert_released(i, k - SLOTS_E)
                    expert_piece(i % N_EXPERTS, k)
                for k in range(SLOTS_E):
                    expert_released(i, k + E_PIECES - SLOTS_E)
                    expert_piece((i + 1) % N_EXPERTS, k)
            last_i = n * N_EXPERTS - 1
            for k in range(SLOTS_E, E_PIECES):
                expert_released(last_i, k - SLOTS_E)
                expert_piece(N_EXPERTS - 1, k)
            for t in range(NT):
                for i in range(2):
                    sp.wait_ge(sem("out_ready"), 2 * t + i + 1)
                    s = slice(i * 512, (i + 1) * 512)
                    sp.dma_start(out[0, t * P:(t + 1) * P, s], tok[:, t, s]).then_inc(sem("stored"), 16)
            sp.wait_ge(sem("stored"), 16 * 2 * NT)

        @block.tensor
        def _(pe):
            def mm(o, lhsT, rhs, start=False, stop=False):
                return nc.tensor.matmul(o, lhsT, rhs, start=start, stop=stop, skip_group_check=True)

            def chunk_to_features(name, l, c2, t):
                for cc in range(2):
                    last = nc.tensor.transpose(bank(name, l)[:, cc * 256 + t * P:cc * 256 + t * P + P],
                                               tok[:, t, (2 * c2 + cc) * P:(2 * c2 + cc + 1) * P], ident)
                return last

            def rows_to_features(names, l, which):
                for t in range(NT):
                    for c2 in range(4):
                        if c2 % 2 == 0:
                            pe.wait_ge(sem("h_ready"), 2 * (NT * norm_index(l, which) + t) + c2 // 2 + 1)
                        if t == 0:
                            wait_open(pe, names[c2], l)
                        last = chunk_to_features(names[c2], l, c2, t)
                        if t == NT - 1:
                            fills(last, names[c2], l)

            def wait_features(names, l, k):
                if names and k % 2 == 0:
                    wait_evacuated(pe, names[k // 2], l)

            def mix_to_features(c2, l):
                wait_open(pe, f"M{c2}", l)
                for t in range(NT):
                    last = chunk_to_features(f"M{c2}", l, c2, t)
                fills(last, f"M{c2}", l)

            def project_features(name, l, n, cols, features=None):
                wait_piece(pe, n)
                wait_open(pe, name, l)
                w = ring[:, slot(n), 0:KC * pieces[n][3]].rearrange("p (c n) -> p c n", c=KC)
                for j, (c0, m) in enumerate(cols):
                    for k in range(KC):
                        if j == 0:
                            wait_features(features, l, k)
                        last = mm(bank(name, l)[0:m, j * SEQ:(j + 1) * SEQ], w[:, k, c0:c0 + m], hT[:, k, :],
                                  start=(j == 0 and k == 0), stop=(k == KC - 1))
                fills(last, name, l)

            def project_tokens(name, l, n, m):
                wait_piece(pe, n)
                wait_open(pe, name, l)
                w = ring[:, slot(n), 0:KC * pieces[n][3]].rearrange("p (c n) -> p c n", c=KC)
                for t in range(NT):
                    for k in range(KC):
                        last = mm(bank(name, l)[:, t * m:(t + 1) * m], hT[:, k, t * P:(t + 1) * P], w[:, k, 0:m],
                                  start=(t == 0 and k == 0), stop=(k == KC - 1))
                fills(last, name, l)

            def layer_mixers(l):
                both = ((0, 128), (128, 128))
                n0 = order["w_in", l, D_OFF + 768, 256]
                rows_to_features(("T0", "T1", "T2", "T3"), l, 0)
                project_features("P0", l, n0, both, ("T0", "T1", "T2", "T3"))
                project_features("P1", l, n0 + 1, both)
                project_features("P2", l, n0 + 2, both)
                pe.wait_ge(sem("tables_landed"), 16)
                pe.wait_ge(sem("params_landed"), 16 * N_PARAM_DMAS * (l + 1))
                pe.wait_ge(sem("lora_in"), l + 1)
                wait_open(pe, "LW", l)
                for j in range(2):
                    last = mm(bank("LW", l)[:, j * SEQ:(j + 1) * SEQ], lora[0:64, j * P:(j + 1) * P], d_th[0:64, :],
                              start=(j == 0), stop=True)
                fills(last, "LW", l)
                wait_open(pe, "LA", l)
                pe.wait_ge(sem("al_mixed"), l + 1)
                for j in range(2):
                    last = mm(bank("LA", l)[:, j * SEQ:(j + 1) * SEQ], lora[64:128, j * P:(j + 1) * P],
                              mixed[64:128, 6, :], start=(j == 0), stop=True)
                fills(last, "LA", l)
                project_features("P3", l, n0 + 3, both)
                wait_open(pe, "G", l)
                pe.wait_ge(sem("gl_sig"), l + 1)
                for t in range(NT):
                    last = mm(bank("G", l)[:, t * GW:(t + 1) * GW], d_gl[:, t * P:(t + 1) * P], lora[:, 256:512],
                              start=(t == 0), stop=True)
                fills(last, "G", l)
                project_features("P4", l, n0 + 4, both)
                project_features("P5", l, n0 + 5, both)
                project_tokens("P6", l, n0 + 6, GW)
                wait_evacuated(pe, "P4", l)
                wait_evacuated(pe, "P5", l)
                for j in range(2):
                    name = f"Z{j}"
                    wait_open(pe, name, l)
                    z = bank(name, l)
                    mm(z[:, :], c_k[:, j, 0:P], c_q[:, j, :, :].rearrange("p h t -> p (h t)"), start=True)
                    fills(mm(z[:, :].rearrange("p (h t) -> p h t", h=2)[:, :, 0:P], ident, over(const("c_mask"), 2),
                             stop=True), name, l)
                wait_open(pe, "Z2", l)
                z = bank("Z2", l)
                for j in range(2):
                    mm(z[:, j * 256:(j + 1) * 256].rearrange("p (h t) -> p h t", h=2), c_k[:, j, P:SEQ],
                       c_q[:, j, :, P:SEQ], start=(j == 0))
                fills(mm(z[:, :].rearrange("p (h t) -> p h t", h=4), ident, over(const("c_mask"), 4), stop=True), "Z2", l)
                wait_open(pe, "KN", l)
                pe.wait_ge(sem("kk_squared"), l + 1)
                fills(mm(bank("KN", l)[:, :], const("same_head"), d_kk2, start=True, stop=True), "KN", l)
                project_features("P7", l, n0 + 7, both)
                project_tokens("P8", l, n0 + 8, GW)
                project_tokens("P9", l, n0 + 9, GW)
                project_features("P10", l, n0 + 9, ((256, LR),))
                wait_evacuated(pe, "P10", l)
                wait_open(pe, "GA", l)
                fills(mm(bank("GA", l)[:, 0:SEQ], lora[0:LR, 512:640], b_lr[0:LR, :], start=True, stop=True), "GA", l)
                wait_open(pe, "VT", l)
                pe.wait_ge(sem("v_mixed"), l + 1)
                for t in range(NT):
                    for j in range(2):
                        last = nc.tensor.transpose(bank("VT", l)[:, t * GW + j * P:t * GW + (j + 1) * P],
                                                   mixed[:, 4 + j, t * P:(t + 1) * P], ident)
                fills(last, "VT", l)
                for i in range(3):
                    wait_evacuated(pe, f"Z{i}", l)
                for j in range(2):
                    wait_open(pe, f"ZC{j}", l)
                    z = bank(f"ZC{j}", l)
                    mm(z[:, :], const("rev_cum"), c_s[j])
                    fills(mm(z[:, :].rearrange("p (h t) -> p h t", h=2)[:, :, P:SEQ], const("rev_all"),
                             c_s[2][:, j * 256:(j + 1) * 256].rearrange("p (h t) -> p h t", h=2), stop=True),
                          f"ZC{j}", l)
                wait_open(pe, "ZC2", l)
                fills(mm(bank("ZC2", l)[:, :], const("rev_cum"), c_s[2], stop=True), "ZC2", l)
                pe.wait_ge(sem("bk_ready"), l + 1)
                wait_open(pe, "BKT", l)
                for i, src in enumerate((d_bt, d_kt)):
                    for j in range(2):
                        last = nc.tensor.transpose(bank("BKT", l)[:, i * 256 + j * P:i * 256 + (j + 1) * P],
                                                   src[:, j * SEQ:j * SEQ + P], ident)
                fills(last, "BKT", l)
                pe.wait_ge(sem("rk_ready"), l + 1)
                wait_open(pe, "BON", l)
                for t in range(NT):
                    for j in range(2):
                        last = mm(bank("BON", l)[:, t * 4 + 2 * j:t * 4 + 2 * j + 2],
                                  d_rk[:, j * SEQ + t * P:j * SEQ + (t + 1) * P], const("head_sel"),
                                  start=(t == 0 and j == 0), stop=True)
                fills(last, "BON", l)
                project_tokens("P11", l, n0 + 10, GW)
                grams(l, 0)
                for i in range(3):
                    wait_evacuated(pe, f"ZC{i}", l)
                wait_evacuated(pe, "P6", l)
                wait_open(pe, "CO", l)
                for h in range(4):
                    j, hh = h // 2, h % 2
                    a0 = c_e[j].rearrange("p (h t) -> p h t", h=2)
                    a1 = c_e[2].rearrange("p (h t) -> p h t", h=4)
                    v = slice(h * HD, (h + 1) * HD)
                    o = bank("CO", l)
                    mm(o[:, h * HD:(h + 1) * HD], a0[:, hh, 0:P], c_v[:, 0, v], start=(h == 0), stop=True)
                    mm(o[:, GW + h * HD:GW + (h + 1) * HD], a0[:, hh, P:SEQ], c_v[:, 0, v])
                    last = mm(o[:, GW + h * HD:GW + (h + 1) * HD], a1[:, h, :], c_v[:, 1, v], stop=True)
                fills(last, "CO", l)
                grams(l, 1)
                project_tokens("P12", l, n0 + 11, GW)
                steps = {1: b_scores, 2: b_states, 3: a_transpose, 4: a_scores, 5: b_output, 6: first_rows, 7: a_probs,
                         8: a_output}
                middle = {2: b_state, 4: a_score, 7: a_prob}
                for r in range(len(ROUNDS)):
                    if r in steps:
                        steps[r](l)
                    for c in range(NT):
                        inverse_round(l, r, c)
                        if c == 0 and r in MIDDLE:
                            middle[r](l, 2)
                recurrence(l)

            def b_scores(l):
                pe.wait_ge(sem("gla_ready"), l + 1)
                wait_open(pe, "KDT", l)
                for t in range(NT):
                    last = nc.tensor.transpose(bank("KDT", l)[:, t * P:(t + 1) * P], b_kd[:, t * P:(t + 1) * P], ident)
                fills(last, "KDT", l)
                wait_open(pe, "GAT", l)
                for n in range(4):
                    p0 = (n % 2) * 64
                    o = bank("GAT", l)[p0:p0 + 64, (n // 2) * 256:(n // 2) * 256 + 256]
                    last = mm(o.rearrange("p (h t) -> p h t", h=4), b_kh[:, n * 64:(n + 1) * 64],
                              b_q[:, :, n * 64:(n + 1) * 64], start=(n < 2), stop=True)
                fills(last, "GAT", l)

            def b_states(l):
                wait_evacuated(pe, "KDT", l)
                wait_evacuated(pe, "P8", l)
                for n in range(2):
                    b_state(l, n)

            def b_state(l, n):
                p0 = (n % 2) * 64
                wait_open(pe, f"KV{n}", l)
                fills(mm(bank(f"KV{n}", l)[:, 0:256], b_kdt[p0:p0 + 64, n // 2, :], b_v[p0:p0 + 64, n // 2, :],
                         start=True, stop=True), f"KV{n}", l)

            def b_output(l):
                wait_evacuated(pe, "GAT", l)
                wait_open(pe, "GO", l)
                o = bank("GO", l)
                for t in range(NT):
                    for h in range(4):
                        mm(o[:, t * GW + h * HD:t * GW + (h + 1) * HD], b_att[:, t, h, :],
                           b_v[:, t, h * HD:(h + 1) * HD], start=(t == 0 and h == 0), stop=True)
                pe.wait_ge(sem("gla_state"), l + 1)
                for n in range(1, 4):
                    p0 = (n % 2) * 64
                    last = mm(o[p0:p0 + 64, (n // 2) * GW:(n // 2 + 1) * GW], b_qd[:, n * 64:(n + 1) * 64],
                              b_kv[:, n - 1, :], stop=True)
                fills(last, "GO", l)

            def grams(l, c):
                if c == 0:
                    pe.wait_ge(sem("ar_ready"), l + 1)
                for kind, src in (("BG", d_bt), ("KG", d_kt)):
                    for j in range(2):
                        name = f"{kind}{c}{j}"
                        wait_open(pe, name, l)
                        fills(mm(bank(name, l)[:, :].rearrange("p (h n) -> p h n", h=2),
                                 src[:, j * SEQ + c * P:j * SEQ + (c + 1) * P], ar[:, j, :, c, :],
                                 start=True, stop=True), name, l)
                wait_open(pe, f"LP{c}", l)
                for h in range(4):
                    last = mm(bank(f"LP{c}", l)[:, h * P:(h + 1) * P], ar[:, h // 2, h % 2, c, 0:P],
                              d_bt[:, (h // 2) * SEQ + c * P:(h // 2) * SEQ + (c + 1) * P], start=(h == 0), stop=True)
                fills(last, f"LP{c}", l)

            PRODUCTS = {"N2": ("Nt", "N"), "N2t": ("N", "Nt"), "N4": ("N2t", "N2"), "N4t": ("N2", "N2t"),
                        "T2": ("Tt", "N2"), "T2t": ("N2", "Tt"), "N8": ("N4t", "N4"), "T3": ("Tt", "N4"),
                        "T3t": ("N4", "Tt"), "T4": ("Tt", "N8"), "T4t": ("N8", "Tt"),
                        "X": ("Et", "T"), "T": ("Tt", "X"), "Tt": ("X", "Tt")}

            def inverse_round(l, r, c):
                buf = inv[c]
                if r == 0:
                    pe.wait_ge(sem(f"n_ready{c}"), l + 1)
                else:
                    for name in ROUNDS[r - 1]:
                        wait_evacuated(pe, f"{name}_{c}", l)
                if r == 1:
                    pe.wait_ge(sem(f"t_ready{c}"), l + 1)
                if r in (4, 6, 8):
                    pe.wait_ge(sem(f"e_ready{c}"), 3 * l + (r - 4) // 2 + 1)
                for name in ROUNDS[r]:
                    key = name if r < 4 else {"X": "X", "T": "T"}[name[0]] + ("t" if name.endswith("t") else "")
                    a, b = PRODUCTS[key]
                    wait_open(pe, f"{name}_{c}", l)
                    for h in range(4):
                        s = slice(h * P, (h + 1) * P)
                        last = mm(bank(f"{name}_{c}", l)[:, s], buf[a][:, s], buf[b][:, s], start=(h == 0), stop=True)
                    fills(last, f"{name}_{c}", l)

            def a_transpose(l):
                pe.wait_ge(sem("rotated"), l + 1)
                for name, slots, o in (("QT", (0, 1), 0), ("KT", (2,), 0)):
                    wait_open(pe, name, l)
                    for i, s in enumerate(slots):
                        for t in range(NT):
                            last = nc.tensor.transpose(
                                bank(name, l)[:, i * SEQ + t * P:i * SEQ + (t + 1) * P],
                                a_rot[:, t, 2 * s:2 * s + 2, :].rearrange("p s d -> p (s d)"), ident)
                    fills(last, name, l)

            def a_scores(l):
                wait_evacuated(pe, "QT", l)
                wait_evacuated(pe, "KT", l)
                wait_open(pe, "S0", l)
                for j in range(2):
                    last = mm(bank("S0", l)[:, j * 256:(j + 1) * 256].rearrange("p (g k) -> p g k", g=2),
                              a_qt[:, j, 0:P], a_k[:, :, 0:P], start=(j == 0), stop=True)
                fills(last, "S0", l)
                a_score(l, 1)

            def a_score(l, i):
                j = i - 1
                wait_open(pe, f"S1{j}", l)
                fills(mm(bank(f"S1{j}", l)[:, :], a_qt[:, j, P:SEQ], a_k[:, :, :].rearrange("p g k -> p (g k)"),
                         start=True, stop=True), f"S1{j}", l)

            def a_probs(l):
                pe.wait_ge(sem("probs"), l + 1)
                for i in range(2):
                    a_prob(l, i)

            def a_prob(l, i):
                wait_open(pe, f"PT{i}", l)
                for s in range(4):
                    src = a_s0[:, s, :] if i == 0 else a_s1[:, s, (i - 1) * P:i * P]
                    last = nc.tensor.transpose(bank(f"PT{i}", l)[:, s * P:(s + 1) * P], src, ident)
                fills(last, f"PT{i}", l)

            def a_output(l):
                for i in range(3):
                    wait_evacuated(pe, f"PT{i}", l)
                wait_open(pe, "AO", l)
                o = bank("AO", l)
                for s in range(4):
                    g = s % 2
                    v = slice(g * HD, (g + 1) * HD)
                    c = slice(s * HD, (s + 1) * HD)
                    mm(o[:, c], a_pt[:, s, :], a_v[:, 0, v], start=(s == 0), stop=True)
                    c = slice(GW + s * HD, GW + (s + 1) * HD)
                    mm(o[:, c], a_pt[:, 4 + s, :], a_v[:, 0, v])
                    last = mm(o[:, c], a_pt[:, 8 + s, :], a_v[:, 1, v], stop=True)
                fills(last, "AO", l)

            def right_hand_side(l, c):
                name = f"RH{c}"
                wait_open(pe, name, l)
                for h in range(4):
                    o = bank(name, l)[:, h * HD:(h + 1) * HD]
                    last = mm(o, mg[:, c, h, 0:P], d_v[:, c * GW + h * HD:c * GW + (h + 1) * HD],
                              start=(h == 0), stop=(c == 0))
                    if c == 1:
                        last = mm(o, ar[:, h // 2, h % 2, 1, 0:P], d_s[:, h // 2, :], stop=True)
                fills(last, name, l)

            def first_rows(l):
                right_hand_side(l, 0)

            def solve(l, c):
                wait_evacuated(pe, f"RH{c}", l)
                wait_evacuated(pe, f"Tct_{c}", l)
                wait_open(pe, f"U{c}", l)
                for h in range(4):
                    last = mm(bank(f"U{c}", l)[:, h * HD:(h + 1) * HD], inv[c]["Tt"][:, h * P:(h + 1) * P],
                              d_rh[:, c, h * HD:(h + 1) * HD], start=(h == 0), stop=True)
                fills(last, f"U{c}", l)

            def tile_output(l, c):
                wait_open(pe, f"Y{c}", l)
                for h in range(4):
                    o = bank(f"Y{c}", l)[:, h * HD:(h + 1) * HD]
                    s = slice(h * HD, (h + 1) * HD)
                    mm(o, lg[:, c, h, P:256], d_u[:, c, s], start=(h == 0))
                    last = mm(o, mg[:, c, h, P:256], d_v[:, c * GW + h * HD:c * GW + (h + 1) * HD], stop=(c == 0))
                    if c == 1:
                        last = mm(o, ar[:, h // 2, h % 2, 1, P:256], d_s[:, h // 2, :], stop=True)
                fills(last, f"Y{c}", l)

            def w_out_products(l, k2, parts):
                if parts[0] == 0:
                    wait_evacuated(pe, f"M{k2}", l)
                    wait_piece(pe, order["w_out", l, 2 * k2, 2])
                w = ring[:, slot(order["w_out", l, 2 * k2, 2]), 0:2 * D].rearrange("p (c n) -> p c n", c=2)
                for i in parts:
                    t, half = i // 2, i % 2
                    if k2 == W_OUT_ORDER[0]:
                        wait_open(pe, f"O{i}", l)
                    for kk in range(2):
                        k = 2 * k2 + kk
                        last = mm(bank(f"O{i}", l)[:, :], hT[:, k, t * P:(t + 1) * P],
                                  w[:, kk, half * 512:(half + 1) * 512], start=(k2 == W_OUT_ORDER[0] and kk == 0),
                                  stop=(k == KC - 1))
                    if k2 == W_OUT_ORDER[-1]:
                        fills(last, f"O{i}", l)
                if parts[-1] == 3 and k2 != W_OUT_ORDER[-1]:
                    last.then_inc(sem("w_out_used"), 1)

            def recurrence(l):
                pe.wait_ge(sem("gla_done"), l + 1)
                mix_to_features(1, l)
                solve(l, 0)
                pe.wait_ge(sem("stick_done"), l + 1)
                mix_to_features(2, l)
                wait_evacuated(pe, "U0", l)
                wait_open(pe, "SU", l)
                for j in range(2):
                    o = bank("SU", l)[:, j * P:(j + 1) * P]
                    mm(o, d_bk[:, j * P:(j + 1) * P], d_u[:, 0, j * P:(j + 1) * P], start=(j == 0))
                    last = mm(o, d_bk[:, 256 + j * P:256 + (j + 1) * P], d_v[:, j * P:(j + 1) * P], stop=True)
                fills(last, "SU", l)
                tile_output(l, 0)
                w_out_products(l, 1, (0, 1, 2, 3))
                pe.wait_ge(sem("window_done"), l + 1)
                mix_to_features(0, l)
                pe.wait_ge(sem("state"), l + 1)
                right_hand_side(l, 1)
                w_out_products(l, 2, (0,))
                solve(l, 1)
                w_out_products(l, 2, (1,))
                wait_evacuated(pe, "U1", l)
                tile_output(l, 1)
                w_out_products(l, 2, (2, 3))
                w_out_products(l, 0, (0, 1, 2, 3))
                pe.wait_ge(sem("mix_ready"), l + 1)
                mix_to_features(3, l)
                w_out_products(l, 3, (0, 1, 2, 3))

            def up_chunk(o, w1, w3, l, features):
                for i, w in enumerate((w1, w3)):
                    for k in range(KC):
                        if i == 0:
                            wait_features(features, l, k)
                        last = mm(o[:, i * SEQ:(i + 1) * SEQ], w[:, k, :], hT[:, k, :], start=(i == 0 and k == 0),
                                  stop=(k == KC - 1))
                return last

            def dense(l):
                for i in range(D_FF // 256):
                    n1, n3 = order["w1", l, 256 * i, 256], order["w3", l, 256 * i, 256]
                    wait_piece(pe, n1)
                    wait_piece(pe, n3)
                    w1 = ring[:, slot(n1), 0:KC * 256].rearrange("p (c n) -> p c n", c=KC)
                    w3 = ring[:, slot(n3), 0:KC * 256].rearrange("p (c n) -> p c n", c=KC)
                    for jj in range(2):
                        name = f"up{2 * i + jj}"
                        wait_open(pe, name, l)
                        fills(up_chunk(bank(name, l), w1[:, :, jj * P:(jj + 1) * P], w3[:, :, jj * P:(jj + 1) * P], l,
                                       ("F0", "F1", "F2", "F3") if i == jj == 0 else None), name, l)
                for i in range(4):
                    wait_open(pe, f"dn{i}", l)
                steps = D_FF // 256
                for k2 in range(steps):
                    n = order["w2", l, 2 * k2, 2]
                    wait_piece(pe, n)
                    wait_evacuated(pe, f"up{2 * k2}", l)
                    wait_evacuated(pe, f"up{2 * k2 + 1}", l)
                    w = ring[:, slot(n), 0:2 * D].rearrange("p (c n) -> p c n", c=2)
                    for i in range(4):
                        t, half = i // 2, i % 2
                        for kk in range(2):
                            k = 2 * k2 + kk
                            last = mm(bank(f"dn{i}", l)[:, :], act_t[:, k, t * P:(t + 1) * P],
                                      w[:, kk, half * 512:(half + 1) * 512], start=(k == 0), stop=(k == 2 * steps - 1))
                        if k2 == steps - 1:
                            fills(last, f"dn{i}", l)
                    if k2 < steps - 1:
                        last.then_inc(sem("w2_used"), 1)

            def experts(l):
                wait_open(pe, "RT", l)
                for t in range(NT):
                    for k in range(KC):
                        if t == 0:
                            wait_features(("F0", "F1", "F2", "F3"), l, k)
                        last = mm(bank("RT", l)[:, t * N_EXPERTS:(t + 1) * N_EXPERTS], hT[:, k, t * P:(t + 1) * P],
                                  router_sb[:, k, :], start=(t == 0 and k == 0), stop=(k == KC - 1))
                fills(last, "RT", l)

                pe.wait_ge(sem("chosen_ready"), 1)
                wait_open(pe, "POS", l)
                o = bank("POS", l)
                before, sel = const("upper")[:, 0:P], (chosen[:, 0, 0:N_EXPERTS], chosen[:, 1, 0:N_EXPERTS])
                mm(o[:, 0:8], before, sel[0], start=True, stop=True)
                mm(o[:, 8:16], const("all"), sel[0])
                mm(o[:, 8:16], before, sel[1], stop=True)
                mm(o[:, 16:24], const("all"), sel[0])
                fills(mm(o[:, 16:24], const("all"), sel[1], stop=True), "POS", l)

                def gather(b, waits):
                    for h in range(2):
                        if waits is not None:
                            pe.wait_ge(free[6 + h], waits[h])
                        for c in range(4):
                            for t in range(NT):
                                last = mm(banks[6 + h][:, c * CAP:(c + 1) * CAP],
                                          tok[:, t, (4 * h + c) * P:(4 * h + c + 1) * P], pick[:, t, :],
                                          start=(c == 0 and t == 0), stop=(t == NT - 1))
                        last.then_inc(full[6 + h], 1)

                pe.wait_ge(sem("picks"), 1)
                wait_open(pe, "G0", l)
                wait_open(pe, "G1", l)
                gather(0, None)

                def landed_piece(i, k):
                    s, n = expert_landed(i, k)
                    pe.wait_ge(s, n)

                pe.wait_ge(sem("passes_ready"), 1)
                n_passes = pe.value_load(passes_i[0:1, 0:1], min_val=1, max_val=MAX_PASSES)
                with pe.Fori(0, n_passes * N_EXPERTS) as i:
                    pe.wait_ge(free[6], nth(i, 6, 0))
                    pe.wait_ge(free[7], nth(i, 7, 0))
                    for p2 in range(UP2):
                        m = min(256, D_FFE - 256 * p2)
                        landed_piece(i, 2 * p2)
                        landed_piece(i, 2 * p2 + 1)
                        w1 = expert_slot(2 * p2, KC * m).rearrange("p (c n) -> p c n", c=KC)
                        w3 = expert_slot(2 * p2 + 1, KC * m).rearrange("p (c n) -> p c n", c=KC)
                        for jj in range(m // P):
                            j = 2 * p2 + jj
                            b = j % 2
                            pe.wait_ge(free[b], nth(i, b, j // 2))
                            for f, w in enumerate((w1, w3)):
                                for k in range(KC):
                                    last = mm(banks[b][:, f * CAP:(f + 1) * CAP], w[:, k, jj * P:(jj + 1) * P],
                                              slot_h[:, k, :], start=(f == 0 and k == 0), stop=(k == KC - 1))
                            last.then_inc(full[b], 1)
                    pe.wait_ge(sem("weighs"), i + 1)
                    pe.wait_ge(free[2], nth(i, 2, 0))
                    for t in range(NT):
                        last = nc.tensor.transpose(banks[2][0:CAP, t * P:(t + 1) * P], weigh[:, t, :], ident)
                    last.then_inc(full[2], 1)
                    pe.wait_ge(sem("picks"), i + 2)
                    gather(i, (nth(i, 6, 0), nth(i, 7, 0)))
                    pe.wait_ge(free[2], nth(i, 2, 1))
                    pe.wait_ge(free[3], nth(i, 3, 0))
                    for k2 in range(UP2):
                        m = min(2, UPC - 2 * k2)
                        landed_piece(i, 2 * UP2 + k2)
                        w = expert_slot(2 * UP2 + k2, m * D).rearrange("p (c n) -> p c n", c=m)
                        for kk in range(m):
                            j = 2 * k2 + kk
                            pe.wait_ge(free[j % 2], nth(i, j % 2, j // 2 + 1))
                        for half in range(2):
                            for kk in range(m):
                                k = 2 * k2 + kk
                                last = mm(banks[2 + half][0:CAP, :], slot_act[:, k, :],
                                          w[:, kk, half * 512:(half + 1) * 512], start=(k == 0), stop=(k == UPC - 1))
                            if k2 == UP2 - 1:
                                last.then_inc(full[2 + half], 1)
                        if k2 < UP2 - 1:
                            last.then_inc(sem("moe_w2_used"), 1)
                    for q, (b, t, half) in enumerate(SCATTER):
                        pe.wait_ge(free[2 + half], nth(i, 2 + half, 2 - half))
                        if b > 3:
                            pe.wait_ge(free[b], nth(i, b, 0))
                        mm(banks[b][:, :], weigh_t[:, t, :], slot_y[:, half * 512:(half + 1) * 512],
                           start=True, stop=True).then_inc(full[b], 1)

            pe.wait_ge(sem("zeros"), 1)
            for _ in range(WARM_UP):
                mm(banks[5][:, 0:256], hT[:, 0, 0:P], hT[:, 0, :], start=True, stop=True)
            pe.wait_ge(sem("ident_landed"), 16)
            for l in range(DEPTH):
                layer_mixers(l)
                rows_to_features(("F0", "F1", "F2", "F3"), l, 1)
                if l % 2 == 0:
                    dense(l)
                else:
                    pe.wait_ge(sem("router_landed"), 16)
                    experts(l)

        @block.scalar
        def _(act):
            chain = [0]

            def link(ins):
                chain[0] += 1
                ins.then_inc(sem("act_chain"), 1)
                act.wait_ge(sem("act_chain"), chain[0])

            def load_gains(l):
                act.dma_start(params[:, :], t_in["params"][l]).then_inc(sem("gains_landed"), 16)

            def load_params(l):
                w2, a2 = t_in["rwkv_w2"][l], t_in["rwkv_a2"][l]
                act.dma_start(rows[:, :], t_in["rows"][l:l + 1, :].broadcast_to([P, N_ROWS])).then_inc(
                    sem("params_landed"), 16)
                act.dma_start(lora[0:64, 0:256], w2).then_inc(sem("params_landed"), 16)
                act.dma_start(lora[64:128, 0:256], a2).then_inc(sem("params_landed"), 16)
                act.dma_start(lora[:, 256:512], t_in["rwkv_g2"][l]).then_inc(sem("params_landed"), 16)
                act.dma_start(lora[0:LR, 512:640], t_in["gla_w_a2"][l]).then_inc(sem("params_landed"), 16)

            def square_sums(k):
                for t in range(NT):
                    if k == 0:
                        act.wait_ge(sem(f"x_landed{t}"), 16)
                    for i in range(2):
                        if k:
                            act.wait_ge(sem("x_updated"), 2 * (NT * (k - 1) + t) + i + 1)
                        s = slice(i * 512, (i + 1) * 512)
                        nc.scalar.activation(tok[:, t, s], x_sb[:, t, s], ACT.Square,
                                             accum_out=ss[:, 2 * t + i:2 * t + i + 1]).then_inc(sem("squares"), 1)

            def feature_evacuation(names, l, gain):
                for c2 in (0, 2):
                    wait_full(act, names[c2], l)
                    for cc in range(2):
                        src = bank(names[c2], l)[:, cc * 256:(cc + 1) * 256]
                        dst = hT[:, 2 * c2 + cc, :]
                        if gain is None:
                            last = nc.scalar.copy(dst, src)
                        else:
                            last = nc.scalar.activation(dst, src, ACT.Copy, scale=param(gain, 2 * c2 + cc))
                    frees(last, names[c2], l)

            def evacuate(name, l, dst, src):
                wait_full(act, name, l)
                frees(nc.scalar.copy(dst, src), name, l)

            def both(ap):
                return ap.rearrange("p (c t) -> p c t", c=2)

            def layer_mixers(l):
                feature_evacuation(("T0", "T1", "T2", "T3"), l, "attn_norm")
                if l == 0:
                    act.wait_ge(sem("angles"), 1)
                    nc.scalar.activation(trig[:, 1, :], trig[:, 1, :], ACT.Sin)
                    nc.scalar.activation(trig[:, 2, :], trig[:, 2, :], ACT.Sin).then_inc(sem("sines"), 1)
                evacuate("P0", l, raw[:, 6:8, 1:257], both(bank("P0", l)[:, :]))
                evacuate("P1", l, raw[:, 0:2, 1:257], both(bank("P1", l)[:, :]))
                act.wait_ge(sem("al_mixed"), l + 1)
                nc.scalar.activation(d_th[0:64, :], mixed[0:64, 6, :], ACT.Tanh).then_inc(sem("lora_in"), 1)
                act.wait_ge(sem("gl_mixed"), l + 1)
                nc.scalar.activation(d_gl, mixed[:, 7, :], ACT.Sigmoid).then_inc(sem("gl_sig"), 1)
                evacuate("P2", l, raw[:, 2:4, 1:257], both(bank("P2", l)[:, :]))
                for name, off, dst in (("LW", "w0", d_lw), ("LA", "a0", d_a)):
                    wait_full(act, name, l)
                    for j in range(2):
                        last = nc.scalar.activation(dst[:, j * SEQ:(j + 1) * SEQ],
                                                    bank(name, l)[:, j * SEQ:(j + 1) * SEQ], ACT.Sigmoid,
                                                    bias=param(off, j))
                    frees(last, name, l)
                evacuate("P3", l, raw[:, 4:6, 1:257], both(bank("P3", l)[:, :]))
                evacuate("G", l, d_g, bank("G", l)[:, :])
                wait_full(act, "P4", l)
                for hh in range(2):
                    r = slice(hh * 64, (hh + 1) * 64)
                    last = nc.scalar.mul(c_q[r, :, hh, :], both(bank("P4", l)[r, :]), HD ** -0.5)
                frees(last, "P4", l)
                evacuate("P5", l, c_k, both(bank("P5", l)[:, :]))
                evacuate("P6", l, c_v, both(bank("P6", l)[:, :]))
                act.wait_ge(sem("decays_summed"), l + 1)
                nc.scalar.activation(d_ep, d_cen, ACT.Exp)
                nc.scalar.activation(d_em, d_cen, ACT.Exp, scale=-1.0)
                nc.scalar.activation(d_es, d_es, ACT.Exp)
                nc.scalar.activation(d_eend, d_arg, ACT.Exp).then_inc(sem("decay_exps"), 1)
                for i in range(3):
                    wait_full(act, f"Z{i}", l)
                    last = nc.scalar.activation(c_e[i], bank(f"Z{i}", l)[:, :], ACT.Abs)
                link(last)
                for i in range(3):
                    last = nc.scalar.activation(c_e[i], c_e[i], ACT.Exp, scale=-1.0)
                link(last)
                for i in range(3):
                    last = nc.scalar.activation(c_e[i], c_e[i], ACT.Ln, bias=1.0)
                last.then_inc(sem("log_terms"), 1)
                act.wait_ge(sem("kk_sums"), l + 1)
                nc.scalar.activation(d_rn, d_rn, ACT.Sqrt).then_inc(sem("kk_roots"), 1)
                evacuate("P7", l, b_raw, both(bank("P7", l)[:, :]))
                evacuate("P8", l, b_v, both(bank("P8", l)[:, :]))
                wait_full(act, "P9", l)
                frees(nc.scalar.activation(b_g, both(bank("P9", l)[:, :]), ACT.Silu), "P9", l)
                evacuate("P10", l, b_lr[0:LR, :], bank("P10", l)[0:LR, 0:SEQ])
                evacuate("VT", l, d_v, bank("VT", l)[:, :])
                wait_evacuated(act, "GA", l)
                link(nc.scalar.activation(b_e, b_x, ACT.Abs))
                link(nc.scalar.activation(b_e, b_e, ACT.Exp, scale=-1.0))
                nc.scalar.activation(b_e, b_e, ACT.Ln, bias=1.0).then_inc(sem("gate_log"), 1)
                for i in range(3):
                    wait_full(act, f"ZC{i}", l)
                    frees(nc.scalar.activation(c_e[i], bank(f"ZC{i}", l)[:, :], ACT.Exp), f"ZC{i}", l)
                act.wait_ge(sem("gla_sums"), l + 1)
                nc.scalar.activation(b_arg, b_arg, ACT.Exp, scale=1.0 / 16.0).then_inc(sem("gla_exps"), 1)
                evacuate("BKT", l, d_bk, bank("BKT", l)[:, :])
                evacuate("BON", l, bonus, bank("BON", l)[:, 0:8])
                wait_full(act, "P11", l)
                for t in range(NT):
                    src = bank("P11", l)[:, t * GW:(t + 1) * GW].rearrange("p (g j d) -> p g j d", g=2, j=2)
                    dst = a_raw[:, t, 0:4, :].rearrange("p (j g) d -> p g j d", g=2)
                    last = nc.scalar.mul(dst, src, HD ** -0.5)
                frees(last, "P11", l)
                evacuate("CO", l, normed[:, 0, :], bank("CO", l)[:, :])
                wait_full(act, "P12", l)
                src = bank("P12", l)[:, :].rearrange("p (t s n) -> p t s n", t=NT, s=2)
                nc.scalar.copy(a_v, src[:, :, 1, :])
                frees(nc.scalar.copy(a_raw[:, :, 4:6, :], src[:, :, 0, :].rearrange("p t (s d) -> p t s d", s=2)),
                      "P12", l)
                def probs_out(i):
                    evacuate(f"PT{i}", l, a_pt[:, 4 * i:4 * i + 4, :],
                             bank(f"PT{i}", l)[:, :].rearrange("p (n q) -> p n q", n=4))

                def right_hand_side(c):
                    wait_full(act, f"RH{c}", l)
                    frees(nc.scalar.mul(d_rh[:, c, :], bank(f"RH{c}", l)[:, 0:GW], -1.0), f"RH{c}", l)

                for r in range(len(ROUNDS)):
                    if r == 1:
                        evacuate("KDT", l, b_kdt, both(bank("KDT", l)[:, 0:256]))
                    elif r == 6:
                        right_hand_side(0)
                    elif r == 7:
                        for i in range(3):
                            probs_out(i)
                    for c in range(NT):
                        for name in ROUNDS[r]:
                            if name[0] in "NX":
                                evacuate(f"{name}_{c}", l, inv[c]["X" if name[0] == "X" else name],
                                         bank(f"{name}_{c}", l)[:, :])
                    if r == 3:
                        evacuate("QT", l, a_qt, both(bank("QT", l)[:, :]))
                        wait_full(act, "KT", l)
                        for g in range(2):
                            s = slice(g * 64, (g + 1) * 64)
                            last = nc.scalar.copy(a_k[s, g, :], bank("KT", l)[s, 0:SEQ])
                        frees(last, "KT", l)
                    elif r == 5:
                        act.wait_ge(sem("stick_done"), l + 1)
                        evacuate("GO", l, normed[:, 0, :], bank("GO", l)[:, :])
                        act.wait_ge(sem("a_masked"), l + 1)
                        for s in range(4):
                            nc.scalar.activation(a_s0[:, s, :], a_s0[:, s, :], ACT.Exp, bias=a_neg[:, s:s + 1],
                                                 accum_out=a_den[:, s:s + 1])
                        for s in range(4):
                            nc.scalar.activation(a_s1[:, s, :], a_s1[:, s, :], ACT.Exp, bias=a_neg[:, 4 + s:5 + s],
                                                 accum_out=a_den[:, 4 + s:5 + s])
                        nc.scalar.activation(a_es, a_es, ACT.Exp).then_inc(sem("probs"), 1)
                evacuate("M1", l, hT[:, 2:4, :], both(bank("M1", l)[:, :]))
                evacuate("U0", l, d_u[:, 0, :], bank("U0", l)[:, 0:GW])
                evacuate("M2", l, hT[:, 4:6, :], both(bank("M2", l)[:, :]))
                evacuate("M0", l, hT[:, 0:2, :], both(bank("M0", l)[:, :]))
                right_hand_side(1)
                evacuate("U1", l, d_u[:, 1, :], bank("U1", l)[:, 0:GW])
                evacuate("M3", l, hT[:, 6:8, :], both(bank("M3", l)[:, :]))

            act.dma_start(pos_i[:, :], t_in["positions"]).then_inc(sem("positions_landed"), 16)
            load_gains(0)
            for l in range(DEPTH):
                square_sums(norm_index(l, 0))
                if l == 0:
                    load_params(0)
                    act.dma_start(router_sb[:, :, :], t_in["router"][0].rearrange("(c p) e -> p c e", p=P)).then_inc(
                        sem("router_landed"), 16)
                act.wait_ge(sem("gains_landed"), 16 * (l + 1))
                layer_mixers(l)
                square_sums(norm_index(l, 1))
                feature_evacuation(("F0", "F1", "F2", "F3"), l, "ffn_norm")
                if l + 1 < DEPTH:
                    act.wait_ge(sem("params_used"), l + 1)
                    wait_evacuated(act, "F2", l)
                    load_gains(l + 1)
                    load_params(l + 1)
                if l % 2 == 0:
                    for j in range(D_FF // P):
                        wait_full(act, f"up{j}", l)
                        nc.scalar.activation(silu_tmp[:, j % 2, :], bank(f"up{j}", l)[:, 0:SEQ],
                                             ACT.Silu).then_inc(sem("silu"), 1)
                else:
                    act.wait_ge(sem("gates_shifted"), 1)
                    nc.scalar.activation(comb, comb, ACT.Exp)
                    nc.scalar.activation(r_s[:, 0:2], r_s[:, 0:2], ACT.Exp).then_inc(sem("gates_exp"), 1)
                    def slots_in(c, b):
                        return nc.scalar.activation(slot_h[:, c, :], banks[b][:, (c % 4) * CAP:(c % 4 + 1) * CAP],
                                                    ACT.Copy, scale=param("ffn_norm", c))

                    wait_full(act, "G0", l)
                    for c in range(4):
                        last = slots_in(c, 6)
                    frees(last, "G0", l)
                    act.wait_ge(sem("passes_ready"), 1)
                    act.dma_start(final_row, t_in["final_norm"].broadcast_to([P, D])).then_inc(
                        sem("final_landed"), 16)
                    n_passes = act.value_load(passes_i[0:1, 0:1], min_val=1, max_val=MAX_PASSES)
                    with act.Fori(0, n_passes * N_EXPERTS) as i:
                        for j in range(UPC):
                            b = j % 2
                            act.wait_ge(full[b], nth(i, b, j // 2 + 1))
                            nc.scalar.activation(slot_silu[:, b, :], banks[b][:, 0:CAP],
                                                 ACT.Silu).then_inc(sem("moe_silu"), 1)
                        act.wait_ge(full[2], nth(i, 2, 1))
                        nc.scalar.copy(weigh_t, banks[2][0:CAP, 0:SEQ].rearrange("p (t n) -> p t n", t=NT)).then_inc(
                            free[2], 1)
                        act.wait_ge(full[6], nth(i, 6, 1))
                        for c in range(4):
                            last = slots_in(c, 6)
                        last.then_inc(free[6], 1)
                        act.wait_ge(full[2], nth(i, 2, 2))
                        nc.scalar.copy(slot_y[:, 0:512], banks[2][0:CAP, :]).then_inc(free[2], 1)
            square_sums(2 * DEPTH)

        @block.gpsimd
        def _(pool):
            g = nc.gpsimd

            taken = [0]

            def power(ap_in, ap_out):
                taken[0] += 1
                pool.wait_ge(sem("means_ready"), taken[0])
                n = ap_in.shape[1]
                g.tensor_tensor(ap_out, ap_in, m_half[:, 0:n], ALU.pow).then_inc(sem("rstd_ready"), 1)

            def row_powers():
                for t in range(NT):
                    power(ms[:, t:t + 1], rstd[:, t:t + 1])

            g.memset(hT[:, 0, :], 0.0).then_inc(sem("zeros"), 1)
            g.memset(m_half, -0.5).then_inc(sem("halves"), 1)
            pool.wait_ge(sem("halves"), 1)
            row_powers()
            g.memset(c_q[:, :, :, :], 0.0)
            g.memset(ar[:, :, :, :, :], 0.0)
            g.memset(b_q[:, :, :], 0.0)
            g.memset(b_att[:, :, :, :], 0.0)
            g.memset(a_k[:, :, :], 0.0)
            for i in range(N_EXPERTS):
                last = g.memset(descend[:, i:i + 1], float(N_EXPERTS - i))
            last.then_inc(sem("cleared"), 1)
            pool.wait_ge(sem("cleared"), 1)
            pool.wait_ge(sem("tables_landed"), 16)
            for l in range(DEPTH):
                if l:
                    row_powers()
                for c in range(NT):
                    buf = inv[c]
                    v = {n: buf[n].rearrange("p (h n) -> p h n", h=4) for n in buf}
                    lt = lg[:, c, :, 0:P]
                    pool.wait_ge(sem(f"lt_ready{c}"), l + 1)
                    g.tensor_tensor(v["Nt"], lt, over(const("blk16"), 4), ALU.mult)
                    pool.wait_ge(sem(f"l_ready{c}"), l + 1)
                    g.tensor_tensor(v["N"], v["L"], over(const("blk16"), 4), ALU.mult).then_inc(sem(f"n_ready{c}"), 1)
                    pool.wait_ge(sem(f"n_ready{c}"), l + 1)
                    g.tensor_tensor(v["T"], v["N"], over(ident, 4), ALU.add)
                    g.tensor_tensor(v["Tt"], v["Nt"], over(ident, 4), ALU.add).then_inc(sem(f"t_ready{c}"), 1)
                pool.wait_ge(sem("gla_ready"), l + 1)
                g.memset(b_kv[:, :, :], 0.0).then_inc(sem("kv_cleared"), 1)
                for c in range(NT):
                    v = inv[c]["Et"].rearrange("p (h n) -> p h n", h=4)
                    g.tensor_tensor(v, lg[:, c, :, 0:P], over(const("off32"), 4), ALU.mult).then_inc(
                        sem(f"e_ready{c}"), 1)
                power(h_ms, h_rstd)
                for name, before in (("off64", "Xa"), ("off128", "Xb")):
                    for c in range(NT):
                        v = inv[c]["Et"].rearrange("p (h n) -> p h n", h=4)
                        wait_full(pool, f"{before}_{c}", l)
                        g.tensor_tensor(v, lg[:, c, :, 0:P], over(const(name), 4),
                                        ALU.mult).then_inc(sem(f"e_ready{c}"), 1)
                power(h_ms, h_rstd)
                power(h_ms, h_rstd)
                power(h_ms, h_rstd)
                row_powers()
            row_powers()

        @block.vector
        def _(dve):
            v = nc.vector
            chain = [0]
            means = [0]

            def link(ins):
                chain[0] += 1
                ins.then_inc(sem("dve_chain"), 1)
                dve.wait_ge(sem("dve_chain"), chain[0])

            def tt(o, a, b, op):
                return v.tensor_tensor(o, a, b, op)

            def stt(o, a, s, b, op0, op1):
                return v.scalar_tensor_tensor(out=o, in0=a, scalar=s, in1=b, op0=op0, op1=op1)

            def root(ins):
                means[0] += 1
                ins.then_inc(sem("means_ready"), 1)
                dve.wait_ge(sem("rstd_ready"), means[0])

            def row_scale(k, t):
                dve.wait_ge(sem("squares"), 2 * (NT * k + t) + 1)
                link(v.tensor_scalar(ms[:, t:t + 1], ss[:, 2 * t:2 * t + 1], 1.0 / D, EPS, ALU.mult, ALU.add))
                dve.wait_ge(sem("squares"), 2 * (NT * k + t) + 2)
                root(v.tensor_scalar(ms[:, t:t + 1], ss[:, 2 * t + 1:2 * t + 2], 1.0 / D, ms[:, t:t + 1], ALU.mult,
                                     ALU.add))
                return rstd[:, t:t + 1]

            def norm_rows(k):
                for t in range(NT):
                    scale = row_scale(k, t)
                    for i in range(2):
                        s = slice(i * 512, (i + 1) * 512)
                        v.tensor_scalar(tok[:, t, s], x_sb[:, t, s], scale, None, ALU.mult).then_inc(
                            sem("h_ready"), 1)

            def feature_evacuation(names, l, gain):
                for c2 in (1, 3):
                    wait_full(dve, names[c2], l)
                    for cc in range(2):
                        src = bank(names[c2], l)[:, cc * 256:(cc + 1) * 256]
                        dst = hT[:, 2 * c2 + cc, :]
                        if gain is None:
                            last = v.tensor_copy(dst, src)
                        else:
                            last = v.tensor_scalar(dst, src, param(gain, 2 * c2 + cc), None, ALU.mult)
                    frees(last, names[c2], l)

            def mix_tokens(name, l, c0):
                wait_evacuated(dve, name, l)
                link(tt(mixed[:, c0:c0 + 2, :], raw[:, c0:c0 + 2, 0:256], raw[:, c0:c0 + 2, 1:257], ALU.subtract))
                for c in (c0, c0 + 1):
                    last = stt(mixed[:, c, :], mixed[:, c, :], param("mu", c), raw[:, c, 1:257], ALU.mult, ALU.add)
                    if c == 6:
                        last.then_inc(sem("al_mixed"), 1)
                    elif c == 7:
                        last.then_inc(sem("gl_mixed"), 1)
                    elif c == 5:
                        last.then_inc(sem("v_mixed"), 1)
                    else:
                        link(last)

            def head_norm(src, gain, dst, times=None):
                link(tt(normed[:, 1, :], src, src, ALU.mult))
                link(v.tensor_reduce(h_ss, heads(normed[:, 1, :]), AX_X, ALU.add))
                root(v.tensor_scalar(h_ms, h_ss, 1.0 / HD, EPS, ALU.mult, ALU.add))
                link(tt(heads(normed[:, 1, :]), heads(src), along(h_rstd, HD), ALU.mult))
                n = normed[:, 1, :].rearrange("p (t n) -> p t n", t=NT)
                if times is None:
                    return tt(dst, n, over(gain, NT), ALU.mult)
                link(tt(n, n, over(gain, NT), ALU.mult))
                return tt(dst, n, times, ALU.mult)

            def layer_mixers(l):
                link(v.memset(raw[:, :, 0:1], 0.0))
                feature_evacuation(("T0", "T1", "T2", "T3"), l, "attn_norm")
                if l == 0:
                    rope_angles()
                    dve.wait_ge(sem("cleared"), 1)
                dve.wait_ge(sem("params_landed"), 16 * N_PARAM_DMAS * (l + 1))
                mix_tokens("P0", l, 6)
                mix_tokens("P1", l, 0)
                if l == 0:
                    rope_cosines()
                wait_evacuated(dve, "LW", l)
                link(v.tensor_scalar(d_lw, d_lw, -DECAY, None, ALU.mult))
                link(v.tensor_tensor_scan(d_cum, const("reset128"), d_lw, 0.0, ALU.mult, ALU.add))
                c4 = d_cum.rearrange("p (b t) -> p b t", b=4)
                link(tt(d_cen.rearrange("p (b t) -> p b t", b=4), c4, c4[:, :, 63:64].broadcast_to([P, 4, P]),
                        ALU.subtract))
                e4 = d_cen.rearrange("p (b t) -> p b t", b=4)
                tt(d_es, d_cen, d_lw, ALU.subtract)
                b2 = "p (j c) t -> p j c t"
                tt(d_arg.unsqueeze(2), e4.rearrange(b2, j=2)[:, :, 0, 127:128], c4.rearrange(b2, j=2)[:, :, 1, 63:64],
                   ALU.add).then_inc(sem("decays_summed"), 1)
                mix_tokens("P2", l, 2)
                mix_tokens("P3", l, 4)
                r_, k_ = mixed[:, 0:2, :], mixed[:, 2:4, :]
                kk3 = d_kk.rearrange("p (j t) -> p j t", j=2)
                for j in range(2):
                    last = v.tensor_scalar(kk3[:, j, :], k_[:, j, :], param("k_k", j), None, ALU.mult)
                link(last)
                tt(d_kk2, d_kk, d_kk, ALU.mult).then_inc(sem("kk_squared"), 1)
                wait_evacuated(dve, "LA", l)
                for j in range(2):
                    last = v.tensor_scalar(d_tmp[:, j * SEQ:(j + 1) * SEQ], d_a[:, j * SEQ:(j + 1) * SEQ], -1.0,
                                           param("k_a", j), ALU.add, ALU.mult)
                link(last)
                kp3 = d_kp.rearrange("p (j t) -> p j t", j=2)
                link(stt(kp3, d_tmp.rearrange("p (j t) -> p j t", j=2), 1.0, k_, ALU.add, ALU.mult))
                for j in range(2):
                    last = stt(d_rk[:, j * SEQ:(j + 1) * SEQ], r_[:, j, :], param("r_k", j), kp3[:, j, :],
                               ALU.mult, ALU.mult)
                last.then_inc(sem("rk_ready"), 1)
                wait_full(dve, "KN", l)
                kn = v.tensor_scalar(d_rn, bank("KN", l)[:, :], 1e-12, None, ALU.add)
                frees(kn, "KN", l)
                wait_evacuated(dve, "KN", l)
                v.sem_inc(sem("kk_sums"), 1)
                dve.wait_ge(sem("log_terms"), l + 1)
                for i in range(3):
                    frees(stt(c_s[i], bank(f"Z{i}", l)[:, :], 0.0, c_e[i], ALU.max, ALU.add), f"Z{i}", l)
                dve.wait_ge(sem("kk_roots"), l + 1)
                link(v.reciprocal(d_rn, d_rn))
                link(tt(d_kk, d_kk, d_rn, ALU.mult))
                link(tt(d_kk2, d_kk, d_a, ALU.mult))
                dve.wait_ge(sem("decay_exps"), l + 1)
                tt(d_bt, d_kk2, d_em, ALU.mult)
                tt(d_kt, d_kp, d_em, ALU.mult).then_inc(sem("bk_ready"), 1)
                for hh in range(2):
                    r = slice(hh * 64, (hh + 1) * 64)

                    def four(ap):
                        return ap[r, :].rearrange("p (j c t) -> p j c t", j=2, c=NT)

                    tt(ar[r, :, hh, :, 0:P], four(d_kk), four(d_es), ALU.mult)
                    last = tt(ar[r, :, hh, :, P:256], r_[r, :, :].rearrange("p j (c t) -> p j c t", c=NT), four(d_ep),
                              ALU.mult)
                last.then_inc(sem("ar_ready"), 1)
                wait_full(dve, "GA", l)
                v_x = v.tensor_scalar(b_x, bank("GA", l)[:, 0:SEQ], param("b_a", 0), None, ALU.add)
                frees(v_x, "GA", l)
                wait_evacuated(dve, "GA", l)
                dve.wait_ge(sem("gate_log"), l + 1)
                link(stt(b_e, b_x, 0.0, b_e, ALU.min, ALU.subtract))
                link(v.tensor_tensor_scan(b_cum, const("reset64"), b_e, 0.0, ALU.mult, ALU.add))
                bc = b_cum.rearrange("p (n t) -> p n t", n=4)
                arg = b_arg.rearrange("p (i n t) -> p i n t", i=4, n=4)
                v.tensor_copy(arg[:, 2, :, :], bc)
                tt(arg[:, 1, :, :], bc[:, :, 31:32].broadcast_to([P, 4, 64]), bc, ALU.subtract)
                tt(arg[:, 3, :, :], bc[:, :, 63:64].broadcast_to([P, 4, 64]), bc, ALU.subtract)
                tt(arg[:, 0, :, :], bc, bc[:, :, 31:32].broadcast_to([P, 4, 64]),
                   ALU.subtract).then_inc(sem("gla_sums"), 1)
                gram_evacuation(l, 0)
                gram_evacuation(l, 1)
                dve.wait_ge(sem("gla_exps"), l + 1)
                wait_evacuated(dve, "P7", l)
                wait_evacuated(dve, "P12", l)
                ex = b_arg.rearrange("p (i t) -> p i t", i=4)
                q_, kb = b_raw[:, 0, :], b_raw[:, 1, :]
                v.tensor_copy(b_dec.unsqueeze(2), arg[:, 2, :, 63:64])
                stt(b_qd, q_, 32.0 ** -0.5, ex[:, 2, :], ALU.mult, ALU.mult)
                tt(b_kh, kb, ex[:, 1, :], ALU.mult)
                tt(b_kd, kb, ex[:, 3, :], ALU.mult)
                for h in range(4):
                    r = slice(32 * h, 32 * h + 32)
                    last = stt(b_q[r, h, :], q_[r, :], 32.0 ** -0.5, ex[r, 0, :], ALU.mult, ALU.mult)
                last.then_inc(sem("gla_ready"), 1)
                wait_evacuated(dve, "CO", l)
                head_norm(normed[:, 0, :], row("sb"), tok[:, :, 2 * GW:3 * GW]).then_inc(sem("stick_done"), 1)
                dve.wait_ge(sem("stick_done"), l + 1)
                before = {2: b_states, 4: window_sums}
                middle = {2: b_state, 4: window_sum}
                after = {1: b_masks, 4: window_masks, 6: b_output, 8: window_output, 9: window_norm}
                for r in range(len(ROUNDS)):
                    if r in before:
                        before[r](l)
                    for c in range(NT):
                        for name in ROUNDS[r]:
                            if name[0] == "T":
                                dst = inv[c]["Tt" if name.endswith("t") else "T"]
                                wait_full(dve, f"{name}_{c}", l)
                                frees(tt(dst, dst, bank(f"{name}_{c}", l)[:, :], ALU.add if r < 4 else ALU.subtract),
                                      f"{name}_{c}", l)
                        if c == 0 and r in middle:
                            middle[r](l, 2)
                    if r in after:
                        after[r](l)
                wait_full(dve, "SU", l)
                for j in range(2):
                    for hh in range(2):
                        s = slice(hh * 64, (hh + 1) * 64)
                        last = v.tensor_scalar(d_s[s, j, :], bank("SU", l)[s, j * P + hh * 64:j * P + hh * 64 + 64],
                                               d_eend[s, j:j + 1], None, ALU.mult)
                frees(last, "SU", l)
                wait_evacuated(dve, "SU", l)
                v.sem_inc(sem("state"), 1)
                rwkv_output(l)

            def b_masks(l):
                wait_full(dve, "GAT", l)
                for t in range(NT):
                    for half in range(2):
                        r = slice(half * 64, half * 64 + 64)
                        last = v.copy_predicated(
                            b_att[r, t, :, half * 64:half * 64 + 64],
                            over(const("gla_mask")[r, :], 4).bitcast(I32),
                            bank("GAT", l)[r, t * 256:(t + 1) * 256].rearrange("p (h t) -> p h t", h=4))
                frees(last, "GAT", l)
                wait_evacuated(dve, "P11", l)
                if l == 0:
                    dve.wait_ge(sem("trig_ready"), 1)
                x1, x2 = a_raw[:, :, :, 0:32], a_raw[:, :, :, 32:64]
                cos = trig[:, 3, :].rearrange("p (t d) -> p t d", t=NT).unsqueeze(2).broadcast_to([P, NT, 6, 32])
                sin = trig[:, 1, :].rearrange("p (t d) -> p t d", t=NT).unsqueeze(2).broadcast_to([P, NT, 6, 32])
                tt(a_t1, x1, cos, ALU.mult)
                link(tt(a_t2, x2, sin, ALU.mult))
                link(tt(a_rot[:, :, :, 0:32], a_t1, a_t2, ALU.subtract))
                tt(a_t1, x2, cos, ALU.mult)
                link(tt(a_t2, x1, sin, ALU.mult))
                tt(a_rot[:, :, :, 32:64], a_t1, a_t2, ALU.add).then_inc(sem("rotated"), 1)

            def b_states(l):
                dve.wait_ge(sem("kv_cleared"), l + 1)
                for n in range(2):
                    b_state(l, n)

            def b_state(l, n):
                wait_full(dve, f"KV{n}", l)
                for h in range(4):
                    r, c = slice(32 * h, 32 * h + 32), slice(h * HD, (h + 1) * HD)
                    if n == 0:
                        last = v.tensor_copy(b_kv[r, n, c], bank(f"KV{n}", l)[r, c])
                    else:
                        last = stt(b_kv[r, n, c], b_kv[r, n - 1, c], b_dec[r, n:n + 1], bank(f"KV{n}", l)[r, c],
                                   ALU.mult, ALU.add)
                frees(last, f"KV{n}", l)
                wait_evacuated(dve, f"KV{n}", l)
                if n == 2:
                    v.sem_inc(sem("gla_state"), 1)

            def b_output(l):
                wait_evacuated(dve, "GO", l)
                wait_evacuated(dve, "P9", l)
                head_norm(normed[:, 0, :], row("gla"), tok[:, :, GW:2 * GW], b_g).then_inc(sem("gla_done"), 1)
                dve.wait_ge(sem("gla_done"), l + 1)

            def gram_evacuation(l, c):
                if c == 0:
                    dve.wait_ge(sem("ar_ready"), l + 1)
                up = over(const("upper"), 2)
                for kind, dst in (("BG", lg), ("KG", mg)):
                    for j in range(2):
                        name = f"{kind}{c}{j}"
                        wait_full(dve, name, l)
                        frees(tt(dst[:, c, 2 * j:2 * j + 2, :], bank(name, l)[:, :].rearrange("p (h n) -> p h n", h=2),
                                 up, ALU.mult), name, l)
                    if kind == "BG":
                        wait_evacuated(dve, name, l)
                        v.sem_inc(sem(f"lt_ready{c}"), 1)
                wait_full(dve, f"LP{c}", l)
                frees(tt(inv[c]["L"].rearrange("p (h n) -> p h n", h=4),
                         bank(f"LP{c}", l)[:, :].rearrange("p (h n) -> p h n", h=4), over(const("lower"), 4),
                         ALU.mult), f"LP{c}", l)
                wait_evacuated(dve, f"LP{c}", l)
                v.sem_inc(sem(f"l_ready{c}"), 1)

            def window_sums(l):
                wait_full(dve, "S0", l)
                frees(tt(a_s0, bank("S0", l)[:, :].rearrange("p (s k) -> p s k", s=4),
                         over(const("a_mask")[:, P:256], 4), ALU.add), "S0", l)
                window_sum(l, 1)

            def window_sum(l, i):
                j = i - 1
                wait_full(dve, f"S1{j}", l)
                frees(tt(a_s1[:, 2 * j:2 * j + 2, :], bank(f"S1{j}", l)[:, :].rearrange("p (s k) -> p s k", s=2),
                         over(const("a_mask"), 2), ALU.add), f"S1{j}", l)

            def window_masks(l):
                wait_evacuated(dve, "S0", l)
                wait_evacuated(dve, "S10", l)
                wait_evacuated(dve, "S11", l)
                v.tensor_reduce(a_max[:, 0:4], a_s0, AX_X, ALU.max)
                link(v.tensor_reduce(a_max[:, 4:8], a_s1, AX_X, ALU.max))
                sinks = row("sinks").rearrange("p (g j) -> p j g", g=2).unsqueeze(1).broadcast_to([P, NT, 2, 2])
                m4 = a_max.rearrange("p (t j g) -> p t j g", t=NT, j=2)
                link(tt(m4, m4, sinks, ALU.max))
                v.tensor_scalar(a_neg, a_max, -1.0, None, ALU.mult)
                tt(a_es.rearrange("p (t j g) -> p t j g", t=NT, j=2), sinks, m4,
                   ALU.subtract).then_inc(sem("a_masked"), 1)

            def window_output(l):
                dve.wait_ge(sem("probs"), l + 1)
                link(tt(a_den, a_den, a_es, ALU.add))
                link(v.reciprocal(a_den, a_den))
                wait_full(dve, "AO", l)
                for t in range(NT):
                    src = bank("AO", l)[:, t * GW:(t + 1) * GW].rearrange("p (j g d) -> p g j d", j=2, g=2)
                    den = a_den[:, 4 * t:4 * t + 4].rearrange("p (j g) -> p g j", j=2).unsqueeze(3).broadcast_to(
                        [P, 2, 2, HD])
                    last = tt(normed[:, 0, t * GW:(t + 1) * GW].rearrange("p (g j d) -> p g j d", g=2, j=2), src, den,
                              ALU.mult)
                frees(last, "AO", l)
                wait_evacuated(dve, "AO", l)

            def window_norm(l):
                head_norm(normed[:, 0, :], row("swa"), tok[:, :, 0:GW]).then_inc(sem("window_done"), 1)
                dve.wait_ge(sem("window_done"), l + 1)

            def rwkv_output(l):
                y = normed[:, 0, :]
                for c in range(NT):
                    wait_full(dve, f"Y{c}", l)
                    frees(v.tensor_copy(y[:, c * GW:(c + 1) * GW], bank(f"Y{c}", l)[:, 0:GW]), f"Y{c}", l)
                    wait_evacuated(dve, f"Y{c}", l)
                link(v.tensor_reduce(h_ss, heads(y), AX_X, ALU.add))
                link(v.tensor_scalar(h_ms, h_ss, 1.0 / HD, None, ALU.mult))
                link(tt(heads(y), heads(y), along(h_ms, HD), ALU.subtract))
                link(tt(normed[:, 1, :], y, y, ALU.mult))
                link(v.tensor_reduce(h_ss, heads(normed[:, 1, :]), AX_X, ALU.add))
                root(v.tensor_scalar(h_ms, h_ss, 1.0 / HD, GN_EPS, ALU.mult, ALU.add))
                link(tt(heads(y), heads(y), along(h_rstd, HD), ALU.mult))
                y2 = y.rearrange("p (t n) -> p t n", t=NT)
                link(tt(y2, y2, over(row("ln_w"), NT), ALU.mult))
                link(tt(y2, y2, over(row("ln_b"), NT), ALU.add))
                link(tt(heads(normed[:, 1, :]), heads(d_v), along(bonus, HD), ALU.mult))
                link(tt(y, y, normed[:, 1, :], ALU.add))
                tt(tok[:, :, 3 * GW:4 * GW], y2, d_g.rearrange("p (t n) -> p t n", t=NT),
                   ALU.mult).then_inc(sem("mix_ready"), 1)

            def add_banks(prefix, l):
                for t in range(NT):
                    for i in (2 * t, 2 * t + 1):
                        wait_full(dve, f"{prefix}{i}", l)
                        s = x_sb[:, t, (i % 2) * 512:(i % 2 + 1) * 512]
                        frees(tt(s, s, bank(f"{prefix}{i}", l)[:, :], ALU.add), f"{prefix}{i}", l)
                        wait_evacuated(dve, f"{prefix}{i}", l)
                        v.sem_inc(sem("x_updated"), 1)

            def rope_angles():
                ang, sn, hf, cs, tmp, num = [trig[:, i, :] for i in range(6)]
                dve.wait_ge(sem("tables_landed"), 16)
                dve.wait_ge(sem("positions_landed"), 16)
                link(v.tensor_copy(r_s[:, 0:2], pos_i[:, :]))
                for t in range(NT):
                    last = v.tensor_scalar(ang[:, t * 32:(t + 1) * 32], const("inv_freq"), r_s[:, t:t + 1], None,
                                           ALU.mult)
                link(last)
                link(v.tensor_scalar(num, ang, 1.0 / TWO_PI, MAGIC, ALU.mult, ALU.add))
                link(v.tensor_scalar(num, num, -MAGIC, None, ALU.add))
                for part in (TWO_PI_1, TWO_PI_2, TWO_PI_3):
                    link(stt(ang, num, -part, ang, ALU.mult, ALU.add))
                v.tensor_scalar(sn, ang, 3.1415925, -3.1415925, ALU.min, ALU.max)
                v.tensor_scalar(hf, ang, 0.5, None, ALU.mult).then_inc(sem("angles"), 1)

            def rope_cosines():
                sn, hf, cs = [trig[:, i, :] for i in (1, 2, 3)]
                dve.wait_ge(sem("sines"), 1)
                link(tt(cs, hf, hf, ALU.mult))
                v.tensor_scalar(cs, cs, -2.0, 1.0, ALU.mult, ALU.add).then_inc(sem("trig_ready"), 1)

            def one_hot(dst, i, values):
                for t in range(NT):
                    last = v.tensor_scalar(dst[:, t, :], const("iota"), place[:, t, bass.ds(i, 1)],
                                           values[:, t, bass.ds(i, 1)], ALU.is_equal, ALU.mult)
                return last

            def gates(l):
                wait_full(dve, "RT", l)
                lg3 = logits.rearrange("p (t e) -> p t e", t=NT)
                oh = r_oh.rearrange("p (t e) -> p t e", t=NT)
                tm = r_tmp.rearrange("p (t e) -> p t e", t=NT)
                cb = comb.rearrange("p (t e) -> p t e", t=NT)
                best, second, rank = r_s[:, 2:4], r_s[:, 4:6], r_s[:, 6:8]
                frees(v.tensor_copy(logits, bank("RT", l)[:, 0:16]), "RT", l)
                wait_evacuated(dve, "RT", l)

                def first_of(src, top, o):
                    link(v.tensor_reduce(top, src, AX_X, ALU.max))
                    for t in range(NT):
                        last = stt(o[:, t, :], src[:, t, :], top[:, t:t + 1], descend[:, :], ALU.is_equal, ALU.mult)
                    link(last)
                    link(v.tensor_reduce(rank, o, AX_X, ALU.max))
                    link(tt(o, over(descend[:, :], NT), along(rank, N_EXPERTS), ALU.is_equal))

                first_of(lg3, best, oh)
                link(stt(tm, oh, -3.0e38, lg3, ALU.mult, ALU.add))
                first_of(tm, second, cb)
                link(tt(oh, oh, cb, ALU.add))
                tables = [slice(q * N_EXPERTS, (q + 1) * N_EXPERTS) for q in range(MAX_PASSES + 1)]
                for e8 in tables:
                    last = v.tensor_copy(chosen[:, :, e8], oh)
                last.then_inc(sem("chosen_ready"), 1)
                link(tt(cb, lg3, along(best, N_EXPERTS), ALU.subtract))
                tt(r_s[:, 0:2], second, best, ALU.subtract).then_inc(sem("gates_shifted"), 1)
                wait_full(dve, "POS", l)
                at = bank("POS", l)[:, 0:16].rearrange("p (t e) -> p t e", t=NT)
                for q in range(MAX_PASSES + 1):
                    v.tensor_scalar(place[:, :, tables[q]], at, -float(CAP * q), None, ALU.add)
                frees(v.tensor_copy(count, bank("POS", l)[:, 16:24]), "POS", l)
                wait_evacuated(dve, "POS", l)
                one_hot(pick, 0, chosen).then_inc(sem("picks"), 1)
                dve.wait_ge(sem("gates_exp"), 1)
                link(v.tensor_scalar(r_s[:, 0:2], r_s[:, 0:2], 1.0, None, ALU.add))
                link(v.reciprocal(r_s[:, 0:2], r_s[:, 0:2]))
                link(tt(cb, cb, oh, ALU.mult))
                link(tt(cb, cb, along(r_s[:, 0:2], N_EXPERTS), ALU.mult))
                for e8 in tables:
                    last = v.tensor_copy(share[:, :, e8], cb)
                link(last)
                link(v.tensor_reduce(most[:, 0:1], count, AX_X, ALU.max))
                for q in range(1, MAX_PASSES):
                    last = v.tensor_scalar(most[:, q:q + 1], most[:, 0:1], float(CAP * q), None, ALU.is_gt)
                link(last)
                link(v.tensor_reduce(most[:, 4:5], most[:, 1:MAX_PASSES], AX_X, ALU.add))
                v.tensor_scalar(passes_i[:, :], most[:, 4:5], 1.0, None, ALU.add).then_inc(sem("passes_ready"), 1)
                dve.wait_ge(sem("passes_ready"), 1)

            for l in range(DEPTH):
                norm_rows(norm_index(l, 0))
                dve.wait_ge(sem("gains_landed"), 16 * (l + 1))
                layer_mixers(l)
                add_banks("O", l)
                norm_rows(norm_index(l, 1))
                feature_evacuation(("F0", "F1", "F2", "F3"), l, "ffn_norm")
                wait_evacuated(dve, "F3", l)
                v.sem_inc(sem("params_used"), 1)
                if l % 2 == 0:
                    for j in range(D_FF // P):
                        dve.wait_ge(sem("silu"), j + 1)
                        frees(tt(act_t[:, j, :], silu_tmp[:, j % 2, :], bank(f"up{j}", l)[:, SEQ:2 * SEQ], ALU.mult),
                              f"up{j}", l)
                    add_banks("dn", l)
                else:
                    gates(l)
                    def slots_in(c, b):
                        return v.tensor_scalar(slot_h[:, c, :], banks[b][:, (c % 4) * CAP:(c % 4 + 1) * CAP],
                                               param("ffn_norm", c), None, ALU.mult)

                    wait_full(dve, "G1", l)
                    for c in range(4, 8):
                        last = slots_in(c, 7)
                    frees(last, "G1", l)
                    n_passes = dve.value_load(passes_i[0:1, 0:1], min_val=1, max_val=MAX_PASSES)
                    with dve.Fori(0, n_passes * N_EXPERTS) as i:
                        one_hot(weigh, i, share).then_inc(sem("weighs"), 1)
                        one_hot(pick, i + 1, chosen).then_inc(sem("picks"), 1)
                        for j in range(UPC):
                            dve.wait_ge(sem("moe_silu"), i * UPC + j + 1)
                            tt(slot_act[:, j, :], slot_silu[:, j % 2, :], banks[j % 2][:, CAP:2 * CAP],
                               ALU.mult).then_inc(free[j % 2], 1)
                        dve.wait_ge(full[7], nth(i, 7, 1))
                        for c in range(4, 8):
                            last = slots_in(c, 7)
                        last.then_inc(free[7], 1)
                        dve.wait_ge(full[3], nth(i, 3, 1))
                        v.tensor_copy(slot_y[:, 512:1024], banks[3][0:CAP, :]).then_inc(free[3], 1)
                        for b, t, half in SCATTER:
                            dve.wait_ge(full[b], nth(i, b, per[b]))
                            s = x_sb[:, t, half * 512:(half + 1) * 512]
                            tt(s, s, banks[b][:, :], ALU.add).then_inc(free[b], 1)
                        for b, t, half in SCATTER:
                            dve.wait_ge(free[b], nth(i, b, per[b]))
                    for t in range(2 * NT):
                        v.sem_inc(sem("x_updated"), 1)
            dve.wait_ge(sem("final_landed"), 16)
            for t in range(NT):
                scale = row_scale(2 * DEPTH, t)
                for i in range(2):
                    s = slice(i * 512, (i + 1) * 512)
                    stt(tok[:, t, s], x_sb[:, t, s], scale, final_row[:, s], ALU.mult,
                        ALU.mult).then_inc(sem("out_ready"), 1)


N_PARAM_DMAS = 5
WARM_UP = 10
SCATTER = ((4, 0, 0), (5, 0, 1), (2, 1, 0), (3, 1, 1))


def kernel(**inputs):
    import concourse.bacc as bacc
    from concourse.bass_utils import run_bass_kernel_spmd

    nc = bacc.Bacc("TRN2", target_bir_lowering=False, num_devices=1)
    a = {k: np.ascontiguousarray(v) for k, v in inputs.items()}

    def columns(v, n):
        return np.moveaxis(v.reshape(DEPTH, n, P), 1, 2)

    arrays = {
        "x": a["x"],
        "positions": np.ascontiguousarray(a["positions"].reshape(NT, P).T),
        "params": np.ascontiguousarray(np.concatenate([
            columns(a["attn_norm"], 8), columns(a["ffn_norm"], 8), columns(a["rwkv_mu"], 8), columns(a["rwkv_w0"], 2),
            columns(a["rwkv_a0"], 2), columns(a["rwkv_k_k"], 2), columns(a["rwkv_k_a"], 2),
            columns(a["rwkv_r_k"], 2), columns(a["gla_b_a"], 1)], axis=2)),
        "rows": np.ascontiguousarray(np.concatenate([
            a["swa_out_norm"].reshape(DEPTH, GW), a["gla_out_norm"].reshape(DEPTH, GW),
            a["sb_out_norm"].reshape(DEPTH, GW), a["rwkv_ln_w"].reshape(DEPTH, GW),
            a["rwkv_ln_b"].reshape(DEPTH, GW), a["swa_sinks"]], axis=1)),
        "final_norm": a["final_norm"].reshape(1, D),
        "consts": shape_constants(),
    }
    for name in ("w_in", "w_out", "gla_w_a2", "rwkv_w2", "rwkv_a2", "rwkv_g2", "ffn_w1", "ffn_w3", "ffn_w2",
                 "router", "moe_w1", "moe_w3", "moe_w2"):
        arrays[name] = a[name]
    t_in = {n: nc.dram_tensor(f"in_{n}", v.shape, mybir.dt.from_np(v.dtype), kind="ExternalInput").ap()
            for n, v in arrays.items()}
    out = nc.dram_tensor("out", (1, SEQ, D), F32, kind="ExternalOutput").ap()
    build(nc, t_in, out)
    r = run_bass_kernel_spmd(nc, [{f"in_{n}": v for n, v in arrays.items()}], core_ids=[0])
    return r.results[0]["out"]
```
